# Optimizing a Trainium2 kernel written in Bass

```python
import jax, jax.numpy as jnp
from jax import lax
import numpy as np

D_MODEL = 1024
BATCH = 1
SEQ = 512
DEPTH = 1
DEC_BATCH = 8
DEC_SEQ = 1
PAST_LEN = 4096
PAGE_SIZE = 128

D_POOL = D_MODEL // 2
D_RNN = D_MODEL - D_POOL
POOL_WINDOWS = (2, 4, 8, 16)
N_POOL_GROUPS = len(POOL_WINDOWS)
POOL_GROUP = D_POOL // N_POOL_GROUPS
POOL_BUF = max(POOL_WINDOWS) - 1
RNN_HEADS = 8
RNN_HEAD_DIM = D_RNN // RNN_HEADS
CONV_WIDTH = 4
LRU_C = 8.0
D_IN = D_POOL + 2 * D_RNN
N_MEM = 256
XA_HEADS = 4
XA_HEAD_DIM = D_MODEL // XA_HEADS
N_EXPERTS = 64
TOP_K = 8
N_EXPERT_GROUPS = 8
TOPK_GROUPS = 4
D_EXPERT = D_MODEL // 4
D_SHARED = D_EXPERT
ROUTED_SCALE = 2.5
MOE_BLOCK = 128
EPS = 1e-6

kernel_name = 'hybrid_pool_rglru_moe_step'

def rms_norm(x, g):
    xf = x.astype(jnp.float32)
    y = xf * lax.rsqrt(jnp.mean(xf * xf, axis=-1, keepdims=True) + EPS)
    return (y * g.astype(jnp.float32)).astype(x.dtype)

def multiscale_pool(u, prev, pos0, w_grp, scale):
    B, S, _ = u.shape
    ext = jnp.concatenate([prev.astype(u.dtype), u], axis=1)
    extf = ext.astype(jnp.float32)
    cs = jnp.concatenate([jnp.zeros((B, 1, D_POOL), jnp.float32), jnp.cumsum(extf, axis=1)], axis=1)
    pos = pos0 + jnp.arange(S)
    hi = cs[:, POOL_BUF + 1:]
    means = []
    for g, w in enumerate(POOL_WINDOWS):
        sl = slice(g * POOL_GROUP, (g + 1) * POOL_GROUP)
        lo = cs[:, POOL_BUF + 1 - w: POOL_BUF + 1 - w + S, sl]
        cnt = jnp.minimum(w, pos + 1).astype(jnp.float32)[None, :, None]
        means.append((hi[..., sl] - lo) / cnt)
    mean = jnp.stack(means, axis=2)
    d = mean - u.astype(jnp.float32).reshape(B, S, N_POOL_GROUPS, POOL_GROUP)
    y = jnp.einsum('bsgc,gcd->bsgd', d, w_grp.astype(jnp.float32)).reshape(B, S, D_POOL)
    y = y * scale.astype(jnp.float32)
    return y.astype(u.dtype), ext[:, -POOL_BUF:]

def causal_conv(u, prev, w, b):
    S = u.shape[1]
    ext = jnp.concatenate([prev.astype(u.dtype), u], axis=1)
    y = b + sum(ext[:, k:k + S] * w[k] for k in range(CONV_WIDTH))
    return y, ext[:, -(CONV_WIDTH - 1):]

def block_diag(x, w, b):
    B, S, _ = x.shape
    y = jnp.einsum('bshi,hij->bshj', x.reshape(B, S, RNN_HEADS, RNN_HEAD_DIM), w.astype(x.dtype))
    return y.reshape(B, S, D_RNN) + b.astype(x.dtype)

def rg_lru(x, h0, pos0, wa, ba, wx, bx, lam):
    B, S, _ = x.shape
    xf = x.astype(jnp.float32)
    r = jax.nn.sigmoid(block_diag(xf, wa, ba))
    i = jax.nn.sigmoid(block_diag(xf, wx, bx))
    log_a = -LRU_C * r * jax.nn.softplus(-lam.astype(jnp.float32))
    a = jnp.exp(log_a)
    mult = jnp.sqrt(-jnp.expm1(2.0 * log_a))
    pos = pos0 + jnp.arange(S)
    mult = jnp.where((pos == 0)[None, :, None], 1.0, mult)
    bt = mult * i * xf

    def step(h, ab):
        a_t, b_t = ab
        h = a_t * h + b_t
        return h, h

    hT, hs = lax.scan(step, h0.astype(jnp.float32), (a.swapaxes(0, 1), bt.swapaxes(0, 1)))
    return hs.swapaxes(0, 1).astype(x.dtype), hT.astype(h0.dtype)

def mixing(x, pool_prev, conv_prev, h0, pos0, g, w_in, pool_w, pool_scale, conv_w, conv_b,
           wa, ba, wx, bx, lam, g_pool, g_rnn, w_out):
    h = rms_norm(x, g)
    z = h @ w_in
    u_pool = z[..., :D_POOL]
    u_rnn = z[..., D_POOL:D_POOL + D_RNN]
    u_gate = z[..., D_POOL + D_RNN:]
    y_pool, pool_state = multiscale_pool(u_pool, pool_prev, pos0, pool_w, pool_scale)
    c, conv_state = causal_conv(u_rnn, conv_prev, conv_w, conv_b)
    hs, hT = rg_lru(c, h0, pos0, wa, ba, wx, bx, lam)
    y_rnn = hs * jax.nn.gelu(u_gate)
    merged = jnp.concatenate([rms_norm(y_pool, g_pool), rms_norm(y_rnn, g_rnn)], axis=-1)
    return merged @ w_out, pool_state, conv_state, hT

def memory_kv(mem, g, wk, wv):
    m = rms_norm(mem, g)
    B, M, _ = m.shape
    k = (m @ wk).reshape(B, M, XA_HEADS, XA_HEAD_DIM)
    v = (m @ wv).reshape(B, M, XA_HEADS, XA_HEAD_DIM)
    return k, v

def cross_attention(x, k, v, g, wq, wo):
    B, S, _ = x.shape
    h = rms_norm(x, g)
    q = (h @ wq).reshape(B, S, XA_HEADS, XA_HEAD_DIM)
    s = jnp.einsum('bshd,bmhd->bhsm', q.astype(jnp.float32), k.astype(jnp.float32)) * (XA_HEAD_DIM ** -0.5)
    p = jax.nn.softmax(s, axis=-1)
    o = jnp.einsum('bhsm,bmhd->bshd', p, v.astype(jnp.float32)).reshape(B, S, D_MODEL)
    return o.astype(x.dtype) @ wo

def route(h, w_r, bias):
    T = h.shape[0]
    scores = jax.nn.sigmoid(h.astype(jnp.float32) @ w_r.astype(jnp.float32))
    biased = scores + bias.astype(jnp.float32)
    grp = biased.reshape(T, N_EXPERT_GROUPS, N_EXPERTS // N_EXPERT_GROUPS)
    grp_score = lax.top_k(grp, 2)[0].sum(-1)
    _, gidx = lax.top_k(grp_score, TOPK_GROUPS)
    gmask = jnp.any(gidx[..., None] == jnp.arange(N_EXPERT_GROUPS), axis=-2)
    emask = jnp.repeat(gmask, N_EXPERTS // N_EXPERT_GROUPS, axis=1)
    masked = jnp.where(emask, biased, -jnp.inf)
    _, eidx = lax.top_k(masked, TOP_K)
    w = jnp.take_along_axis(scores, eidx, axis=-1)
    w = w / jnp.sum(w, axis=-1, keepdims=True) * ROUTED_SCALE
    return eidx, w

def routed_experts(h, eidx, gw, w_gate, w_up, w_down):
    T, D = h.shape
    A = T * TOP_K
    flat_e = eidx.reshape(-1)
    flat_tok = jnp.arange(A, dtype=jnp.int32) // TOP_K
    flat_w = gw.reshape(-1)
    order = jnp.argsort(flat_e)
    se, st, sw = flat_e[order], flat_tok[order], flat_w[order]
    counts = jnp.bincount(flat_e, length=N_EXPERTS)
    padded = (counts + MOE_BLOCK - 1) // MOE_BLOCK * MOE_BLOCK
    pad_end = jnp.cumsum(padded)
    pad_start = pad_end - padded
    start = jnp.cumsum(counts) - counts
    dest = pad_start[se] + jnp.arange(A) - start[se]
    n_blocks = -(-A // MOE_BLOCK) + N_EXPERTS
    cap = n_blocks * MOE_BLOCK
    tok_buf = jnp.full((cap,), T, jnp.int32).at[dest].set(st)
    w_buf = jnp.zeros((cap,), jnp.float32).at[dest].set(sw)
    blk_exp = jnp.minimum(jnp.searchsorted(pad_end, jnp.arange(n_blocks) * MOE_BLOCK, side='right'), N_EXPERTS - 1)
    h_pad = jnp.concatenate([h, jnp.zeros((1, D), h.dtype)], axis=0)

    def body(acc, blk):
        tok, wt, e = blk
        xb = h_pad[tok]
        a = jax.nn.silu(xb @ w_gate[e]) * (xb @ w_up[e])
        yb = (a @ w_down[e]).astype(jnp.float32) * wt[:, None]
        return acc.at[tok].add(yb), None

    acc, _ = lax.scan(body, jnp.zeros((T + 1, D), jnp.float32),
                      (tok_buf.reshape(n_blocks, MOE_BLOCK), w_buf.reshape(n_blocks, MOE_BLOCK), blk_exp))
    return acc[:T].astype(h.dtype)

def moe_ffn(x, g, w_r, bias, w_gate, w_up, w_down, s_gate, s_up, s_down):
    B, S, D = x.shape
    h = rms_norm(x, g).reshape(B * S, D)
    eidx, gw = route(h, w_r, bias)
    y = routed_experts(h, eidx, gw, w_gate, w_up, w_down)
    y = y + (jax.nn.silu(h @ s_gate) * (h @ s_up)) @ s_down
    return y.reshape(B, S, D)

def setup_inputs(seed: int = 0) -> dict:
    key = jax.random.key(seed)
    ks = iter(jax.random.split(key, 48))
    f32 = jnp.float32

    def nrm(shape, scale):
        return jax.random.normal(next(ks), shape, f32) * scale

    def gain(shape):
        return 1.0 + 0.05 * jax.random.normal(next(ks), shape, f32)

    L = DEPTH
    a0 = jax.random.uniform(next(ks), (L, D_RNN), f32, minval=0.9, maxval=0.999)
    return {
        'x_prompt': nrm((BATCH, SEQ, D_MODEL), 1.0),
        'x_sample': nrm((DEC_BATCH, DEC_SEQ, D_MODEL), 1.0),
        'state_pool': nrm((L, DEC_BATCH, POOL_BUF, D_POOL), 1.0),
        'state_conv': nrm((L, DEC_BATCH, CONV_WIDTH - 1, D_RNN), 1.0),
        'state_h': nrm((L, DEC_BATCH, D_RNN), 1.0),
        'cache_mem_k': nrm((L, DEC_BATCH, N_MEM, XA_HEADS, XA_HEAD_DIM), 1.0),
        'cache_mem_v': nrm((L, DEC_BATCH, N_MEM, XA_HEADS, XA_HEAD_DIM), 1.0),
        'mem_prompt': nrm((BATCH, N_MEM, D_MODEL), 1.0),
        'norm_mix': gain((L, D_MODEL)),
        'w_in': nrm((L, D_MODEL, D_IN), D_MODEL ** -0.5),
        'pool_w': nrm((L, N_POOL_GROUPS, POOL_GROUP, POOL_GROUP), POOL_GROUP ** -0.5),
        'pool_scale': gain((L, D_POOL)),
        'conv_w': nrm((L, CONV_WIDTH, D_RNN), 0.5),
        'conv_b': nrm((L, D_RNN), 0.02),
        'gate_a_w': nrm((L, RNN_HEADS, RNN_HEAD_DIM, RNN_HEAD_DIM), RNN_HEAD_DIM ** -0.5),
        'gate_a_b': nrm((L, D_RNN), 0.02),
        'gate_x_w': nrm((L, RNN_HEADS, RNN_HEAD_DIM, RNN_HEAD_DIM), RNN_HEAD_DIM ** -0.5),
        'gate_x_b': nrm((L, D_RNN), 0.02),
        'lru_lambda': jnp.log(a0) - jnp.log1p(-a0),
        'norm_pool_out': gain((L, D_POOL)),
        'norm_rnn_out': gain((L, D_RNN)),
        'w_out': nrm((L, D_MODEL, D_MODEL), D_MODEL ** -0.5),
        'norm_xattn': gain((L, D_MODEL)),
        'norm_mem': gain((L, D_MODEL)),
        'xa_wq': nrm((L, D_MODEL, D_MODEL), D_MODEL ** -0.5),
        'xa_wk': nrm((L, D_MODEL, D_MODEL), D_MODEL ** -0.5),
        'xa_wv': nrm((L, D_MODEL, D_MODEL), D_MODEL ** -0.5),
        'xa_wo': nrm((L, D_MODEL, D_MODEL), D_MODEL ** -0.5),
        'norm_ffn': gain((L, D_MODEL)),
        'router_w': nrm((L, D_MODEL, N_EXPERTS), D_MODEL ** -0.5),
        'router_bias': nrm((L, N_EXPERTS), 0.01),
        'exp_w_gate': nrm((L, N_EXPERTS, D_MODEL, D_EXPERT), D_MODEL ** -0.5),
        'exp_w_up': nrm((L, N_EXPERTS, D_MODEL, D_EXPERT), D_MODEL ** -0.5),
        'exp_w_down': nrm((L, N_EXPERTS, D_EXPERT, D_MODEL), D_EXPERT ** -0.5),
        'sh_w_gate': nrm((L, D_MODEL, D_SHARED), D_MODEL ** -0.5),
        'sh_w_up': nrm((L, D_MODEL, D_SHARED), D_MODEL ** -0.5),
        'sh_w_down': nrm((L, D_SHARED, D_MODEL), D_SHARED ** -0.5),
        'norm_final': gain((D_MODEL,)),
    }

def reference(x_prompt, x_sample, state_pool, state_conv, state_h, cache_mem_k, cache_mem_v, mem_prompt,
              norm_mix, w_in, pool_w, pool_scale, conv_w, conv_b, gate_a_w, gate_a_b, gate_x_w, gate_x_b,
              lru_lambda, norm_pool_out, norm_rnn_out, w_out, norm_xattn, norm_mem, xa_wq, xa_wk, xa_wv, xa_wo,
              norm_ffn, router_w, router_bias, exp_w_gate, exp_w_up, exp_w_down, sh_w_gate, sh_w_up, sh_w_down,
              norm_final):
    xp, xs = x_prompt, x_sample
    Bp = xp.shape[0]
    zero_pool = jnp.zeros((Bp, POOL_BUF, D_POOL), xp.dtype)
    zero_conv = jnp.zeros((Bp, CONV_WIDTH - 1, D_RNN), xp.dtype)
    zero_h = jnp.zeros((Bp, D_RNN), xp.dtype)
    pool_p, conv_p, h_p, mk_p, mv_p = [], [], [], [], []
    pool_s, conv_s, h_s = [], [], []
    for l in range(DEPTH):
        mix_w = (norm_mix[l], w_in[l], pool_w[l], pool_scale[l], conv_w[l], conv_b[l], gate_a_w[l], gate_a_b[l],
                 gate_x_w[l], gate_x_b[l], lru_lambda[l], norm_pool_out[l], norm_rnn_out[l], w_out[l])
        moe_w = (norm_ffn[l], router_w[l], router_bias[l], exp_w_gate[l], exp_w_up[l], exp_w_down[l],
                 sh_w_gate[l], sh_w_up[l], sh_w_down[l])
        d, ps, cs, hT = mixing(xp, zero_pool, zero_conv, zero_h, 0, *mix_w)
        xp = xp + d
        mk, mv = memory_kv(mem_prompt, norm_mem[l], xa_wk[l], xa_wv[l])
        xp = xp + cross_attention(xp, mk, mv, norm_xattn[l], xa_wq[l], xa_wo[l])
        xp = xp + moe_ffn(xp, *moe_w)
        pool_p.append(ps); conv_p.append(cs); h_p.append(hT); mk_p.append(mk); mv_p.append(mv)
        d, ps, cs, hT = mixing(xs, state_pool[l], state_conv[l], state_h[l], PAST_LEN, *mix_w)
        xs = xs + d
        xs = xs + cross_attention(xs, cache_mem_k[l], cache_mem_v[l], norm_xattn[l], xa_wq[l], xa_wo[l])
        xs = xs + moe_ffn(xs, *moe_w)
        pool_s.append(ps); conv_s.append(cs); h_s.append(hT)
    y_prompt = rms_norm(xp, norm_final)
    y_sample = rms_norm(xs, norm_final)
    return (y_prompt, y_sample,
            jnp.stack(pool_p), jnp.stack(conv_p), jnp.stack(h_p), jnp.stack(mk_p), jnp.stack(mv_p),
            jnp.stack(pool_s), jnp.stack(conv_s), jnp.stack(h_s))


_drawn_inputs = setup_inputs


def setup_inputs(seed=0):
    import zlib

    import numpy as np

    out = dict(_drawn_inputs(seed))
    spreads = {}
    factors = {}
    for name, (base, spread) in spreads.items():
        noise = np.random.default_rng([zlib.crc32(name.encode()), seed]).standard_normal(out[name].shape)
        drawn = base * np.exp(spread * noise) if base else spread * noise
        out[name] = __import__('jax').numpy.asarray(drawn.astype(out[name].dtype))
    for name, factor in factors.items():
        out[name] = (out[name] * factor).astype(out[name].dtype)
    return out
```

```python
from contextlib import ExitStack

import concourse.bass as bass
from concourse import mybir

F32, I32, U32 = mybir.dt.float32, mybir.dt.int32, mybir.dt.uint32
ACT, ALU, AX = mybir.ActivationFunctionType, mybir.AluOpType, mybir.AxisListType

P = 128
D = 1024
KD = D // P
SEQ, DEC = 512, 8
NT = SEQ + DEC
HALF = NT // 2
TT = SEQ // P
TILES = [(t * P, P) for t in range(TT)] + [(SEQ, DEC)]
NTT = len(TILES)
DP = D // 2
KP = DP // P
WINDOWS = (2, 4, 8, 16)
PBUF, CBUF = 15, 3
NMEM, MT = 256, 2
HEADS, HD = 4, 256
NE, NG, EG, TOPG = 64, 8, 8, 4
FE, KF = 256, 2
EPS = 1e-6
SCALE = HD ** -0.5
LRU_C = 8.0
ROUTED = 2.5
FAR = 1024
RING = 3
MAXB = P

ROWS = [("norm_mix", 8), ("norm_xattn", 8), ("norm_mem", 8), ("norm_ffn", 8), ("pool_scale", 4), ("conv_w", 16),
        ("conv_b", 4), ("gate_a_b", 4), ("gate_x_b", 4), ("lru_lambda", 4), ("norm_pool_out", 4), ("norm_rnn_out", 4)]
COL, NROWS = {}, 0
for _n, _k in ROWS:
    COL[_n] = NROWS
    NROWS += _k


class Count:

    def __init__(self):
        self.n = {}

    def add(self, ins, sem, k=1):
        ins.then_inc(sem, k)
        self.n[id(sem)] = self.n.get(id(sem), 0) + k
        return sem, self.n[id(sem)]


class Products:

    def __init__(self, order, made, taken):
        self.names = [n for n, _ in order]
        self.no = {n: j for j, n in enumerate(self.names)}
        self.by = [e for _, e in order]
        self.made, self.taken = made, taken
        self.at = [self.by[:j + 1].count(e) for j, e in enumerate(self.by)]
        self.began, self.sent = 0, dict.fromkeys(taken, 0)

    def begin(self, pe, name):
        j = self.no[name]
        assert j == self.began, (name, self.names[self.began])
        self.began += 1
        if j >= 3:
            pe.wait_ge(self.taken[self.by[j - 3]], self.at[j - 3])
        return j % 3

    def made_by(self, ins):
        ins.then_inc(self.made, 1)

    def wait_made(self, eng, name):
        j = self.no[name]
        eng.wait_ge(self.made, j + 1)
        return j % 3

    def take(self, ins, name):
        j = self.no[name]
        e = self.by[j]
        self.sent[e] += 1
        assert self.sent[e] == self.at[j], name
        ins.then_inc(self.taken[e], 1)
        return self.taken[e], self.at[j]

    def wait_taken(self, eng, name):
        j = self.no[name]
        eng.wait_ge(self.taken[self.by[j]], self.at[j])


def product_order():
    o = [("par", "dve")] + [(("xT", k), "dve") for k in range(KD)] + [("nb1", "dve")]
    o += [(("z", m), "act") for m in (4, 5, 6, 7, 8, 9, 10, 11)]
    for i in range(KP):
        o += [(("r", i), "act"), (("i", i), "act")]
    o += [(("z", m), "act") for m in range(4)] + [("st", "act")]
    o += [(("mT", q), "act") for q in range(2)]
    o += [(("K", t), "act") for t in range(MT)] + [(("V", t), "act") for t in range(MT)] + [(("KT", q), "act") for q in range(2)]
    o += [(("yp", g), "act") for g in range(KP)] + [("nbp", "dve"), ("nbr", "dve"), ("hl", "act")]
    o += [(("x1", m), "dve") for m in range(KD)] + [("nb2", "dve")]
    o += [(("q", m), "act") for m in range(KD)] + [("qs", "act")]
    steps = [(h, t) for h in range(HEADS) for t in range(TT)]
    for n in range(len(steps) + 2):
        if n < len(steps):
            o.append((("s", *steps[n]), "act"))
        if n >= 2:
            h, t = steps[n - 2]
            o.append((("pT", h, t), "act"))
            if t == TT - 1:
                o += [(("o", h, c), "act") for c in range(2)]
    o += [("sS", "act"), ("pS", "act"), ("oS", "act")]
    o += [(("x2", m), "dve") for m in range(KD)] + [("nb3", "dve")]
    o += [("rt", "act")]
    o += [(("hR", t), "act") for t in range(NTT)]
    for m in range(KF):
        o += [(("sg", m), "act"), (("su", m), "dve")]
    o += [("pos", "dve"), ("tab", "dve")]
    for t in range(NTT):
        o += [(("xR", t), "act"), (("sd", t), "dve")]
    return o


def trunk(nc, x_prompt, x_sample, state_pool, state_conv, state_h, cache_mem_k, cache_mem_v, mem_prompt, norm_mix,
          w_in, pool_w, pool_scale, conv_w, conv_b, gate_a_w, gate_a_b, gate_x_w, gate_x_b, lru_lambda,
          norm_pool_out, norm_rnn_out, w_out, norm_xattn, norm_mem, xa_wq, xa_wk, xa_wv, xa_wo, norm_ffn, router_w,
          router_bias, exp_w_gate, exp_w_up, exp_w_down, sh_w_gate, sh_w_up, sh_w_down, norm_final,
          y_prompt, y_sample, new_pool_p, new_conv_p, new_h_p, new_k, new_v, new_pool_s, new_conv_s, new_h_s,
          h_rows, acc_rows, q_rows):
    with ExitStack() as ctx:
        def sb(name, shape, dt=F32):
            return ctx.enter_context(nc.sbuf_tensor(name, shape, dt))

        def sem(name):
            return ctx.enter_context(nc.semaphore(name))

        xT = sb("xT", [P, KD, NT])
        hT = sb("hT", [P, KD, NT])
        regA = sb("regA", [P, 12288])
        regB = sb("regB", [P, 8192])
        regC = sb("regC", [P, 8192])
        regL = sb("regL", [P, 14640])
        par = sb("par", [P, NROWS])
        ident = sb("ident", [P, P])
        ones = sb("ones", [P, P])
        small = sb("small", [P, 160])

        def view(reg, at, *shape):
            n = 1
            for s in shape:
                n *= s
            v = reg[:, at:at + n]
            if len(shape) == 2:
                v = v.rearrange("p (a b) -> p a b", a=shape[0])
            elif len(shape) == 3:
                v = v.rearrange("p (a b c) -> p a b c", a=shape[0], b=shape[1])
            return v

        ssq, rs = small[:, 0:5], small[:, 5:10]
        mss, mrs = small[:, 10:12], small[:, 12:14]
        eps_c = small[:, 14:15]
        nsp, psp = small[:, 16:20], small[:, 20:24]
        spt = small[:, 24:64]
        r15 = small[:, 64:80]
        amax, asum = small[:, 80:84], small[:, 84:88]
        nmax, rsum = small[:, 88:92], small[:, 92:96]
        smx, snm, sss, srs = (small[:, 96 + j:97 + j] for j in range(4))
        zero5 = small[:, 104:109]
        fin = small[:, 110:130]

        w_in_v = view(regA, 0, KD, 3 * DP)
        xraw = view(regL, 6312, NTT, D)
        rawP, rawC, rawH = view(regL, 4232, DP), view(regL, 4232 + DP, DP), view(regL, 4232 + 2 * DP, DP)
        rawR = view(regL, 4232 + 3 * DP, P)
        uP = view(regL, 0, KP, PBUF + NT)
        uR = view(regL, 2140, KP, CBUF + NT)
        aT = view(regL, 2140, KP, NT)
        gT = view(regL, 4232, KP, NT)
        cT = view(regL, 6312, KP, NT)
        rT = view(regL, 8392, KP, NT)
        iT = view(regL, 10472, KP, NT)
        sqT = view(regL, 8392, KD, NT)
        stP = view(regL, 12552, KP, DEC, PBUF)
        stC = view(regL, 13032, KP, DEC, CBUF)
        stH = view(regL, 13128, KP, DEC)
        bdw = view(regL, 13160, 2, KP, P)
        hflat = hT[:, :, :].rearrange("p k n -> p (k n)")
        dT = hT[:, 0:KP, :]
        ptmp = [hflat[:, 2080 + 535 * j:2080 + 535 * (j + 1)] for j in range(2)]
        a2 = hflat[:, 3150:3670]
        sqP = view(regL, 0, KP, NT)
        stO = view(regA, 8192, 2, DP)
        plw = view(regA, 10240, KP, P)
        hlO = view(regA, 9216, DP)
        wk_v, wv_v = view(regB, 0, KD, D), view(regC, 0, KD, D)
        mraw = view(regA, 0, MT, D)
        KT = view(regA, 0, KD, NMEM)
        mT = view(regA, 2048, KD, NMEM)
        Kt, Vt = view(regA, 4096, MT, D), view(regA, 6144, MT, D)
        qT = view(regL, 0, KD, NT)
        PT = view(regL, 4160, 2, MT, SEQ)
        kc = view(regL, 6208, 2, MT, D)
        vspare = [view(regL, 10304, MT, D), view(regL, 12352, MT, D)]
        qb = view(regA, 8192, 2, D)
        pr = view(regA, 10240, 4, NMEM)
        sS = view(regA, 11264, MT, DEC * HEADS)
        pSm = view(regA, 11328, NMEM)
        pST = view(regA, 11584, MT, DEC * HEADS)
        qsr = view(regB, 0, D)
        oT = hT
        vc = [view(regC, 2048 * j, MT, D) for j in range(4)] + vspare + [kc[:, 0], kc[:, 1]]
        sgw, suw = view(regC, 0, KD, FE), view(regC, 2048, KD, FE)
        sdw = view(regC, 4096, KF, D)
        rw = view(regC, 6144, KD, NE)
        sco = view(regC, 6656, NTT, NE)
        bia = view(regC, 6976, NTT, NE)
        rbias = view(regC, 7296, NE)
        msk = view(regC, 7360, NTT, NE)
        gwt = view(regC, 7680, NTT, NE)
        rows = view(regL, 0, NTT, D)
        sA = view(regL, 5120, KF, NT)
        m8 = view(regL, 6160, NTT, NG * 8)
        gs = view(regL, 6480, NTT, NG)
        g8 = view(regL, 6520, NTT, 8)
        gi = view(regL, 6560, NTT, 8)
        gif = view(regL, 6600, NTT, 8)
        gmk = view(regL, 6640, NTT, NG)
        geq = view(regL, 6680, NTT, NG)
        pen = view(regL, 6720, NTT, NG)
        top = view(regL, 6760, NTT, 8)
        mrep = view(regL, 6800, NTT, NE)
        wsu = view(regL, 7120, NTT)
        valid = view(regL, 7125, NTT)
        iot8 = view(regL, 7130, NG)
        low = view(regL, 7140, P)
        slot = view(regL, 7268, NTT, NE)
        nblk, bend, bbase = view(regL, 7588, NE), view(regL, 7652, NE), view(regL, 7716, NE)
        iotp = view(regL, 7780, 1)
        ebc = view(regL, 7781, 2)
        j3 = view(regL, 7784, 48)
        cmp = view(regL, 7832, NE)
        iots = view(regL, 7896, P)
        NI = view(regL, 8024, 8)
        ET = view(regL, 8032, P)
        oneh = view(regL, 8160, NTT, P)
        rhsw = view(regL, 8800, NTT, 2)
        idx = view(regL, 8810, RING)
        wsl = view(regL, 8813, RING)
        sidx = view(regL, 8816, RING)
        swl = view(regL, 8819, RING)
        gath = [view(regL, 8824 + D * j, D) for j in range(RING)]
        hX = view(regL, 11896, KD, P)
        sil = view(regL, 12920, FE)
        act = view(regL, 13176, FE)
        aX = view(regL, 13432, KF, P)
        yX = [view(regL, 0 + D * j, D) for j in range(RING)]
        WG = [view(regA, 0, 2, KD * FE), view(regA, 6144, 2, KD * FE), view(regB, 0, 2, KD * FE)]
        WD = [view(regA, 4096, KF, D), view(regA, 10240, KF, D), view(regB, 4096, KF, D)]
        yf = view(regA, 0, NTT, D)
        gfin = view(regC, 0, D)
        junk = view(regC, 1024, D)

        pair = [ctx.enter_context(nc.psum_tensor(f"pair{j}", [P, 2, 512], F32)) for j in range(3)]
        pS = ctx.enter_context(nc.psum_tensor("pS", [P, 2, 512], F32))

        made, act_took, dve_took = sem("made"), sem("act_took"), sem("dve_took")
        J = Products(product_order(), made, {"act": act_took, "dve": dve_took})
        x_in, rows_in, states_in, mem_in = sem("x_in"), sem("rows_in"), sem("states_in"), sem("mem_in")
        win_in = [sem(f"win_in{j}") for j in range(3)]
        wk_in, wv_in, bd_in, plw_in = sem("wk_in"), sem("wv_in"), sem("bd_in"), sem("plw_in")
        wout_in, wq_in, wo_in, sh_in, rw_in = sem("wout_in"), sem("wq_in"), sem("wo_in"), sem("sh_in"), sem("rw_in")
        consts, bd_zero = sem("consts"), sem("bd_zero")
        dve_step, act_step, pool_step = sem("dve_step"), sem("act_step"), sem("pool_step")
        squares, ss_done, root, inverse, normed = sem("squares"), sem("ss_done"), sem("root"), sem("inverse"), sem("normed")
        mem_scaled, mem_ss, mem_inv = sem("mem_scaled"), sem("mem_ss"), sem("mem_inv")
        conv_done, lru_a, lru_s, lru_m2, lru_m, y_rnn, padded = (
            sem(s) for s in ("conv_done", "lru_a", "lru_s", "lru_m2", "lru_m", "y_rnn", "padded"))
        sp_ready, pooled, d_ready = sem("sp_ready"), sem("pooled"), sem("d_ready")
        stored = sem("stored")
        q_stored, qb_in, qb_used = sem("q_stored"), [sem("qb_in0"), sem("qb_in1")], sem("qb_used")
        kc_in, v_in = [sem("kc_in0"), sem("kc_in1")], [sem(f"v_in{j}") for j in range(3)]
        att_max, att_exp, att_norm = sem("att_max"), sem("att_exp"), sem("att_norm")
        s_max, s_exp, s_norm, s_score = sem("s_max"), sem("s_exp"), sem("s_norm"), sem("s_score")
        silu_done, gated, routed = sem("silu_done"), sem("gated"), sem("routed")
        h_stored, acc_ready, sums_landed, rows_left, clear = sem("h_stored"), sem("acc_ready"), sem("sums_landed"), sem("rows_left"), sem("clear")
        masked, row_table = sem("masked"), sem("row_table")
        wg_in, wd_in = [sem(f"wg_in{j}") for j in range(RING)], [sem(f"wd_in{j}") for j in range(RING)]
        onehot, counted, slots_made, idx_ready = sem("onehot"), sem("counted"), sem("slots_made"), sem("idx_ready")
        sp_in, sp_exp, tab_ready = sem("sp_in"), sem("sp_exp"), sem("tab_ready")
        gath_in = [sem(f"gath_in{j}") for j in range(RING)]
        turned, turned_a, turned_d, gu_made, silu_b, act_b = (sem(s) for s in ("turned", "turned_a", "turned_d", "gu_made", "silu_b", "act_b"))
        at_made, at_taken, down_made, down_a, down_d, sidx_ready = (
            sem(s) for s in ("at_made", "at_taken", "down_made", "down_a", "down_d", "sidx_ready"))
        sco_ones = sem("sco_ones")
        fin_in, fin_ss, fin_root, fin_inv, fin_y, fin_g = (sem(s) for s in ("fin_in", "fin_ss", "fin_root", "fin_inv", "fin_y", "fin_g"))

        block = ctx.enter_context(nc.Block())
        halves = lambda v: v.rearrange("p (h n) -> p h n", h=2)

        def turns(eng):
            return eng.value_load(NI[0:1, 0:1].bitcast(I32), min_val=1, max_val=40)

        @block.sync
        def _(sp):
            xp = x_prompt.rearrange("o (t p) d -> p (o t) d", p=P)
            for t in range(TT):
                sp.dma_start(xraw[:, t, :], xp[:, t, :]).then_inc(x_in, 16)
            sp.dma_start(xraw[0:DEC, TT, :], x_sample.rearrange("b o d -> b (o d)")).then_inc(x_in, 16)
            for name, src in (("norm_mix", norm_mix), ("norm_xattn", norm_xattn), ("norm_mem", norm_mem),
                              ("norm_ffn", norm_ffn), ("pool_scale", pool_scale), ("conv_b", conv_b),
                              ("gate_a_b", gate_a_b), ("gate_x_b", gate_x_b), ("lru_lambda", lru_lambda),
                              ("norm_pool_out", norm_pool_out), ("norm_rnn_out", norm_rnn_out)):
                k = dict(ROWS)[name]
                sp.dma_start(rawR[COL[name]:COL[name] + k, :], src.rearrange("o (k p) -> (o k) p", p=P)).then_inc(rows_in, 16)
            sp.dma_start(rawR[COL["conv_w"]:COL["conv_w"] + 16, :],
                         conv_w.rearrange("o w (k p) -> (o w k) p", p=P)).then_inc(rows_in, 16)
            sp.dma_start(rawP[0:DEC * PBUF, :], state_pool.rearrange("o b r c -> (o b r) c")).then_inc(states_in, 16)
            sp.dma_start(rawC[0:DEC * CBUF, :], state_conv.rearrange("o b r c -> (o b r) c")).then_inc(states_in, 16)
            sp.dma_start(rawH[0:DEC, :], state_h[0]).then_inc(states_in, 16)
            win = w_in.rearrange("o (k p) n -> p (o k) n", p=P)
            for j, c in enumerate((1, 2, 0)):
                sp.dma_start(w_in_v[:, :, c * DP:(c + 1) * DP], win[:, :, c * DP:(c + 1) * DP]).then_inc(win_in[j], 16)
                if j == 0:
                    sp.wait_ge(bd_zero, 1)
                    for s, src in enumerate((gate_a_w, gate_x_w)):
                        for half in range(2):
                            lo = half * 64
                            sp.dma_start(bdw[lo:lo + 64, s, :, lo:lo + 64],
                                         src.rearrange("o (k two) i j -> two i (o k) j", two=2)[half]).then_inc(bd_in, 16)
            sp.dma_start(wk_v, xa_wk.rearrange("o (k p) n -> p (o k) n", p=P)).then_inc(wk_in, 16)
            sp.dma_start(wv_v, xa_wv.rearrange("o (k p) n -> p (o k) n", p=P)).then_inc(wv_in, 16)
            sp.dma_start(new_pool_s[0, :, 0:PBUF - 1, :], state_pool[0, :, 1:PBUF, :]).then_inc(stored, 16)
            sp.dma_start(new_conv_s[0, :, 0:CBUF - 1, :], state_conv[0, :, 1:CBUF, :]).then_inc(stored, 16)
            sp.wait_ge(made, J.no[("z", 3)] + 1)
            sp.dma_start(mraw, mem_prompt.rearrange("o (t p) d -> p (o t) d", p=P)).then_inc(mem_in, 16)
            sp.dma_start(plw, pool_w.rearrange("o g c d -> c (o g) d")).then_inc(plw_in, 16)
            sp.wait_ge(made, J.no[("K", 1)] + 1)
            sp.dma_start(view(regB, 0, KD, D), w_out.rearrange("o (k p) n -> p (o k) n", p=P)).then_inc(wout_in, 16)
            sp.wait_ge(made, J.no[("V", 1)] + 1)
            sp.dma_start(view(regC, 0, KD, D), xa_wq.rearrange("o (k p) n -> p (o k) n", p=P)).then_inc(wq_in, 16)
            J.wait_taken(sp, "st")
            sp.dma_start(new_conv_p[0, 0], stO[0:CBUF, 0, :]).then_inc(stored, 16)
            sp.dma_start(new_conv_s[0, :, CBUF - 1, :], stO[CBUF:CBUF + DEC, 0, :]).then_inc(stored, 16)
            sp.dma_start(new_pool_p[0, 0], stO[0:PBUF, 1, :]).then_inc(stored, 16)
            sp.dma_start(new_pool_s[0, :, PBUF - 1, :], stO[PBUF:PBUF + DEC, 1, :]).then_inc(stored, 16)
            J.wait_taken(sp, ("V", 1))
            sp.dma_start(new_k.rearrange("o b (t p) h d -> p (o b t) (h d)", p=P), Kt).then_inc(stored, 16)
            sp.dma_start(new_v.rearrange("o b (t p) h d -> p (o b t) (h d)", p=P), Vt).then_inc(stored, 16)
            J.wait_taken(sp, "hl")
            sp.dma_start(new_h_p[0], hlO[0:1, :]).then_inc(stored, 16)
            sp.dma_start(new_h_s[0], hlO[1:1 + DEC, :]).then_inc(stored, 16)
            sp.wait_ge(ss_done, 4)
            ck = cache_mem_k.rearrange("o b (t p) h d -> p (o b) t (h d)", p=P)
            cv = cache_mem_v.rearrange("o b (t p) h d -> p (o b) t (h d)", p=P)
            for b in range(2):
                sp.dma_start(kc[:, b], ck[:, b]).then_inc(kc_in[b], 16)
            for b in (4, 5):
                sp.dma_start(vc[b], cv[:, b]).then_inc(v_in[0], 16)
            sp.wait_ge(made, J.no[("q", KD - 1)] + 1)
            for b in range(4):
                sp.dma_start(vc[b], cv[:, b]).then_inc(v_in[1], 16)
            J.wait_taken(sp, "qs")
            sp.dma_start(q_rows, qsr[0:DEC, :]).then_inc(q_stored, 16)
            sp.wait_ge(q_stored, 16)
            sp.wait_ge(stored, 16 * 10)
            for b in range(DEC):
                if b >= 2:
                    sp.wait_ge(qb_used, b - 1)
                    sp.dma_start(kc[:, b % 2], ck[:, b]).then_inc(kc_in[b % 2], 16)
                sp.dma_start(qb[:, b % 2, :], q_rows[b, :].partition_broadcast(P)).then_inc(qb_in[b % 2], 16)
                if b == 0:
                    sp.dma_start(view(regB, 0, KD, D), xa_wo.rearrange("o (k p) n -> p (o k) n", p=P)).then_inc(wo_in, 16)
            sp.wait_ge(qb_used, DEC)
            for b in (6, 7):
                sp.dma_start(vc[b], cv[:, b]).then_inc(v_in[2], 16)
            sp.wait_ge(made, J.no["oS"] + 1)
            sp.dma_start(rw, router_w.rearrange("o (k p) e -> p (o k) e", p=P)).then_inc(rw_in, 16)
            sp.dma_start(rbias, router_bias[0].partition_broadcast(P)).then_inc(rw_in, 16)
            sp.dma_start(sgw, sh_w_gate.rearrange("o (k p) f -> p (o k) f", p=P)).then_inc(sh_in, 16)
            sp.dma_start(suw, sh_w_up.rearrange("o (k p) f -> p (o k) f", p=P)).then_inc(sh_in, 16)
            sp.dma_start(sdw, sh_w_down.rearrange("o (k p) d -> p (o k) d", p=P)).then_inc(sh_in, 16)
            for t, (t0, n) in enumerate(TILES):
                J.wait_taken(sp, ("hR", t))
                sp.dma_start(h_rows[t0:t0 + n, :], rows[0:n, t, :]).then_inc(h_stored, 16)

            sp.wait_ge(row_table, 1)
            sp.wait_ge(made, J.no[("x2", KD - 1)] + 1)
            n_turns = turns(sp)
            eg = exp_w_gate.rearrange("o e (p k) f -> (o e) p (k f)", p=P)
            eu = exp_w_up.rearrange("o e (p k) f -> (o e) p (k f)", p=P)
            ed = exp_w_down.rearrange("o e (p k) d -> (o e) p k d", p=P)

            def load(r, e, b):
                sp.wait_ge(gu_made, b + 1)
                sp.dma_start(WG[r][:, 0:1, :], eg[bass.ds(e, 1)].rearrange("e p n -> p e n")).then_inc(wg_in[r], 16)
                sp.dma_start(WG[r][:, 1:2, :], eu[bass.ds(e, 1)].rearrange("e p n -> p e n")).then_inc(wg_in[r], 16)
                sp.wait_ge(down_made, b + 1)
                sp.dma_start(WD[r][:, :, :], ed[bass.ds(e, 1)].rearrange("e p k d -> p (e k) d")).then_inc(wd_in[r], 16)

            e0 = sp.value_load(ET[0:1, 0:1].bitcast(I32), min_val=0, max_val=NE - 1)
            load(0, e0, 0)
            with sp.Fori(0, n_turns) as i:
                for j in range(RING):
                    e = sp.value_load(ET[0:1, bass.ds(i * RING + (j + 1), 1)].bitcast(I32), min_val=0, max_val=NE - 1)
                    load((j + 1) % RING, e, i * RING + (j + 1))
            sp.wait_ge(sums_landed, n_turns * (RING * 16) + 16 * (NTT + 1))
            sp.dma_start(gfin, norm_final.partition_broadcast(P)).then_inc(fin_g, 16)
            for t, (t0, n) in enumerate(TILES):
                sp.dma_start(yf[0:n, t, :], acc_rows[t0:t0 + n, :]).then_inc(fin_in, 16)
            for t, (t0, n) in enumerate(TILES):
                sp.wait_ge(fin_y, t + 1)
                dst = y_prompt[0, t0:t0 + n, :] if t < TT else y_sample.rearrange("b o d -> b (o d)")
                sp.dma_start(dst, yf[0:n, t, :]).then_inc(stored, 16)
            sp.wait_ge(stored, 16 * 15)

        @block.gpsimd
        def _(pool):
            c = Count()

            def step(ins):
                pool.wait_ge(*c.add(ins, pool_step))

            step(pool.memset(ident[:, :], 0.0))
            pool.affine_select(out=ident[:, :], in_=ident[:, :], compare_op=ALU.not_equal, fill=1.0, base=0,
                               pattern=[[-1, P]], channel_multiplier=1).then_inc(consts, 1)
            pool.memset(ones[:, :], 1.0).then_inc(consts, 1)
            step(pool.memset(small[:, :], 0.0))
            pool.memset(eps_c, EPS).then_inc(consts, 1)
            pool.iota(r15, pattern=[[1, 16]], base=1, channel_multiplier=0,
                      allow_small_or_imprecise_dtypes=True).then_inc(consts, 1)
            pool.memset(bdw, 0.0).then_inc(bd_zero, 1)

            for g, w in enumerate(WINDOWS):
                J.wait_taken(pool, ("z", g))
                if g == 0:
                    pool.wait_ge(made, J.no[("z", 3)] + 1)
                src, have, n = uP[:, g, 0:PBUF + SEQ], 1, 0
                while have < w:
                    last = 2 * have == w
                    lo = PBUF if last else 2 * have - 1
                    out = dT[:, g, 0:SEQ] if last else ptmp[n % 2][:, lo:PBUF + SEQ]
                    ins = pool.tensor_tensor(out, src[:, lo:PBUF + SEQ], src[:, lo - have:PBUF + SEQ - have], ALU.add)
                    if last:
                        ins.then_inc(pooled, 1)
                        pool.wait_ge(pooled, g + 1)
                    else:
                        step(ins)
                    src, have, n = ptmp[n % 2], 2 * have, n + 1
            pool.wait_ge(ss_done, 5)
            step(pool.memset(valid, 1.0))
            step(pool.memset(low, 1.0))
            pool.affine_select(out=valid[:, TT:TT + 1], in_=valid[:, TT:TT + 1], compare_op=ALU.is_gt, fill=0.0,
                               base=DEC, pattern=[[0, 1]], channel_multiplier=-1).then_inc(consts, 1)
            pool.affine_select(out=low, in_=low, compare_op=ALU.is_gt, fill=0.0, base=0, pattern=[[1, P]],
                               channel_multiplier=-1).then_inc(consts, 1)
            for out, pattern, base, up in ((iot8, [[1, NG]], 0, 0), (iotp, [[0, 1]], 0, 1), (j3, [[RING, 48]], 0, 0),
                                           (iots, [[1, P]], 0, 0), (rhsw[:, :, 0], [[P, NTT]], -FAR, 1)):
                pool.iota(out, pattern=pattern, base=base, channel_multiplier=up,
                          allow_small_or_imprecise_dtypes=True).then_inc(consts, 1)
            for j in range(RING):
                pool.memset(gath[j], 0.0).then_inc(consts, 1)

            pool.wait_ge(row_table, 1)
            pool.wait_ge(consts, 14)
            n_turns = turns(pool)
            limit = pool.to_reg(NT - 1)
            pool.wait_ge(h_stored, 16 * NTT)

            def gather(r, b):
                pool.wait_ge(turned, b + 1)
                pool.wait_ge(idx_ready, b + 1)
                pool.sem_inc(clear, 1)
                pool.indirect_dma_start(gath[r], None, h_rows,
                                        bass.IndirectOffsetOnAxis(ap=idx[:, r:r + 1].bitcast(U32), axis=0),
                                        bounds_check=limit, oob_is_err=False).then_inc(gath_in[r], 16)

            def scatter(r, b):
                pool.wait_ge(sidx_ready, b + 1)
                pool.wait_ge(down_a, b + 2)
                pool.wait_ge(down_d, b + 2)
                pool.wait_ge(sums_landed, b * 16 + 16 * NTT)
                pool.sem_inc(rows_left, 1)
                pool.sem_inc(clear, 1)
                pool.indirect_dma_start(acc_rows, bass.IndirectOffsetOnAxis(ap=sidx[:, r:r + 1].bitcast(U32), axis=0),
                                        yX[r], None, bounds_check=limit, oob_is_err=False,
                                        compute_op=ALU.add).then_inc(sums_landed, 16)

            for b in range(3):
                gather(b, b)
            for t, (t0, n) in enumerate(TILES):
                pool.wait_ge(acc_ready, t + 1)
                pool.dma_start(acc_rows[t0:t0 + n, :], rows[0:n, t, :]).then_inc(sums_landed, 16)
            pool.wait_ge(sums_landed, 16 * NTT)
            pool.sem_inc(rows_left, RING - 1)
            with pool.Fori(0, n_turns) as i:
                for j in range(RING):
                    b = i * RING + (j + 1)
                    gather(j, b + 2)
                    scatter(j, b - 1)
            scatter(0, n_turns * RING)
            pool.wait_ge(sums_landed, n_turns * (RING * 16) + 16 * (NTT + 1))

        @block.scalar
        def _(a):
            c = Count()

            def rooted(width):
                n = c.n.get(id(root), 0)
                a.wait_ge(ss_done, n + 1)
                if n:
                    a.wait_ge(inverse, n)
                c.add(a.activation(ssq, pS[:, 0, 0:5], ACT.Sqrt, bias=eps_c, scale=1.0 / width), root)

            def squared(out, x):
                c.add(a.activation(out, x, ACT.Square), squares)

            a.wait_ge(consts, 4)
            for k in range(KD):
                J.wait_taken(a, ("xT", k))
                squared(hT[:, k, :], xT[:, k, :])
            rooted(D)
            a.wait_ge(sp_in, 1)
            c.add(a.activation(spt[:, 12:16], spt[:, 4:8], ACT.Exp), sp_exp)
            a.wait_ge(padded, 1)
            for i in range(KP):
                p = J.wait_made(a, ("z", 4 + i))
                J.take(a.copy(halves(uR[:, i, CBUF:CBUF + NT]), pair[p][:, :, 0:HALF]), ("z", 4 + i))
            for i in range(KP):
                p = J.wait_made(a, ("z", 8 + i))
                J.take(a.activation(halves(gT[:, i, :]), pair[p][:, :, 0:HALF], ACT.Gelu_apprx_tanh), ("z", 8 + i))
            for i in range(KP):
                for what, out, bias in (("r", rT, "gate_a_b"), ("i", iT, "gate_x_b")):
                    p = J.wait_made(a, (what, i))
                    J.take(a.activation(halves(out[:, i, :]), pair[p][:, :, 0:HALF], ACT.Sigmoid,
                                        bias=par[:, COL[bias] + i:COL[bias] + i + 1]), (what, i))
            for g in range(KP):
                p = J.wait_made(a, ("z", g))
                J.take(a.copy(halves(uP[:, g, PBUF:PBUF + NT]), pair[p][:, :, 0:HALF]), ("z", g))
            p = J.wait_made(a, "st")
            a.copy(stO[0:CBUF + DEC, 0, :], pair[p][0:CBUF + DEC, 0, :])
            J.take(a.copy(stO[0:PBUF + DEC, 1, :], pair[p][0:PBUF + DEC, 1, :]), "st")
            a.wait_ge(conv_done, KP)
            a.wait_ge(sp_ready, 2)
            J.wait_taken(a, ("i", KP - 1))
            for i in range(KP):
                c.add(a.activation(aT[:, i, :], rT[:, i, :], ACT.Exp, scale=nsp[:, i:i + 1]), lru_a)
            for i in range(KP):
                c.add(a.activation(rT[:, i, :], rT[:, i, :], ACT.Tanh, scale=psp[:, i:i + 1]), lru_s)
            a.wait_ge(mem_in, 16)
            for t in range(MT):
                c.add(a.activation(Kt[:, t, :], mraw[:, t, :], ACT.Square, accum_out=mss[:, t:t + 1]), act_step)
            a.wait_ge(act_step, MT)
            for i in range(KP):
                a.wait_ge(lru_m2, i + 1)
                c.add(a.activation(rT[:, i, :], rT[:, i, :], ACT.Sqrt), lru_m)
            c.add(a.activation(mss, mss, ACT.Sqrt, bias=eps_c, scale=1.0 / D), mem_ss)
            a.wait_ge(mem_inv, 1)
            for t in range(MT):
                c.add(a.activation(mraw[:, t, :], mraw[:, t, :], ACT.Copy, scale=mrs[:, t:t + 1]), mem_scaled)
            for q in range(2):
                p = J.wait_made(a, ("mT", q))
                for j in range(4):
                    k = 4 * q + j
                    cl = COL["norm_mem"] + k
                    ins = a.activation(mT[:, k, :], pair[p][:, j // 2, (j % 2) * NMEM:(j % 2 + 1) * NMEM], ACT.Copy,
                                       scale=par[:, cl:cl + 1])
                J.take(ins, ("mT", q))
            for what, out in (("K", Kt), ("V", Vt)):
                for t in range(MT):
                    p = J.wait_made(a, (what, t))
                    J.take(a.copy(out[:, t, :].rearrange("p (h n) -> p h n", h=2), pair[p][:, :, :]), (what, t))
            for q in range(2):
                p = J.wait_made(a, ("KT", q))
                J.take(a.copy(KT[:, 4 * q:4 * q + 4, :].rearrange("p (h k) n -> p h (k n)", h=2), pair[p][:, :, :]), ("KT", q))
            for g in range(KP):
                p = J.wait_made(a, ("yp", g))
                cl = COL["pool_scale"] + g
                J.take(a.activation(halves(dT[:, g, :]), pair[p][:, :, 0:HALF], ACT.Copy, scale=par[:, cl:cl + 1]), ("yp", g))
            for g in range(KP):
                J.wait_taken(a, ("yp", g))
                squared(sqP[:, g, :], dT[:, g, :])
            rooted(DP)
            for i in range(KP):
                a.wait_ge(y_rnn, i + 1)
                squared(rT[:, i, :], gT[:, i, :])
            rooted(DP)
            p = J.wait_made(a, "hl")
            J.take(a.copy(hlO[0:1 + DEC, :], pair[p][0:1 + DEC, 0, :]), "hl")
            for m in range(KD):
                J.wait_taken(a, ("x1", m))
                squared(sqT[:, m, :], xT[:, m, :])
            rooted(D)
            for m in range(KD):
                p = J.wait_made(a, ("q", m))
                J.take(a.copy(halves(qT[:, m, :]), pair[p][:, :, 0:HALF]), ("q", m))
            p = J.wait_made(a, "qs")
            J.take(a.copy(qsr[0:DEC, :].rearrange("p (h n) -> p h n", h=2), pair[p][0:DEC, :, :]), "qs")
            a.wait_ge(stored, 16 * 10)
            steps = [(h, t) for h in range(HEADS) for t in range(TT)]

            def turn_p(h, t):
                p = J.wait_made(a, ("pT", h, t))
                J.take(a.copy(PT[:, h % 2, :, t * P:(t + 1) * P],
                              pair[p][:, 0, 0:NMEM].rearrange("p (m n) -> p m n", m=MT)), ("pT", h, t))
                if t == TT - 1:
                    for cc in range(2):
                        p = J.wait_made(a, ("o", h, cc))
                        J.take(a.copy(oT[:, 2 * h + cc, 0:SEQ], pair[p][:, 0, :]), ("o", h, cc))

            for n in range(len(steps) + 2):
                if n < len(steps):
                    p = J.wait_made(a, ("s", *steps[n]))
                    r = n % 4
                    a.wait_ge(att_max, n + 1)
                    if n >= 4:
                        a.wait_ge(made, J.no[("pT", *steps[n - 4])] + 1)
                    J.take(a.activation(pr[:, r, :], pair[p][:, 0, 0:NMEM], ACT.Exp, bias=nmax[:, r:r + 1],
                                        scale=SCALE, accum_out=asum[:, r:r + 1]), ("s", *steps[n]))
                if n >= 2:
                    turn_p(*steps[n - 2])
            nb = DEC * HEADS
            p = J.wait_made(a, "sS")
            a.wait_ge(s_max, 1)
            J.take(a.activation(pSm[0:nb, :], pair[p][0:nb, 0, 0:NMEM], ACT.Exp, bias=snm[0:nb, :], scale=SCALE,
                                accum_out=sss[0:nb, :]), "sS")
            p = J.wait_made(a, "pS")
            J.take(a.copy(pST, pair[p][:, 0, 0:MT * nb].rearrange("p (m n) -> p m n", m=MT)), "pS")
            p = J.wait_made(a, "oS")
            J.take(a.copy(oT[:, :, SEQ:NT], pair[p][:, 0, 0:KD * DEC].rearrange("p (k b) -> p k b", k=KD)), "oS")
            for m in range(KD):
                J.wait_taken(a, ("x2", m))
                squared(sqT[:, m, :], xT[:, m, :])
            rooted(D)
            p = J.wait_made(a, "rt")
            a.wait_ge(sco_ones, 1)
            a.activation(sco[:, 0:TT, :], pair[p][:, 0, 0:TT * NE].rearrange("p (t e) -> p t e", t=TT), ACT.Sigmoid)
            J.take(a.activation(sco[0:DEC, TT, :], pair[p][0:DEC, 0, TT * NE:NTT * NE], ACT.Sigmoid), "rt")
            for t, (t0, n) in enumerate(TILES):
                p = J.wait_made(a, ("hR", t))
                J.take(a.copy(rows[0:n, t, :].rearrange("p (h n) -> p h n", h=2), pair[p][0:n, :, :]), ("hR", t))
            for m in range(KF):
                p = J.wait_made(a, ("sg", m))
                J.take(a.activation(halves(sA[:, m, :]), pair[p][:, :, 0:HALF], ACT.Silu), ("sg", m))
            a.wait_ge(h_stored, 16 * NTT)
            for t, (t0, n) in enumerate(TILES):
                p = J.wait_made(a, ("xR", t))
                J.take(a.copy(rows[0:n, t, :].rearrange("p (h n) -> p h n", h=2), pair[p][0:n, :, :]), ("xR", t))

            a.wait_ge(row_table, 1)
            n_turns = turns(a)
            a.sem_inc(down_a, 1)

            def silu(b, first=False):
                a.wait_ge(gu_made, b + (1 + RING))
                if not first:
                    a.wait_ge(act_b, b)
                a.activation(sil, pair[0][:, 0, 0:FE], ACT.Silu).then_inc(silu_b, 1)

            def turn(b):
                a.wait_ge(turned, b + (1 + RING))
                a.copy(hX[:, 0:4, :].rearrange("p k n -> p (k n)"), pair[1][:, 0, :]).then_inc(turned_a, 1)

            def at(b):
                a.wait_ge(at_made, b + 1)
                a.copy(aX.rearrange("p k n -> p (k n)"), pair[0][:, 1, 0:FE]).then_inc(at_taken, 1)

            def down(r, b):
                a.wait_ge(down_made, b + (1 + RING))
                a.wait_ge(sidx_ready, b + 1)
                a.activation(yX[r][:, 0:512], pair[2][:, 0, :], ACT.Copy, scale=swl[:, r:r + 1]).then_inc(down_a, 1)

            turn(0)
            silu(0, first=True)
            turn(1)
            with a.Fori(0, n_turns) as i:
                for j in range(RING):
                    b = i * RING + (j + 1)
                    at(b - 1)
                    silu(b)
                    turn(b + 1)
                    down(j, b - 1)
            at(n_turns * RING)
            down(0, n_turns * RING)

            a.wait_ge(fin_in, 16 * NTT)
            for t, (t0, n) in enumerate(TILES):
                if t:
                    a.wait_ge(fin_ss, t)
                a.activation(junk[0:n, :], yf[0:n, t, :], ACT.Square, accum_out=fin[0:n, t:t + 1]).then_inc(fin_ss, 1)
            a.wait_ge(fin_ss, NTT)
            a.activation(fin[:, 5:10], fin[:, 0:5], ACT.Sqrt, bias=eps_c, scale=1.0 / D).then_inc(fin_root, 1)

        @block.vector
        def _(v):
            c = Count()

            def mark(ins):
                return c.add(ins, dve_step)

            def step(ins):
                v.wait_ge(*mark(ins))

            def inverted():
                n = c.n.get(id(inverse), 0)
                v.wait_ge(root, n + 1)
                c.add(v.reciprocal(rs, ssq), inverse)

            def apply(nb, src, dst, gain, tiles):
                p = J.wait_made(v, nb)
                for k in range(tiles):
                    ins = v.scalar_tensor_tensor(halves(dst[:, k, :]), halves(src[:, k, :]),
                                                 par[:, COL[gain] + k:COL[gain] + k + 1],
                                                 pair[p][:, :, 0:HALF], ALU.mult, ALU.mult)
                    if k < tiles - 1:
                        c.add(ins, normed)
                    else:
                        J.take(ins, nb)

            p = J.wait_made(v, "par")
            v.tensor_copy(par[:, :], pair[p][:, 1, 128:128 + NROWS])
            v.tensor_copy(stP.rearrange("p k b r -> p (k b r)"), pair[p][:, 0, 0:480])
            J.take(v.tensor_copy(view(regL, 13032, 128), pair[p][:, 1, 0:128]), "par")
            for k in range(KD):
                p = J.wait_made(v, ("xT", k))
                v.tensor_copy(xT[:, k, 0:SEQ], pair[p][:, 0, :])
                J.take(v.tensor_copy(xT[:, k, SEQ:NT], pair[p][:, 1, 0:DEC]), ("xT", k))
            v.memset(uP[:, :, 0:PBUF], 0.0)
            c.add(v.memset(uR[:, :, 0:CBUF], 0.0), padded)
            inverted()
            apply("nb1", xT, hT, "norm_mix", KD)
            lam = par[:, COL["lru_lambda"]:COL["lru_lambda"] + 4]
            v.wait_ge(consts, 4)
            J.wait_taken(v, "par")
            sp4 = lambda j: spt[:, 4 * j:4 * j + 4]
            step(v.tensor_scalar(sp4(0), lam, -1.0, None, ALU.mult))
            v.tensor_tensor(sp4(1), sp4(0), lam, ALU.min)
            c.add(v.tensor_scalar(sp4(2), sp4(0), 0.0, None, ALU.max), sp_in)
            v.wait_ge(sp_exp, 1)
            step(v.tensor_scalar(sp4(4), sp4(3), 2.0, None, ALU.add))
            step(v.reciprocal(sp4(5), sp4(4)))
            step(v.tensor_tensor(sp4(6), sp4(3), sp4(5), ALU.mult))
            step(v.tensor_tensor(sp4(7), sp4(6), sp4(6), ALU.mult))
            step(v.tensor_scalar(sp4(8), sp4(7), 1.0 / 17, 1.0 / 15, ALU.mult, ALU.add))
            for k in (13, 11, 9, 7, 5, 3, 1):
                step(v.tensor_tensor(sp4(8), sp4(8), sp4(7), ALU.mult))
                step(v.tensor_scalar(sp4(8), sp4(8), 1.0 / k, None, ALU.add))
            step(v.tensor_tensor(sp4(8), sp4(8), sp4(6), ALU.mult))
            step(v.scalar_tensor_tensor(sp4(8), sp4(8), 2.0, sp4(2), ALU.mult, ALU.add))
            c.add(v.tensor_scalar(nsp, sp4(8), -LRU_C, None, ALU.mult), sp_ready)
            c.add(v.tensor_scalar(psp, sp4(8), LRU_C, None, ALU.mult), sp_ready)
            step(v.reciprocal(r15, r15))

            wcol = lambda k, i: par[:, COL["conv_w"] + 4 * k + i:COL["conv_w"] + 4 * k + i + 1]
            bcol = lambda i: par[:, COL["conv_b"] + i:COL["conv_b"] + i + 1]
            for i in range(KP):
                J.wait_taken(v, ("z", 4 + i))
                u = uR[:, i, :]
                v.tensor_scalar(cT[:, i, SEQ:NT], u[:, CBUF + SEQ:CBUF + NT], wcol(3, i), bcol(i), ALU.mult, ALU.add)
                step(v.tensor_scalar(cT[:, i, 0:SEQ], u[:, 0:SEQ], wcol(0, i), bcol(i), ALU.mult, ALU.add))
                for k in range(1, 4):
                    v.scalar_tensor_tensor(cT[:, i, SEQ:NT], stC[:, i, :, k - 1], wcol(k - 1, i), cT[:, i, SEQ:NT],
                                           ALU.mult, ALU.add)
                    ins = v.scalar_tensor_tensor(cT[:, i, 0:SEQ], u[:, k:k + SEQ], wcol(k, i), cT[:, i, 0:SEQ],
                                                 ALU.mult, ALU.add)
                    if k < 3:
                        step(ins)
                    else:
                        c.add(ins, conv_done)
            for g, w in enumerate(WINDOWS):
                v.wait_ge(pooled, g + 1)
                step(v.tensor_reduce(dT[:, g, SEQ:NT], stP[:, g, :, PBUF - w + 1:PBUF], AX.X, ALU.add))
                v.tensor_tensor(dT[:, g, SEQ:NT], dT[:, g, SEQ:NT], uP[:, g, PBUF + SEQ:PBUF + NT], ALU.add)
                step(v.scalar_tensor_tensor(dT[:, g, 0:w - 1], dT[:, g, 0:w - 1], float(w), r15[:, 0:w - 1],
                                            ALU.mult, ALU.mult))
                c.add(v.scalar_tensor_tensor(dT[:, g, :], dT[:, g, :], 1.0 / w, uP[:, g, PBUF:PBUF + NT],
                                             ALU.mult, ALU.subtract), d_ready)
            for i in range(KP):
                v.wait_ge(lru_a, i + 1)
                step(v.tensor_tensor(a2, aT[:, i, :], aT[:, i, :], ALU.mult))
                v.wait_ge(lru_s, i + 1)
                v.wait_ge(*c.add(v.scalar_tensor_tensor(rT[:, i, :], a2, 1.0, rT[:, i, :], ALU.add, ALU.mult), lru_m2))
            v.wait_ge(mem_ss, 1)
            c.add(v.reciprocal(mrs, mss), mem_inv)
            v.wait_ge(lru_m, KP)
            step(v.memset(rT[:, :, 0:1], 1.0))
            t0 = [mark(v.tensor_tensor(iT[:, i, :], iT[:, i, :], rT[:, i, :], ALU.mult)) for i in range(KP)]
            t1 = []
            for i in range(KP):
                v.wait_ge(*t0[i])
                t1.append(mark(v.tensor_tensor(iT[:, i, :], iT[:, i, :], cT[:, i, :], ALU.mult)))
            v.wait_ge(*t1[-1])
            t2 = mark(v.tensor_tensor(stH, aT[:, :, SEQ:NT], stH, ALU.mult))
            t3 = [mark(v.tensor_tensor_scan(cT[:, i, 0:SEQ], aT[:, i, 0:SEQ], iT[:, i, 0:SEQ], 0.0, ALU.mult, ALU.add))
                  for i in range(KP)]
            v.wait_ge(*t2)
            step(v.tensor_tensor(cT[:, :, SEQ:NT], stH, iT[:, :, SEQ:NT], ALU.add))
            for i in range(KP):
                c.add(v.tensor_tensor(gT[:, i, :], cT[:, i, :], gT[:, i, :], ALU.mult), y_rnn)
            inverted()
            apply("nbp", dT, dT, "norm_pool_out", KP)
            inverted()
            apply("nbr", gT, gT, "norm_rnn_out", KP)

            def residual(what):
                for m in range(KD):
                    p = J.wait_made(v, (what, m))
                    J.take(v.tensor_tensor(halves(xT[:, m, :]), halves(xT[:, m, :]), pair[p][:, :, 0:HALF], ALU.add), (what, m))

            residual("x1")
            inverted()
            apply("nb2", xT, hT, "norm_xattn", KD)

            steps = [(h, t) for h in range(HEADS) for t in range(TT)]
            units = [(b, mt) for b in range(DEC) for mt in range(MT)]

            def scores(b, mt):
                if mt == 0:
                    v.wait_ge(qb_in[b % 2], 16 * (b // 2 + 1))
                    v.wait_ge(kc_in[b % 2], 16 * (b // 2 + 1))
                for h in range(HEADS):
                    kk = kc[:, b % 2, mt, h * HD:(h + 1) * HD]
                    ins = v.tensor_tensor_reduce(kk, kk, qb[:, b % 2, h * HD:(h + 1) * HD], 1.0, 0.0, ALU.mult, ALU.add,
                                                 sS[:, mt, b * HEADS + h:b * HEADS + h + 1])
                if mt == MT - 1:
                    ins.then_inc(qb_used, 1)

            def norm_p(n):
                J.wait_taken(v, ("s", *steps[n]))
                r = n % 4
                step(v.reciprocal(rsum[:, r:r + 1], asum[:, r:r + 1]))
                c.add(v.tensor_scalar(pr[:, r, :], pr[:, r, :], rsum[:, r:r + 1], None, ALU.mult), att_norm)

            for n in range(len(steps) + 1):
                if n < len(steps):
                    p = J.wait_made(v, ("s", *steps[n]))
                    r = n % 4
                    step(v.tensor_reduce(amax[:, r:r + 1], pair[p][:, 0, 0:NMEM], AX.X, ALU.max))
                    c.add(v.tensor_scalar(nmax[:, r:r + 1], amax[:, r:r + 1], -SCALE, None, ALU.mult), att_max)
                if n >= 1:
                    norm_p(n - 1)
                if 4 <= n < 12:
                    scores(*units[2 * n - 8])
                    scores(*units[2 * n - 7])
            nb = DEC * HEADS
            p = J.wait_made(v, "sS")
            step(v.tensor_reduce(smx[0:nb, :], pair[p][0:nb, 0, 0:NMEM], AX.X, ALU.max))
            c.add(v.tensor_scalar(snm[0:nb, :], smx[0:nb, :], -SCALE, None, ALU.mult), s_max)
            J.wait_taken(v, "sS")
            step(v.reciprocal(srs[0:nb, :], sss[0:nb, :]))
            c.add(v.tensor_scalar(pSm[0:nb, :], pSm[0:nb, :], srs[0:nb, :], None, ALU.mult), s_norm)
            v.wait_ge(made, J.no["oS"] + 1)
            c.add(v.memset(sco, 1.0), sco_ones)
            residual("x2")
            inverted()
            apply("nb3", xT, hT, "norm_ffn", KD)

            J.wait_taken(v, "rt")
            v.wait_ge(rw_in, 32)
            v.wait_ge(consts, 14)
            over = lambda x, n: x.unsqueeze(1).to_broadcast((P, NTT, n))
            step(v.tensor_tensor(bia, sco, over(rbias, NE), ALU.add))
            for t in range(NTT):
                for g in range(NG):
                    ins = v.max(m8[:, t, g * 8:(g + 1) * 8], bia[:, t, g * EG:(g + 1) * EG])
            step(ins)
            m8v = m8.rearrange("p t (g j) -> p t g j", j=8)
            step(v.tensor_tensor(gs, m8v[:, :, :, 0], m8v[:, :, :, 1], ALU.add))
            for t in range(NTT):
                ins = v.max(g8[:, t, :], gs[:, t, :])
            step(ins)
            for t in range(NTT):
                ins = v.max_index(gi[:, t, :].bitcast(U32), g8[:, t, :], gs[:, t, :])
            step(ins)
            step(v.tensor_copy(gif, gi.bitcast(U32)))
            for j in range(TOPG):
                out = gmk if j == 0 else geq
                step(v.tensor_tensor(out, over(iot8, NG), gif[:, :, j:j + 1].to_broadcast((P, NTT, NG)), ALU.is_equal))
                if j:
                    step(v.tensor_tensor(gmk, gmk, geq, ALU.add))
            step(v.tensor_scalar(pen, gmk, -1.0, 1e30, ALU.add, ALU.mult))
            gm4 = lambda x: x.unsqueeze(3).to_broadcast((P, NTT, NG, EG))
            b4 = bia.rearrange("p t (g j) -> p t g j", j=EG)
            for t in range(NTT):
                ins = v.tensor_tensor(b4[:, t], b4[:, t], gmk[:, t, :].unsqueeze(2).to_broadcast((P, NG, EG)), ALU.mult)
            step(ins)
            for t in range(NTT):
                ins = v.tensor_tensor(b4[:, t], b4[:, t], pen[:, t, :].unsqueeze(2).to_broadcast((P, NG, EG)), ALU.add)
            step(ins)
            for t in range(NTT):
                ins = v.max(top[:, t, :], bia[:, t, :])
            step(ins)
            for t in range(NTT):
                ins = v.match_replace(mrep[:, t, :], top[:, t, :], bia[:, t, :], -3e38)
            step(ins)
            step(v.tensor_scalar(msk, mrep, -3e38, None, ALU.is_equal))
            step(v.tensor_tensor(gwt, msk, sco, ALU.mult))
            step(v.tensor_reduce(wsu, gwt, AX.X, ALU.add))
            step(v.reciprocal(wsu, wsu))
            step(v.tensor_scalar(wsu, wsu, ROUTED, None, ALU.mult))
            t0 = mark(v.tensor_tensor(gwt, gwt, wsu.unsqueeze(2).to_broadcast((P, NTT, NE)), ALU.mult))
            c.add(v.tensor_tensor(msk, msk, valid.unsqueeze(2).to_broadcast((P, NTT, NE)), ALU.mult), masked)
            for m in range(KF):
                p = J.wait_made(v, ("su", m))
                J.wait_taken(v, ("sg", m))
                J.take(v.tensor_tensor(halves(sA[:, m, :]), halves(sA[:, m, :]), pair[p][:, :, 0:HALF], ALU.mult), ("su", m))
            p = J.wait_made(v, "pos")
            v.wait_ge(*t0)
            cnt = pair[p][:, 0, NTT * NE:(NTT + 1) * NE]
            step(v.tensor_scalar(nblk, cnt, 0.0, None, ALU.is_gt))
            for k in range(1, -(-NT // P)):
                step(v.scalar_tensor_tensor(nblk, cnt, float(P * k), nblk, ALU.is_gt, ALU.add))
            step(v.tensor_tensor_scan(bend, ones[:, 0:NE], nblk, 0.0, ALU.mult, ALU.add))
            step(v.tensor_tensor(bbase, bend, nblk, ALU.subtract))
            step(v.tensor_scalar(bbase, bbase, float(P), 1.0, ALU.mult, ALU.add))
            J.take(v.tensor_tensor(slot, pair[p][:, 0, 0:NTT * NE].rearrange("p (t e) -> p t e", t=NTT), over(bbase, NE), ALU.add), "pos")
            J.wait_taken(v, "pos")
            step(v.tensor_tensor(slot, slot, msk, ALU.mult))
            step(v.tensor_scalar(slot, slot, -1.0, None, ALU.add))
            step(v.tensor_scalar(cmp, bend, iotp, 0.0, ALU.is_le, ALU.add, accum_out=ebc[:, 0:1]))
            c.add(v.tensor_scalar(ebc[:, 0:1], ebc[:, 0:1], float(NE - 1), None, ALU.min), tab_ready)
            step(v.tensor_scalar(ebc[:, 1:2], bend[:, NE - 1:NE], -1.0, None, ALU.add))
            step(v.tensor_scalar(cmp[:, 0:48], j3, ebc[:, 1:2], 0.0, ALU.is_lt, ALU.add, accum_out=cmp[:, 48:49]))
            step(v.tensor_copy(NI[:, 0:1].bitcast(I32), cmp[:, 48:49]))
            p = J.wait_made(v, "tab")
            J.take(v.tensor_copy(ET[0:1, :].bitcast(I32), pair[p][0:1, 0, 0:P]), "tab")
            J.wait_taken(v, "tab")
            c.add(v.tensor_copy(cmp[:, 49:50], cmp[:, 48:49]), row_table)
            v.wait_ge(row_table, 1)
            n_turns = turns(v)
            for t, (t0_, n) in enumerate(TILES):
                p = J.wait_made(v, ("sd", t))
                J.wait_taken(v, ("xR", t))
                row = rows[0:n, t, :].rearrange("p (h n) -> p h n", h=2)
                J.take(v.tensor_tensor(row, row, pair[p][0:n, :, :], ALU.add), ("sd", t))
                J.wait_taken(v, ("sd", t))
                c.add(v.tensor_copy(cmp[:, 50:51], cmp[:, 48:49]), acc_ready)

            v.sem_inc(down_d, 1)

            def onehot_(b):
                e = v.value_load(ET[0:1, bass.ds(b, 1)].bitcast(I32), min_val=0, max_val=NE - 1)
                v.tensor_tensor(oneh, iots.unsqueeze(1).to_broadcast((P, NTT, P)),
                                slot[:, :, bass.ds(e, 1)].to_broadcast((P, NTT, P)), ALU.is_equal)
                v.tensor_copy(rhsw[:, :, 1:2], gwt[:, :, bass.ds(e, 1)]).then_inc(onehot, 1)
                v.wait_ge(onehot, b + 1)
                v.tensor_scalar(iots, iots, float(P), None, ALU.add).then_inc(counted, 1)
                v.wait_ge(counted, b + 1)

            def slots(r, b):
                v.wait_ge(slots_made, b + 1)
                v.tensor_copy(wsl[:, r:r + 1], pS[:, 0, 1:2])
                v.tensor_scalar(idx[:, r:r + 1].bitcast(U32), pS[:, 0, 0:1], float(FAR), None, ALU.add).then_inc(idx_ready, 1)

            def keep(r, b):
                v.wait_ge(idx_ready, b + 1)
                v.wait_ge(rows_left, b + 1)
                v.tensor_copy(swl[:, r:r + 1], wsl[:, r:r + 1])
                v.tensor_copy(sidx[:, r:r + 1].bitcast(U32), idx[:, r:r + 1].bitcast(U32)).then_inc(sidx_ready, 1)

            def turn(b):
                v.wait_ge(turned, b + (1 + RING))
                v.tensor_copy(hX[:, 4:8, :].rearrange("p k n -> p (k n)"), pair[1][:, 1, :]).then_inc(turned_d, 1)

            def gate(b, first=False):
                v.wait_ge(silu_b, b + 1)
                if not first:
                    v.wait_ge(at_made, b)
                v.tensor_tensor(act, sil, pair[0][:, 0, FE:2 * FE], ALU.mult).then_inc(act_b, 1)

            def down(r, b):
                v.wait_ge(down_made, b + (1 + RING))
                v.wait_ge(sidx_ready, b + 1)
                v.tensor_scalar(yX[r][:, 512:D], pair[2][:, 1, :], swl[:, r:r + 1], None, ALU.mult).then_inc(down_d, 1)

            onehot_(0)
            for b in range(3):
                slots(b, b)
                onehot_(b + 1)
            turn(0)
            gate(0, first=True)
            turn(1)
            with v.Fori(0, n_turns) as i:
                for j in range(RING):
                    b = i * RING + (j + 1)
                    keep(j, b - 1)
                    v.wait_ge(sidx_ready, b)
                    slots(j, b + 2)
                    onehot_(b + 3)
                    gate(b)
                    turn(b + 1)
                    down(j, b - 1)
            keep(0, n_turns * RING)
            down(0, n_turns * RING)

            v.wait_ge(fin_root, 1)
            v.reciprocal(fin[:, 10:15], fin[:, 5:10]).then_inc(fin_inv, 1)
            v.wait_ge(fin_inv, 1)
            v.wait_ge(fin_g, 16)
            for t, (t0_, n) in enumerate(TILES):
                v.scalar_tensor_tensor(yf[0:n, t, :], yf[0:n, t, :], fin[0:n, 10 + t:11 + t], gfin[0:n, :],
                                       ALU.mult, ALU.mult).then_inc(fin_y, 1)

        @block.tensor
        def _(pe):
            seen = {"squares": 0}

            def project(name, weights, acts, ks, ready=None):
                p = J.begin(pe, name)
                for k in ks:
                    if ready:
                        ready(k)
                    for h in range(2):
                        ins = pe.matmul(pair[p][:, h, 0:HALF], weights(k), acts(k)[:, h * HALF:(h + 1) * HALF],
                                        start=k == ks[0], stop=k == ks[-1])
                J.made_by(ins)

            def sum_squares(k, sq, first, last):
                seen["squares"] += 1
                if first:
                    if seen["squares"] > 1:
                        pe.wait_ge(root, seen["norms"])
                    seen["norms"] = seen.get("norms", 0) + 1
                    pe.matmul(pS[:, 0, 0:NTT], ones[:, :], zero5, start=True, stop=False, skip_group_check=True)
                pe.wait_ge(squares, seen["squares"])
                for t, (t0, n) in enumerate(TILES):
                    ins = pe.matmul(pS[0:n, 0, t:t + 1], sq[:, k, t0:t0 + n], ones[:, 0:1], start=False,
                                    stop=last and t == NTT - 1, skip_group_check=True)
                if last:
                    ins.then_inc(ss_done, 1)

            def spread(name):
                p = J.begin(pe, name)
                pe.wait_ge(inverse, seen["norms"])
                for lo, hi, t in ((0, 128, 0), (128, 256, 1), (256, 260, 2), (260, 384, 2), (384, 512, 3), (512, 520, 4)):
                    h, t0 = lo // HALF, t * P
                    ins = pe.matmul(pair[p][:, h, lo - h * HALF:hi - h * HALF], rs[:, t:t + 1].to_broadcast((P, P)),
                                    ident[:, lo - t0:hi - t0], start=True, stop=True)
                J.made_by(ins)

            def normed_tiles(base, nb, tiles):
                def ready(k):
                    if k < tiles - 1:
                        pe.wait_ge(normed, base + k + 1)
                    else:
                        J.wait_taken(pe, nb)
                return ready

            pe.wait_ge(consts, 4)
            pe.wait_ge(rows_in, 16 * 12)
            pe.wait_ge(states_in, 16 * 3)
            p = J.begin(pe, "par")
            for k in range(KP):
                ks = slice(k * P, (k + 1) * P)
                n = DEC * PBUF
                pe.transpose(pair[p][:, 0, k * n:(k + 1) * n], rawP[0:n, ks], ident[0:n, 0:n])
                n = DEC * CBUF
                pe.transpose(pair[p][:, 1, k * n:(k + 1) * n], rawC[0:n, ks], ident[0:n, 0:n])
                pe.transpose(pair[p][:, 1, 96 + k * DEC:96 + (k + 1) * DEC], rawH[0:DEC, ks], ident[0:DEC, 0:DEC])
            J.made_by(pe.transpose(pair[p][:, 1, 128:128 + NROWS], rawR[0:NROWS, :], ident[0:NROWS, 0:NROWS]))
            pe.wait_ge(x_in, 16 * NTT)
            for k in range(KD):
                p = J.begin(pe, ("xT", k))
                for t, (t0, n) in enumerate(TILES):
                    out = pair[p][:, t // TT, t0 % SEQ:t0 % SEQ + n]
                    ins = pe.transpose(out, xraw[0:n, t, k * P:(k + 1) * P], ident[0:n, 0:n])
                J.made_by(ins)
            for k in range(KD):
                sum_squares(k, hT, k == 0, k == KD - 1)
            spread("nb1")
            ready = normed_tiles(0, "nb1", KD)
            for j, m0 in enumerate((4, 8)):
                pe.wait_ge(win_in[j], 16)
                for m in range(m0, m0 + 4):
                    project(("z", m), lambda k: w_in_v[:, k, m * P:(m + 1) * P], lambda k: hT[:, k, :], range(KD), ready)
            pe.wait_ge(bd_in, 16 * 4)
            for i in range(KP):
                pe.wait_ge(conv_done, i + 1)
                for s, what in enumerate("ri"):
                    project((what, i), lambda k: bdw[:, s, i, :], lambda k: cT[:, i, :], range(1))
            pe.wait_ge(win_in[2], 16)
            for m in range(4):
                project(("z", m), lambda k: w_in_v[:, k, m * P:(m + 1) * P], lambda k: hT[:, k, :], range(KD))
            p = J.begin(pe, "st")
            J.wait_taken(pe, ("z", 3))
            for i in range(KP):
                pe.transpose(pair[p][0:CBUF + DEC, 0, i * P:(i + 1) * P], uR[:, i, SEQ:CBUF + NT], ident[:, :])
                ins = pe.transpose(pair[p][0:PBUF + DEC, 1, i * P:(i + 1) * P], uP[:, i, SEQ:PBUF + NT], ident[:, :])
            J.made_by(ins)
            pe.wait_ge(mem_scaled, MT)
            for q in range(2):
                p = J.begin(pe, ("mT", q))
                for j in range(4):
                    for t in range(MT):
                        k = 4 * q + j
                        ins = pe.transpose(pair[p][:, j // 2, (j % 2) * NMEM + t * P:(j % 2) * NMEM + (t + 1) * P],
                                           mraw[:, t, k * P:(k + 1) * P], ident[:, :])
                J.made_by(ins)
            for what, w, arrived in (("K", wk_v, wk_in), ("V", wv_v, wv_in)):
                pe.wait_ge(arrived, 16)
                for t in range(MT):
                    p = J.begin(pe, (what, t))
                    for k in range(KD):
                        if what == "K" and t == 0:
                            J.wait_taken(pe, ("mT", k // 4))
                        for h in range(2):
                            ins = pe.matmul(pair[p][:, h, :], mT[:, k, t * P:(t + 1) * P], w[:, k, h * 512:(h + 1) * 512],
                                            start=k == 0, stop=k == KD - 1)
                    J.made_by(ins)
            for q in range(2):
                p = J.begin(pe, ("KT", q))
                if q == 0:
                    J.wait_taken(pe, ("K", 1))
                for j in range(4):
                    for t in range(MT):
                        k = 4 * q + j
                        ins = pe.transpose(pair[p][:, j // 2, (j % 2) * NMEM + t * P:(j % 2) * NMEM + (t + 1) * P],
                                           Kt[:, t, k * P:(k + 1) * P], ident[:, :])
                J.made_by(ins)
            pe.wait_ge(plw_in, 16)
            for g in range(KP):
                pe.wait_ge(d_ready, g + 1)
                project(("yp", g), lambda k: plw[:, g, :], lambda k: dT[:, g, :], range(1))
            for k in range(KP):
                sum_squares(k, sqP, k == 0, k == KP - 1)
            spread("nbp")
            for k in range(KP):
                sum_squares(k, rT, k == 0, k == KP - 1)
            spread("nbr")
            p = J.begin(pe, "hl")
            for i in range(KP):
                ins = pe.transpose(pair[p][0:1 + DEC, 0, i * P:(i + 1) * P], cT[:, i, SEQ - 1:NT], ident[:, :])
            J.made_by(ins)

            def into_residual(what, w, arrived, acts, ready):
                pe.wait_ge(arrived, 16)
                for m in range(KD):
                    project((what, m), lambda k: w[:, k, m * P:(m + 1) * P], acts, range(KD), ready if m == 0 else None)
                    if m:
                        sum_squares(m - 1, sqT, m == 1, False)
                sum_squares(KD - 1, sqT, False, True)

            rp = normed_tiles(KD - 1, "nbp", KP)
            rr = normed_tiles(KD - 1 + KP - 1, "nbr", KP)
            into_residual("x1", view(regB, 0, KD, D), wout_in, lambda k: dT[:, k, :] if k < KP else gT[:, k - KP, :],
                          lambda k: rp(k) if k < KP else rr(k - KP))
            spread("nb2")
            base = KD - 1 + 2 * (KP - 1)
            ready = normed_tiles(base, "nb2", KD)
            pe.wait_ge(wq_in, 16)
            wq_v = view(regC, 0, KD, D)
            for m in range(KD):
                project(("q", m), lambda k: wq_v[:, k, m * P:(m + 1) * P], lambda k: hT[:, k, :], range(KD), ready if m == 0 else None)
            p = J.begin(pe, "qs")
            for k in range(KD):
                J.wait_taken(pe, ("q", k))
                ins = pe.transpose(pair[p][0:DEC, k // 4, (k % 4) * P:(k % 4 + 1) * P], qT[:, k, SEQ:NT], ident[:, :])
            J.made_by(ins)
            steps = [(h, t) for h in range(HEADS) for t in range(TT)]
            for n in range(len(steps) + 2):
                if n < len(steps):
                    h, t = steps[n]
                    p = J.begin(pe, ("s", h, t))
                    for k in range(2):
                        ins = pe.matmul(pair[p][:, 0, 0:NMEM], qT[:, 2 * h + k, t * P:(t + 1) * P], KT[:, 2 * h + k, :],
                                        start=k == 0, stop=k == 1)
                    J.made_by(ins)
                if n >= 2:
                    h, t = steps[n - 2]
                    p = J.begin(pe, ("pT", h, t))
                    pe.wait_ge(att_norm, n - 1)
                    for m in range(MT):
                        ins = pe.transpose(pair[p][:, 0, m * P:(m + 1) * P], pr[:, (n - 2) % 4, m * P:(m + 1) * P], ident[:, :])
                    J.made_by(ins)
                    if t == TT - 1:
                        for cc in range(2):
                            p = J.begin(pe, ("o", h, cc))
                            J.wait_taken(pe, ("pT", h, t))
                            for m in range(MT):
                                lo = h * HD + cc * P
                                ins = pe.matmul(pair[p][:, 0, :], Vt[:, m, lo:lo + P], PT[:, h % 2, m, :], start=m == 0, stop=m == MT - 1)
                            J.made_by(ins)
            nb = DEC * HEADS
            p = J.begin(pe, "sS")
            pe.wait_ge(qb_used, DEC)
            for m in range(MT):
                ins = pe.transpose(pair[p][0:nb, 0, m * P:(m + 1) * P], sS[:, m, :], ident[:, :])
            J.made_by(ins)
            p = J.begin(pe, "pS")
            pe.wait_ge(s_norm, 1)
            for m in range(MT):
                ins = pe.transpose(pair[p][:, 0, m * nb:(m + 1) * nb], pSm[0:nb, m * P:(m + 1) * P], ident[0:nb, 0:nb])
            J.made_by(ins)
            p = J.begin(pe, "oS")
            J.wait_taken(pe, "pS")
            for b in range(DEC):
                pe.wait_ge(*((v_in[1], 64) if b < 4 else (v_in[0], 32) if b < 6 else (v_in[2], 32)))
                for k in range(KD):
                    for m in range(MT):
                        col = b * HEADS + k // 2
                        ins = pe.matmul(pair[p][:, 0, k * DEC + b:k * DEC + b + 1], vc[b][:, m, k * P:(k + 1) * P],
                                        pST[:, m, col:col + 1], start=m == 0, stop=m == MT - 1)
            J.made_by(ins)
            into_residual("x2", view(regB, 0, KD, D), wo_in, lambda k: oT[:, k, :], lambda k: J.wait_taken(pe, "oS"))
            spread("nb3")
            base += KD - 1
            ready = normed_tiles(base, "nb3", KD)
            p = J.begin(pe, "rt")
            pe.wait_ge(rw_in, 32)
            for t, (t0, n) in enumerate(TILES):
                for k in range(KD):
                    ready(k)
                    ins = pe.matmul(pair[p][0:n, 0, t * NE:(t + 1) * NE], hT[:, k, t0:t0 + n], rw[:, k, :], start=k == 0, stop=k == KD - 1)
            J.made_by(ins)

            def rows_of(name, src, t0, n):
                p = J.begin(pe, name)
                for k in range(KD):
                    ins = pe.transpose(pair[p][0:n, k // 4, (k % 4) * P:(k % 4 + 1) * P], src[:, k, t0:t0 + n], ident[:, :])
                J.made_by(ins)

            for t, (t0, n) in enumerate(TILES):
                rows_of(("hR", t), hT, t0, n)
            pe.wait_ge(sh_in, 48)
            for m in range(KF):
                project(("sg", m), lambda k: sgw[:, k, m * P:(m + 1) * P], lambda k: hT[:, k, :], range(KD))
                project(("su", m), lambda k: suw[:, k, m * P:(m + 1) * P], lambda k: hT[:, k, :], range(KD))
            p = J.begin(pe, "pos")
            pe.wait_ge(masked, 1)
            for t in range(NTT):
                for s in range(t + 1):
                    pe.matmul(pair[p][:, 0, t * NE:(t + 1) * NE], low if s == t else ones[:, :], msk[:, s, :], start=s == 0, stop=s == t)
            for s in range(NTT):
                ins = pe.matmul(pair[p][:, 0, NTT * NE:(NTT + 1) * NE], ones[:, :], msk[:, s, :], start=s == 0, stop=s == NTT - 1)
            J.made_by(ins)
            p = J.begin(pe, "tab")
            pe.wait_ge(tab_ready, 1)
            J.made_by(pe.transpose(pair[p][0:1, 0, 0:P], ebc[:, 0:1], ident[:, :]))
            for t, (t0, n) in enumerate(TILES):
                rows_of(("xR", t), xT, t0, n)
                p = J.begin(pe, ("sd", t))
                for m in range(KF):
                    J.wait_taken(pe, ("su", m))
                    for h in range(2):
                        ins = pe.matmul(pair[p][0:n, h, :], sA[:, m, t0:t0 + n], sdw[:, m, h * 512:(h + 1) * 512],
                                        start=m == 0, stop=m == KF - 1)
                J.made_by(ins)

            pe.sem_inc(gu_made, RING)
            pe.sem_inc(down_made, RING)
            pe.sem_inc(turned, RING)
            pe.wait_ge(row_table, 1)
            n_turns = turns(pe)
            J.wait_taken(pe, ("xR", NTT - 1))
            J.wait_taken(pe, ("sd", NTT - 1))
            J.wait_taken(pe, "pos")

            def slots(b):
                pe.wait_ge(onehot, b + 1)
                for t in range(NTT):
                    ins = pe.matmul(pS[:, 0, 0:2], oneh[:, t, :], rhsw[:, t, :], start=t == 0, stop=t == NTT - 1)
                ins.then_inc(slots_made, 1)

            def turn(r, b, q, first=False):
                pe.wait_ge(gath_in[r], q * 16 + 16)
                if not first:
                    pe.wait_ge(turned_a, b)
                    pe.wait_ge(turned_d, b)
                g3 = gath[r].rearrange("p (f k) -> p k f", k=KD)
                for k in range(KD):
                    ins = pe.transpose(pair[1][:, k // 4, (k % 4) * P:(k % 4 + 1) * P], g3[:, k, :], ident[:, :])
                ins.then_inc(turned, 1)

            def gate_up(r, b, q, ks, first=False):
                if ks[0] == 0:
                    pe.wait_ge(wg_in[r], q * 32 + 32)
                    pe.wait_ge(turned_a, b + 1)
                    pe.wait_ge(turned_d, b + 1)
                    if not first:
                        pe.wait_ge(act_b, b)
                w = WG[r].rearrange("p s (k f) -> p s k f", k=KD)
                for k in ks:
                    ins = pe.matmul(pair[0][:, 0, :].rearrange("p (s f) -> p s f", s=2), hX[:, k, :], w[:, :, k, :],
                                    start=k == 0, stop=k == KD - 1, skip_group_check=True)
                if ks[-1] == KD - 1:
                    ins.then_inc(gu_made, 1)

            def turn_act(b):
                pe.wait_ge(act_b, b + 1)
                a3 = act.rearrange("p (f k) -> p k f", k=KF)
                for k in range(KF):
                    ins = pe.transpose(pair[0][:, 1, k * P:(k + 1) * P], a3[:, k, :], ident[:, :])
                ins.then_inc(at_made, 1)

            def down(r, b, q):
                pe.wait_ge(at_taken, b + 1)
                pe.wait_ge(wd_in[r], q * 16 + 16)
                pe.wait_ge(down_a, b + 1)
                pe.wait_ge(down_d, b + 1)
                for k in range(KF):
                    for h in range(2):
                        ins = pe.matmul(pair[2][:, h, :], aX[:, k, :], WD[r][:, k, h * 512:(h + 1) * 512],
                                        start=k == 0, stop=k == KF - 1)
                ins.then_inc(down_made, 1)

            slots(0)
            for b in (1, 2):
                pe.wait_ge(idx_ready, b)
                slots(b)
            turn(0, 0, 0, first=True)
            gate_up(0, 0, 0, range(KD), first=True)
            turn(1, 1, 0)
            with pe.Fori(0, n_turns) as i:
                for j in range(RING):
                    b = i * RING + (j + 1)
                    pe.wait_ge(idx_ready, b + 2)
                    slots(b + 2)
                    gate_up((j + 1) % RING, b, i + (j + 1) // RING, range(0, 4))
                    turn_act(b - 1)
                    gate_up((j + 1) % RING, b, i + (j + 1) // RING, range(4, KD))
                    turn((j + 2) % RING, b + 1, i + (j + 2) // RING)
                    down(j, b - 1, i)
            turn_act(n_turns * RING)
            down(0, n_turns * RING, n_turns)


_INS = ["x_prompt", "x_sample", "state_pool", "state_conv", "state_h", "cache_mem_k", "cache_mem_v", "mem_prompt",
        "norm_mix", "w_in", "pool_w", "pool_scale", "conv_w", "conv_b", "gate_a_w", "gate_a_b", "gate_x_w",
        "gate_x_b", "lru_lambda", "norm_pool_out", "norm_rnn_out", "w_out", "norm_xattn", "norm_mem", "xa_wq",
        "xa_wk", "xa_wv", "xa_wo", "norm_ffn", "router_w", "router_bias", "exp_w_gate", "exp_w_up", "exp_w_down",
        "sh_w_gate", "sh_w_up", "sh_w_down", "norm_final"]
_OUTS = [(1, SEQ, D), (DEC, 1, D), (1, 1, PBUF, DP), (1, 1, CBUF, DP), (1, 1, DP), (1, 1, NMEM, HEADS, HD),
         (1, 1, NMEM, HEADS, HD), (1, DEC, PBUF, DP), (1, DEC, CBUF, DP), (1, DEC, DP)]


def kernel(**inputs):
    import numpy as _np
    import concourse.bacc as _bacc
    from concourse.bass_utils import run_bass_kernel_spmd as _run

    nc = _bacc.Bacc("TRN2", target_bir_lowering=False, num_devices=1)
    arrays, args = {}, []
    for name in _INS:
        a = _np.ascontiguousarray(inputs[name])
        arrays[f"in_{name}"] = a
        args.append(nc.dram_tensor(f"in_{name}", a.shape, F32, kind="ExternalInput").ap())
    for i, shape in enumerate(_OUTS):
        args.append(nc.dram_tensor(f"out_{i}", shape, F32, kind="ExternalOutput").ap())
    for name, shape in (("h_rows", (NT, D)), ("acc_rows", (NT, D)), ("q_rows", (DEC, D))):
        args.append(nc.dram_tensor(name, shape, F32, kind="Internal").ap())
    trunk(nc, *args)
    r = _run(nc, [arrays], core_ids=[0])
    return tuple(r.results[0][f"out_{i}"] for i in range(len(_OUTS)))
```

```python
from contextlib import ExitStack

import concourse.bass as bass
from concourse import mybir

F32, I32, U32, BF16 = mybir.dt.float32, mybir.dt.int32, mybir.dt.uint32, mybir.dt.bfloat16
F32R = mybir.dt.float32r
ACT, ALU, AX = mybir.ActivationFunctionType, mybir.AluOpType, mybir.AxisListType

P = 128
D = 1024
KD = D // P
SEQ, DEC = 512, 8
NT = SEQ + DEC
HALF = NT // 2
TT = SEQ // P
TILES = [(t * P, P) for t in range(TT)] + [(SEQ, DEC)]
NTT = len(TILES)
DP = D // 2
KP = DP // P
WINDOWS = (2, 4, 8, 16)
PBUF, CBUF = 15, 3
NMEM, MT = 256, 2
HEADS, HD = 4, 256
NE, NG, EG, TOPG = 64, 8, 8, 4
FE, KF = 256, 2
EPS = 1e-6
SCALE = HD ** -0.5
LRU_C = 8.0
ROUTED = 2.5
FAR = 1024
HALF_K = KD // 2
SPLIT_RING = 3
SLOTS = 96
RING = 3
STEPS = [(h, t) for h in range(HEADS) for t in range(TT)]
BEHIND = 3

ROWS = [("norm_mix", 8), ("norm_xattn", 8), ("norm_mem", 8), ("norm_ffn", 8), ("pool_scale", 4), ("conv_w", 16),
        ("conv_b", 4), ("gate_a_b", 4), ("gate_x_b", 4), ("lru_lambda", 4), ("norm_pool_out", 4), ("norm_rnn_out", 4)]
COL, NROWS = {}, 0
for _n, _k in ROWS:
    COL[_n] = NROWS
    NROWS += _k


class Count:

    def __init__(self):
        self.n = {}

    def add(self, ins, sem, k=1):
        ins.then_inc(sem, k)
        self.n[id(sem)] = self.n.get(id(sem), 0) + k
        return sem, self.n[id(sem)]


class Products:

    def __init__(self, order, made, taken):
        self.names = [o[0] for o in order]
        self.no = {n: j for j, n in enumerate(self.names)}
        self.by = [o[1] for o in order]
        self.made, self.taken = made, taken
        self.at = [self.by[:j + 1].count(e) for j, e in enumerate(self.by)]
        self.began, self.sent = 0, dict.fromkeys(taken, 0)
        self.place, self.before, last, nxt = [], [], {}, 0
        for j, o in enumerate(order):
            single = len(o) > 2
            nxt = (nxt if single else nxt + nxt % 2) % 6
            banks = (nxt,) if single else (nxt, nxt + 1)
            self.place.append(nxt if single else nxt // 2)
            self.before.append([last[b] for b in banks if b in last])
            last.update((b, j) for b in banks)
            nxt += len(banks)

    def begin(self, pe, name):
        j = self.no[name]
        assert j == self.began, (name, self.names[self.began])
        self.began += 1
        for e in self.taken:
            earlier = [i for i in self.before[j] if self.by[i] == e]
            if earlier:
                pe.wait_ge(self.taken[e], self.at[max(earlier)])
        return self.place[j]

    def made_by(self, ins):
        ins.then_inc(self.made, 1)

    def wait_made(self, eng, name):
        j = self.no[name]
        eng.wait_ge(self.made, j + 1)
        return self.place[j]

    def take(self, ins, name):
        j = self.no[name]
        e = self.by[j]
        self.sent[e] += 1
        assert self.sent[e] == self.at[j], name
        ins.then_inc(self.taken[e], 1)
        return self.taken[e], self.at[j]

    def wait_taken(self, eng, name):
        j = self.no[name]
        eng.wait_ge(self.taken[self.by[j]], self.at[j])


class SplitWeights:

    def __init__(self, J, names, weights, arrived, parts, hi_made, lo_made, half_used):
        self.J, self.names, self.weights, self.arrived, self.parts = J, names, weights, arrived, parts
        self.hi_made, self.lo_made, self.half_used = hi_made, lo_made, half_used
        self.units = 2 * len(names)

    def cut_hi(self, a, u):
        if u >= self.units:
            return
        if u in self.arrived:
            a.wait_ge(self.arrived[u], 16)
        old = u - SPLIT_RING
        if old >= 0 and old % 2:
            a.wait_ge(self.J.made, self.J.no[self.names[old // 2]] + 1)
        elif old >= 0:
            a.wait_ge(self.half_used, old // 2 + 1)
        a.copy(self.parts[:, u % SPLIT_RING, 0], self.weights(u // 2, u % 2)).then_inc(self.hi_made, 1)

    def cut_lo(self, v, u):
        if u >= self.units:
            return
        v.wait_ge(self.hi_made, u + 1)
        v.tensor_tensor(self.parts[:, u % SPLIT_RING, 1], self.weights(u // 2, u % 2),
                        self.parts[:, u % SPLIT_RING, 0].bitcast(F32), ALU.subtract).then_inc(self.lo_made, 1)

    def product(self, pe, pair, n, acts_hi, acts_lo, ready=None):
        p = self.J.begin(pe, self.names[n])
        for u in (2 * n, 2 * n + 1):
            pe.wait_ge(self.lo_made, u + 1)
            for j in range(HALF_K):
                k = (u % 2) * HALF_K + j
                if ready:
                    ready(k)
                hi, lo = self.parts[:, u % SPLIT_RING, 0, j, :], self.parts[:, u % SPLIT_RING, 1, j, :]
                for h in range(2):
                    cols = slice(h * HALF, (h + 1) * HALF)
                    for i, (w, x) in enumerate(((hi, acts_hi), (lo, acts_hi), (hi, acts_lo))):
                        ins = pe.matmul(pair[p][:, h, 0:HALF], w, x[:, k, cols], start=k == 0 and i == 0,
                                        stop=k == KD - 1 and i == 2)
            if u % 2 == 0:
                ins.then_inc(self.half_used, 1)
        self.J.made_by(ins)


def product_order():
    o = [(("xT", t), "dve") for t in range(NTT)] + [("par", "dve"), ("nb1", "dve"), ("sta", "dve")]
    o += [(("z", m), "act") for m in (4, 5, 6, 7, 8, 9, 10, 11)]
    for i in range(KP):
        o += [(("r", i), "act"), (("i", i), "act")]
    o += [(("mT", q), "act") for q in range(2)]
    o += [(("z", m), "act") for m in range(4)] + [("st", "act")]
    o += [(("K", t), "act") for t in range(MT)] + [(("V", t), "act") for t in range(MT)] + [(("KT", q), "act") for q in range(2)]
    o += [(("yp", g), "act") for g in range(KP)] + [("nbp", "dve"), ("nbr", "dve"), ("hl", "act")]
    o += [(("x1", m), "dve") for m in range(KD)] + [("nb2", "dve")]
    o += [(("q", m), "act") for m in range(KD)] + [("qs", "act")]
    for n in range(len(STEPS) + BEHIND):
        if n < len(STEPS):
            o.append((("s", *STEPS[n]), "act", 1))
        if n >= BEHIND:
            h, t = STEPS[n - BEHIND]
            o.append((("pT", h, t), "act", 1))
            if h and t < 2:
                o.append((("o", h - 1, t), "act", 1))
    o += [(("o", HEADS - 1, 0), "act", 1), ("sS", "act", 1), (("o", HEADS - 1, 1), "act", 1)]
    o += [("pS", "act", 1), ("oS", "act"), ("oST", "act", 1)]
    o += [(("x2", m), "dve") for m in range(KD)] + [("nb3", "dve")]
    o += [("rt", "act")]
    o += [(("hR", t), "act") for t in range(NTT)]
    for m in range(KF):
        o += [(("sg", m), "act"), (("su", m), "dve")]
    o += [("pos", "dve"), (("xR", 0), "act"), (("xR", 1), "act"), ("tab", "dve"), (("sd", 0), "dve"), (("sd", 1), "dve")]
    for t in range(2, NTT):
        o += [(("xR", t), "act"), (("sd", t), "dve")]
    return o


def trunk(nc, x_prompt, x_sample, state_pool, state_conv, state_h, cache_mem_k, cache_mem_v, mem_prompt, norm_mix,
          w_in, pool_w, pool_scale, conv_w, conv_b, gate_a_w, gate_a_b, gate_x_w, gate_x_b, lru_lambda,
          norm_pool_out, norm_rnn_out, w_out, norm_xattn, norm_mem, xa_wq, xa_wk, xa_wv, xa_wo, norm_ffn, router_w,
          router_bias, exp_w_gate, exp_w_up, exp_w_down, sh_w_gate, sh_w_up, sh_w_down, norm_final,
          y_prompt, y_sample, new_pool_p, new_conv_p, new_h_p, new_k, new_v, new_pool_s, new_conv_s, new_h_s,
          h_rows, acc_rows, q_rows):
    with ExitStack() as ctx:
        def sb(name, shape, dt=F32):
            return ctx.enter_context(nc.sbuf_tensor(name, shape, dt))

        def sem(name):
            return ctx.enter_context(nc.semaphore(name))

        xT = sb("xT", [P, KD, NT])
        with nc.sbuf_tensor("h_hi", [P, KD, NT], F32R) as h_hi:
            pass
        hT = sb("hT", [P, KD, NT])
        with nc.sbuf_tensor("unused_A1", [P, 2048], F32), nc.sbuf_tensor("wout_parts", [P, SPLIT_RING, 2, HALF_K, P], F32R) as wout_parts:
            pass
        with nc.sbuf_tensor("unused_A", [P, 8192], F32), nc.sbuf_tensor("wq_parts", [P, SPLIT_RING, 2, HALF_K, P], F32R) as wq_parts:
            pass
        regA = sb("regA", [P, 12288])
        regB = sb("regB", [P, 8192])
        with nc.sbuf_tensor("h1_lo", [P, KD, NT], F32R) as h1_lo, nc.sbuf_tensor("win_parts", [P, SPLIT_RING, 2, HALF_K, P], F32R) as win_parts:
            pass
        regC = sb("regC", [P, 8192])
        with nc.sbuf_tensor("y_lo", [P, KD, NT], F32R) as y_lo:
            pass
        with nc.sbuf_tensor("unused_L", [P, 4160], F32), nc.sbuf_tensor("h2_lo", [P, KD, NT], F32R) as h2_lo:
            pass
        regL = sb("regL", [P, 14640])
        par = sb("par", [P, NROWS])
        ident = sb("ident", [P, P])
        ones = sb("ones", [P, P])
        small = sb("small", [P, 160])

        def view(reg, at, *shape):
            n = 1
            for s in shape:
                n *= s
            v = reg[:, at:at + n]
            if len(shape) == 2:
                v = v.rearrange("p (a b) -> p a b", a=shape[0])
            elif len(shape) == 3:
                v = v.rearrange("p (a b c) -> p a b c", a=shape[0], b=shape[1])
            return v

        ssq, rs = small[:, 0:5], small[:, 5:10]
        mss, mrs = small[:, 10:12], small[:, 12:14]
        eps_c = small[:, 14:15]
        nsp, psp = small[:, 16:20], small[:, 20:24]
        spt = small[:, 24:64]
        r15 = small[:, 64:80]
        amax, asum = small[:, 80:84], small[:, 84:88]
        nmax, rsum = small[:, 88:92], small[:, 92:96]
        smx, snm, sss, srs = (small[:, 96 + j:97 + j] for j in range(4))
        zero5 = small[:, 104:109]
        fin = small[:, 110:130]

        w_in_v = [view(regA, KD * DP * j, KD, DP) for j in range(3)]
        xraw = view(regL, 6312, NTT, D)
        xsq = view(regL, 11432, D)
        htmp1, ytmp, htmp2 = view(regL, 11432, 2, NT), view(regL, 12552, 2, NT), view(regL, 8320, 2, NT)
        rawP, rawC, rawH = view(regL, 4232, DP), view(regL, 4232 + DP, DP), view(regL, 4232 + 2 * DP, DP)
        rawR = view(regL, 4232 + 3 * DP, P)
        uP = view(regL, 0, KP, PBUF + NT)
        uR = view(regL, 2140, KP, CBUF + NT)
        aT = view(regL, 2140, KP, NT)
        gT = view(regL, 4232, KP, NT)
        cT = view(regL, 6312, KP, NT)
        rT = view(regL, 8392, KP, NT)
        iT = view(regL, 10472, KP, NT)
        sqT = view(regL, 8392, KD, NT)
        stP = view(regL, 12552, KP, DEC, PBUF)
        stC = view(regL, 13032, KP, DEC, CBUF)
        stH = view(regL, 13128, KP, DEC)
        bdw = view(regL, 13160, 2, KP, P)
        hflat = hT[:, :, :].rearrange("p k n -> p (k n)")
        dT = hT[:, 0:KP, :]
        ptmp = [hflat[:, 2080 + 535 * j:2080 + 535 * (j + 1)] for j in range(2)]
        a2 = hflat[:, 3150:3670]
        sqP = view(regL, 0, KP, NT)
        stO = view(regA, 8192, 2, DP)
        plw = view(regA, 10240, KP, P)
        hlO = view(regA, 9216, DP)
        wk_v, wv_v = view(regB, 0, KD, D), view(regC, 0, KD, D)
        mraw = view(regA, 0, MT, D)
        KT = view(regA, 0, KD, NMEM)
        mT = view(regA, 2048, KD, NMEM)
        msq = view(regA, 2048, MT, D)
        Kt, Vt = view(regA, 4096, MT, D), view(regA, 6144, MT, D)
        qT = view(regL, 0, KD, NT)
        PT = view(regL, 4160, 2, MT, SEQ)
        kc = [view(regL, 6208 + 2048 * j, MT, D) for j in range(2)]
        kroom = [view(regB, 2048 * j, MT, D) for j in range(4)]
        kcache = kroom + kc + kroom[0:2]
        vspare = [view(regL, 10304, MT, D), view(regL, 12352, MT, D)]
        qb = view(regA, 8192, 2, D)
        pr = view(regA, 10240, 4, NMEM)
        sS = view(regA, 11264, MT, DEC * HEADS)
        pSm = view(regA, 11328, NMEM)
        pad8 = view(regA, 11648, MT * HEADS, DEC * DEC)
        oSr = view(regA, 10240, D)
        qsr = view(regL, 5184, D)
        oT = hT
        vc = [view(regC, 2048 * j, MT, D) for j in range(4)] + vspare + [view(regA, 2048, MT, D), view(regA, 4096, MT, D)]
        sgw, suw = view(regC, 0, KD, FE), view(regC, 2048, KD, FE)
        sdw = view(regC, 4096, KF, D)
        rw = view(regC, 6144, KD, NE)
        sco = view(regC, 6656, NTT, NE)
        bia = view(regC, 6976, NTT, NE)
        rbias = view(regC, 7296, NE)
        msk = view(regC, 7360, NTT, NE)
        gwt = view(regC, 7680, NTT, NE)
        rows = view(regL, 0, NTT, D)
        sA = view(regL, 5120, KF, NT)
        m8 = view(regL, 6160, NTT, NG * 8)
        gs = view(regL, 6480, NTT, NG)
        g8 = view(regL, 6520, NTT, 8)
        gi = view(regL, 6560, NTT, 8)
        gif = view(regL, 6600, NTT, 8)
        gmk = view(regL, 6640, NTT, NG)
        geq = view(regL, 6680, NTT, NG)
        pen = view(regL, 6720, NTT, NG)
        top = view(regL, 6760, NTT, 8)
        mrep = view(regL, 6800, NTT, NE)
        wsu = view(regL, 7120, NTT)
        valid = view(regL, 7125, NTT)
        iot8 = view(regL, 7130, NG)
        low = view(regL, 7140, P)
        slot = view(regL, 7268, NTT, NE)
        nblk, bend, bbase = view(regL, 7588, NE), view(regL, 7652, NE), view(regL, 7716, NE)
        iotp = view(regL, 7780, 1)
        ebc = view(regL, 7781, 2)
        j3 = view(regL, 7784, 48)
        cmp = view(regL, 7832, NE)
        iots = view(regL, 7896, SLOTS)
        NI = view(regL, 8024, 8)
        ET = view(regL, 8032, P)
        oneh = view(regL, 8160, NTT * SLOTS // 2).bitcast(BF16).rearrange("p (t n) -> p t n", t=NTT)
        whole, part = view(regL, 8400, NTT, 2), view(regL, 8410, NTT, NE)
        rhsw = view(regL, 8730, 16).bitcast(BF16)[:, 0:NTT * 6].rearrange("p (t c) -> p t c", t=NTT)
        wparts = view(regL, 13688, 3 * NTT * NE // 2).bitcast(BF16).rearrange("p (c t e) -> p c t e", c=3, t=NTT)
        idx = view(regL, 8810, RING)
        sums = view(regL, 8800, RING, 2)
        sidx = view(regL, 8816, RING)
        swl = view(regL, 8819, RING)
        gath = [view(regL, 8824 + D * j, D) for j in range(RING)]
        hX = view(regL, 11896, KD, SLOTS)
        sil = view(regL, 12920, FE)
        act = view(regL, 13176, FE)
        aX = view(regL, 13432, KF, SLOTS)
        yX = [view(regL, 0 + D * j, D) for j in range(RING)]
        WG = [view(regA, 0, 2, KD * FE), view(regA, 6144, 2, KD * FE), view(regB, 0, 2, KD * FE)]
        WD = [view(regA, 4096, KF, D), view(regA, 10240, KF, D), view(regB, 4096, KF, D)]
        yf = view(regA, 0, NTT, D)
        gfin = view(regC, 0, D)
        junk = view(regC, 1024, D)

        pair = [ctx.enter_context(nc.psum_tensor(f"pair{j}", [P, 2, 512], F32)) for j in range(3)]
        bank = [pair[j // 2][:, j % 2, :] for j in range(6)]
        pS = ctx.enter_context(nc.psum_tensor("pS", [P, 2, 512], F32))

        made, act_took, dve_took = sem("made"), sem("act_took"), sem("dve_took")
        J = Products(product_order(), made, {"act": act_took, "dve": dve_took})
        x_in, rows_in, states_in, mem_in = [sem(f"x_in{t}") for t in range(NTT)], sem("rows_in"), sem("states_in"), sem("mem_in")
        win_in = [sem(f"win_in{j}") for j in range(4)]
        h_made, h_hi_made, h_lo_made = sem("h_made"), sem("h_hi_made"), sem("h_lo_made")
        split_z = [sem(s) for s in ("win_hi", "win_lo", "win_half_used")]
        split_o = [sem(s) for s in ("wout_hi", "wout_lo", "wout_half_used")]
        split_q = [sem(s) for s in ("wq_hi", "wq_lo", "wq_half_used")]
        wk_in, wv_in, bd_in, plw_in = sem("wk_in"), sem("wv_in"), sem("bd_in"), sem("plw_in")
        wout_in, wq_in, wo_in, sh_in, rw_in = sem("wout_in"), sem("wq_in"), sem("wo_in"), sem("sh_in"), sem("rw_in")
        consts, bd_zero = sem("consts"), sem("bd_zero")
        dve_step, act_step, pool_step = sem("dve_step"), sem("act_step"), sem("pool_step")
        squares, ss_done, root, inverse, normed = sem("squares"), sem("ss_done"), sem("root"), sem("inverse"), sem("normed")
        mem_scaled, mem_ss, mem_inv = sem("mem_scaled"), sem("mem_ss"), sem("mem_inv")
        conv_done, lru_a, lru_s, lru_m2, lru_m, y_rnn, padded = (
            sem(s) for s in ("conv_done", "lru_a", "lru_s", "lru_m2", "lru_m", "y_rnn", "padded"))
        sp_ready, pooled, d_ready = sem("sp_ready"), sem("pooled"), sem("d_ready")
        stored = sem("stored")
        q_stored, qb_in, qb_used = sem("q_stored"), [sem("qb_in0"), sem("qb_in1")], sem("qb_used")
        kc_in, kb_in, v_in = [sem(f"kc_in{b}") for b in range(4, DEC)], sem("kb_in"), [sem(f"v_in{j}") for j in range(3)]
        kv_stored = sem("kv_stored")
        att_max, att_inv, att_norm = sem("att_max"), sem("att_inv"), sem("att_norm")
        s_max, s_exp, s_norm, s_score = sem("s_max"), sem("s_exp"), sem("s_norm"), sem("s_score")
        silu_done, gated, routed = sem("silu_done"), sem("gated"), sem("routed")
        h_stored, acc_ready, sums_landed, rows_left, clear = sem("h_stored"), sem("acc_ready"), sem("sums_landed"), sem("rows_left"), sem("clear")
        masked, row_table = sem("masked"), sem("row_table")
        wg_in, wd_in = [sem(f"wg_in{j}") for j in range(RING)], [sem(f"wd_in{j}") for j in range(RING)]
        onehot, counted, slots_made, summed, idx_ready = (sem(s) for s in ("onehot", "counted", "slots_made", "summed", "idx_ready"))
        sp_in, sp_exp, tab_ready = sem("sp_in"), sem("sp_exp"), sem("tab_ready")
        gath_in = [sem(f"gath_in{j}") for j in range(RING)]
        turned, turned_a, turned_d, gu_made, silu_b, act_b = (sem(s) for s in ("turned", "turned_a", "turned_d", "gu_made", "silu_b", "act_b"))
        at_made, at_taken, down_made, down_a, down_d, sidx_ready = (
            sem(s) for s in ("at_made", "at_taken", "down_made", "down_a", "down_d", "sidx_ready"))
        sco_ones = sem("sco_ones")
        fin_in = [sem(f"fin_in{t}") for t in range(NTT)]
        fin_ss, fin_root, fin_inv, fin_y, fin_g, sq_added = (sem(s) for s in ("fin_ss", "fin_root", "fin_inv", "fin_y", "fin_g", "sq_added"))

        z_order = [4, 5, 6, 7, 8, 9, 10, 11, 0, 1, 2, 3]
        wout_v, wq_v = view(regB, 0, KD, D), view(regC, 0, KD, D)
        Z = SplitWeights(J, [("z", m) for m in z_order],
                         lambda n, u: w_in_v[n // 4][:, u * HALF_K:(u + 1) * HALF_K, n % 4 * P:(n % 4 + 1) * P],
                         {0: win_in[3], 1: win_in[0], 8: win_in[1], 16: win_in[2]}, win_parts, *split_z)
        O = SplitWeights(J, [("x1", m) for m in range(KD)],
                         lambda n, u: wout_v[:, u * HALF_K:(u + 1) * HALF_K, n * P:(n + 1) * P],
                         {0: wout_in}, wout_parts, *split_o)
        Q = SplitWeights(J, [("q", m) for m in range(KD)],
                         lambda n, u: wq_v[:, u * HALF_K:(u + 1) * HALF_K, n * P:(n + 1) * P],
                         {0: wq_in}, wq_parts, *split_q)

        block = ctx.enter_context(nc.Block())
        halves = lambda v: v.rearrange("p (h n) -> p h n", h=2)

        def turns(eng):
            return eng.value_load(NI[0:1, 0:1].bitcast(I32), min_val=1, max_val=40)

        @block.sync
        def _(sp):
            xp = x_prompt.rearrange("o (t p) d -> p (o t) d", p=P)
            for t in range(TT):
                sp.dma_start(xraw[:, t, :], xp[:, t, :]).then_inc(x_in[t], 16)
            sp.dma_start(xraw[0:DEC, TT, :], x_sample.rearrange("b o d -> b (o d)")).then_inc(x_in[TT], 16)
            for name, src in (("norm_mix", norm_mix), ("norm_xattn", norm_xattn), ("norm_mem", norm_mem),
                              ("norm_ffn", norm_ffn), ("pool_scale", pool_scale), ("conv_b", conv_b),
                              ("gate_a_b", gate_a_b), ("gate_x_b", gate_x_b), ("lru_lambda", lru_lambda),
                              ("norm_pool_out", norm_pool_out), ("norm_rnn_out", norm_rnn_out)):
                k = dict(ROWS)[name]
                sp.dma_start(rawR[COL[name]:COL[name] + k, :], src.rearrange("o (k p) -> (o k) p", p=P)).then_inc(rows_in, 16)
            sp.dma_start(rawR[COL["conv_w"]:COL["conv_w"] + 16, :],
                         conv_w.rearrange("o w (k p) -> (o w k) p", p=P)).then_inc(rows_in, 16)
            win = w_in.rearrange("o (k p) n -> p (o k) n", p=P)
            for j, c in enumerate((1, 2, 0)):
                if j == 0:
                    sp.dma_start(w_in_v[j][:, 0:4, :], win[:, 0:4, c * DP:(c + 1) * DP]).then_inc(win_in[3], 16)
                    sp.dma_start(w_in_v[j][:, 4:8, :], win[:, 4:8, c * DP:(c + 1) * DP]).then_inc(win_in[j], 16)
                else:
                    sp.dma_start(w_in_v[j], win[:, :, c * DP:(c + 1) * DP]).then_inc(win_in[j], 16)
                if j == 0:
                    sp.wait_ge(bd_zero, 1)
                    for s, src in enumerate((gate_a_w, gate_x_w)):
                        for half in range(2):
                            lo = half * 64
                            sp.dma_start(bdw[lo:lo + 64, s, :, lo:lo + 64],
                                         src.rearrange("o (k two) i j -> two i (o k) j", two=2)[half]).then_inc(bd_in, 16)
            sp.dma_start(wk_v, xa_wk.rearrange("o (k p) n -> p (o k) n", p=P)).then_inc(wk_in, 16)
            sp.dma_start(new_pool_s[0, :, 0:PBUF - 1, :], state_pool[0, :, 1:PBUF, :]).then_inc(stored, 16)
            sp.dma_start(new_conv_s[0, :, 0:CBUF - 1, :], state_conv[0, :, 1:CBUF, :]).then_inc(stored, 16)
            sp.wait_ge(made, J.no[("z", 7)] + 1)
            sp.dma_start(mraw, mem_prompt.rearrange("o (t p) d -> p (o t) d", p=P)).then_inc(mem_in, 16)
            sp.wait_ge(made, J.no[("z", 3)] + 1)
            sp.dma_start(wv_v, xa_wv.rearrange("o (k p) n -> p (o k) n", p=P)).then_inc(wv_in, 16)
            sp.dma_start(plw, pool_w.rearrange("o g c d -> c (o g) d")).then_inc(plw_in, 16)
            sp.wait_ge(made, J.no[("K", 1)] + 1)
            sp.dma_start(view(regB, 0, KD, D), w_out.rearrange("o (k p) n -> p (o k) n", p=P)).then_inc(wout_in, 16)
            sp.wait_ge(made, J.no[("V", 1)] + 1)
            sp.dma_start(view(regC, 0, KD, D), xa_wq.rearrange("o (k p) n -> p (o k) n", p=P)).then_inc(wq_in, 16)
            J.wait_taken(sp, "st")
            sp.dma_start(new_conv_p[0, 0], stO[0:CBUF, 0, :]).then_inc(stored, 16)
            sp.dma_start(new_conv_s[0, :, CBUF - 1, :], stO[CBUF:CBUF + DEC, 0, :]).then_inc(stored, 16)
            sp.dma_start(new_pool_p[0, 0], stO[0:PBUF, 1, :]).then_inc(stored, 16)
            sp.dma_start(new_pool_s[0, :, PBUF - 1, :], stO[PBUF:PBUF + DEC, 1, :]).then_inc(stored, 16)
            J.wait_taken(sp, ("V", 1))
            sp.dma_start(new_k.rearrange("o b (t p) h d -> p (o b t) (h d)", p=P), Kt).then_inc(kv_stored, 16)
            sp.dma_start(new_v.rearrange("o b (t p) h d -> p (o b t) (h d)", p=P), Vt).then_inc(kv_stored, 16)
            ck = cache_mem_k.rearrange("o b (t p) h d -> p (o b) t (h d)", p=P)
            cv = cache_mem_v.rearrange("o b (t p) h d -> p (o b) t (h d)", p=P)
            J.wait_taken(sp, "hl")
            sp.dma_start(new_h_p[0], hlO[0:1, :]).then_inc(stored, 16)
            sp.dma_start(new_h_s[0], hlO[1:1 + DEC, :]).then_inc(stored, 16)
            sp.wait_ge(made, J.no[("x1", KD - 1)] + 1)
            for b in range(4):
                sp.dma_start(kcache[b], ck[:, b]).then_inc(kb_in, 16)
            sp.wait_ge(kv_stored, 32)
            for b in (6, 7):
                sp.dma_start(vc[b], cv[:, b]).then_inc(v_in[2], 16)
            sp.wait_ge(ss_done, 3)
            for b in (4, 5):
                sp.dma_start(vc[b], cv[:, b]).then_inc(v_in[0], 16)
            J.wait_taken(sp, "qs")
            sp.dma_start(q_rows, qsr[0:DEC, :]).then_inc(q_stored, 16)
            sp.wait_ge(q_stored, 16)
            sp.wait_ge(stored, 16 * 8)
            for b in range(DEC):
                if b >= 2:
                    sp.wait_ge(qb_used, b - 1)
                sp.dma_start(qb[:, b % 2, :], q_rows[b, :].partition_broadcast(P)).then_inc(qb_in[b % 2], 16)
                if b == 1:
                    for j in (4, 5):
                        sp.dma_start(kcache[j], ck[:, j]).then_inc(kc_in[j - 4], 16)
                if b in (2, 3):
                    sp.dma_start(kcache[b + 4], ck[:, b + 4]).then_inc(kc_in[b], 16)
                if b >= 4:
                    sp.dma_start(vc[b - 4], cv[:, b - 4]).then_inc(v_in[1], 16)
            sp.wait_ge(qb_used, DEC)
            sp.dma_start(view(regB, 0, KD, D), xa_wo.rearrange("o (k p) n -> p (o k) n", p=P)).then_inc(wo_in, 16)
            sp.wait_ge(made, J.no["oS"] + 1)
            sp.dma_start(rw, router_w.rearrange("o (k p) e -> p (o k) e", p=P)).then_inc(rw_in, 16)
            sp.dma_start(rbias, router_bias[0].partition_broadcast(P)).then_inc(rw_in, 16)
            sp.dma_start(sgw, sh_w_gate.rearrange("o (k p) f -> p (o k) f", p=P)).then_inc(sh_in, 16)
            sp.dma_start(suw, sh_w_up.rearrange("o (k p) f -> p (o k) f", p=P)).then_inc(sh_in, 16)
            sp.dma_start(sdw, sh_w_down.rearrange("o (k p) d -> p (o k) d", p=P)).then_inc(sh_in, 16)
            for t, (t0, n) in enumerate(TILES):
                J.wait_taken(sp, ("hR", t))
                sp.dma_start(h_rows[t0:t0 + n, :], rows[0:n, t, :]).then_inc(h_stored, 16)

            sp.wait_ge(row_table, 1)
            sp.wait_ge(made, J.no[("su", KF - 1)] + 1)
            sp.dma_start(gfin, norm_final.partition_broadcast(P)).then_inc(fin_g, 16)
            n_turns = turns(sp)
            eg = exp_w_gate.rearrange("o e (p k) f -> (o e) p (k f)", p=P)
            eu = exp_w_up.rearrange("o e (p k) f -> (o e) p (k f)", p=P)
            ed = exp_w_down.rearrange("o e (p k) d -> (o e) p k d", p=P)

            def load(r, e, b):
                sp.wait_ge(gu_made, b + 1)
                sp.dma_start(WG[r][:, 0:1, :], eg[bass.ds(e, 1)].rearrange("e p n -> p e n")).then_inc(wg_in[r], 16)
                sp.dma_start(WG[r][:, 1:2, :], eu[bass.ds(e, 1)].rearrange("e p n -> p e n")).then_inc(wg_in[r], 16)
                sp.wait_ge(down_made, b + 1)
                sp.dma_start(WD[r][:, :, :], ed[bass.ds(e, 1)].rearrange("e p k d -> p (e k) d")).then_inc(wd_in[r], 16)

            e0 = sp.value_load(ET[0:1, 0:1].bitcast(I32), min_val=0, max_val=NE - 1)
            load(0, e0, 0)
            sp.wait_ge(clear, 2)
            with sp.Fori(0, n_turns) as i:
                for j in range(RING):
                    e = sp.value_load(ET[0:1, bass.ds(i * RING + (j + 1), 1)].bitcast(I32), min_val=0, max_val=NE - 1)
                    load((j + 1) % RING, e, i * RING + (j + 1))
            sp.wait_ge(sums_landed, n_turns * (RING * 16) + 16 * (NTT + 1))
            for t, (t0, n) in enumerate(TILES):
                sp.dma_start(yf[0:n, t, :], acc_rows[t0:t0 + n, :]).then_inc(fin_in[t], 16)
            for t, (t0, n) in enumerate(TILES):
                sp.wait_ge(fin_y, t + 1)
                dst = y_prompt[0, t0:t0 + n, :] if t < TT else y_sample.rearrange("b o d -> b (o d)")
                sp.dma_start(dst, yf[0:n, t, :]).then_inc(stored, 16)
            sp.wait_ge(stored, 16 * 13)

        @block.gpsimd
        def _(pool):
            c = Count()

            def step(ins):
                pool.wait_ge(*c.add(ins, pool_step))

            step(pool.memset(small[:, :], 0.0))
            pool.memset(eps_c, EPS).then_inc(consts, 1)
            step(pool.memset(ident[:, :], 0.0))
            pool.affine_select(out=ident[:, :], in_=ident[:, :], compare_op=ALU.not_equal, fill=1.0, base=0,
                               pattern=[[-1, P]], channel_multiplier=1).then_inc(consts, 1)
            pool.memset(ones[:, :], 1.0).then_inc(consts, 1)
            pool.dma_start(rawP[0:DEC * PBUF, :], state_pool.rearrange("o b r c -> (o b r) c")).then_inc(states_in, 16)
            pool.dma_start(rawC[0:DEC * CBUF, :], state_conv.rearrange("o b r c -> (o b r) c")).then_inc(states_in, 16)
            pool.dma_start(rawH[0:DEC, :], state_h[0]).then_inc(states_in, 16)
            pool.iota(r15, pattern=[[1, 16]], base=1, channel_multiplier=0,
                      allow_small_or_imprecise_dtypes=True).then_inc(consts, 1)
            pool.memset(bdw, 0.0).then_inc(bd_zero, 1)

            for g, w in enumerate(WINDOWS):
                J.wait_taken(pool, ("z", g))
                if g == 0:
                    pool.wait_ge(made, J.no[("z", 3)] + 1)
                src, have, n = uP[:, g, 0:PBUF + SEQ], 1, 0
                while have < w:
                    last = 2 * have == w
                    lo = PBUF if last else 2 * have - 1
                    out = dT[:, g, 0:SEQ] if last else ptmp[n % 2][:, lo:PBUF + SEQ]
                    ins = pool.tensor_tensor(out, src[:, lo:PBUF + SEQ], src[:, lo - have:PBUF + SEQ - have], ALU.add)
                    if last:
                        ins.then_inc(pooled, 1)
                        pool.wait_ge(pooled, g + 1)
                    else:
                        step(ins)
                    src, have, n = ptmp[n % 2], 2 * have, n + 1
            pool.wait_ge(ss_done, 4)
            step(pool.memset(valid, 1.0))
            step(pool.memset(low, 1.0))
            pool.affine_select(out=valid[:, TT:TT + 1], in_=valid[:, TT:TT + 1], compare_op=ALU.is_gt, fill=0.0,
                               base=DEC, pattern=[[0, 1]], channel_multiplier=-1).then_inc(consts, 1)
            pool.affine_select(out=low, in_=low, compare_op=ALU.is_gt, fill=0.0, base=0, pattern=[[1, P]],
                               channel_multiplier=-1).then_inc(consts, 1)
            for out, pattern, base, up in ((iot8, [[1, NG]], 0, 0), (iotp, [[0, 1]], 0, 1), (j3, [[RING, 48]], 0, 0),
                                           (iots, [[1, SLOTS]], 0, 0), (whole[:, :, 0], [[P, NTT]], -FAR, 0),
                                           (whole[:, :, 1], [[0, NTT]], 0, 1)):
                pool.iota(out, pattern=pattern, base=base, channel_multiplier=up,
                          allow_small_or_imprecise_dtypes=True).then_inc(consts, 1)
            for j in range(RING):
                pool.memset(gath[j], 0.0).then_inc(consts, 1)

            pool.wait_ge(row_table, 1)
            pool.wait_ge(consts, 15)
            n_turns = turns(pool)
            limit = pool.to_reg(NT - 1)
            pool.wait_ge(h_stored, 16 * NTT)

            def gather(r, b):
                pool.wait_ge(turned, b + 1)
                pool.wait_ge(idx_ready, b + 1)
                pool.sem_inc(clear, 1)
                pool.indirect_dma_start(gath[r][0:SLOTS, :], None, h_rows,
                                        bass.IndirectOffsetOnAxis(ap=idx[0:SLOTS, r:r + 1].bitcast(U32), axis=0),
                                        bounds_check=limit, oob_is_err=False).then_inc(gath_in[r], 16)

            def scatter(r, b):
                pool.wait_ge(sidx_ready, b + 1)
                pool.wait_ge(down_a, b + 2)
                pool.wait_ge(down_d, b + 2)
                pool.wait_ge(sums_landed, b * 16 + 16 * NTT)
                pool.sem_inc(rows_left, 1)
                pool.sem_inc(clear, 1)
                pool.indirect_dma_start(acc_rows, bass.IndirectOffsetOnAxis(ap=sidx[0:SLOTS, r:r + 1].bitcast(U32), axis=0),
                                        yX[r][0:SLOTS, :], None, bounds_check=limit, oob_is_err=False,
                                        compute_op=ALU.add).then_inc(sums_landed, 16)

            for b in range(3):
                gather(b, b)
            for t, (t0, n) in enumerate(TILES):
                pool.wait_ge(acc_ready, t + 1)
                pool.dma_start(acc_rows[t0:t0 + n, :], rows[0:n, t, :]).then_inc(sums_landed, 16)
            pool.wait_ge(sums_landed, 16 * NTT)
            pool.sem_inc(rows_left, RING - 1)
            with pool.Fori(0, n_turns) as i:
                for j in range(RING):
                    b = i * RING + (j + 1)
                    gather(j, b + 2)
                    scatter(j, b - 1)
            scatter(0, n_turns * RING)
            pool.wait_ge(sums_landed, n_turns * (RING * 16) + 16 * (NTT + 1))

        @block.scalar
        def _(a):
            c = Count()

            def rooted(width):
                n = c.n.get(id(root), 0)
                a.wait_ge(ss_done, n)
                a.wait_ge(inverse, n)
                c.add(a.activation(ssq, pS[:, 0, 0:5], ACT.Sqrt, bias=eps_c, scale=1.0 / width), root)

            def squared(out, x):
                c.add(a.activation(out, x, ACT.Square), squares)

            a.wait_ge(consts, 4)
            for t, (t0, n) in enumerate(TILES):
                a.wait_ge(x_in[t], 16)
                if t:
                    a.wait_ge(act_step, t)
                c.add(a.activation(xsq[0:n, :], xraw[0:n, t, :], ACT.Square, accum_out=ssq[0:n, t:t + 1]), act_step)
            a.wait_ge(act_step, NTT)
            c.add(a.activation(ssq, ssq, ACT.Sqrt, bias=eps_c, scale=1.0 / D), root)

            def cut_norm(tmp, before, first=0, tiles=KD):
                for k in range(tiles):
                    a.wait_ge(h_made, before + k + 1)
                    a.copy(h_hi[:, first + k, :], tmp[:, k % 2, :]).then_inc(h_hi_made, 1)

            Z.cut_hi(a, 0)
            Z.cut_hi(a, 1)
            cut_norm(htmp1, 0)
            Z.cut_hi(a, 2)
            a.wait_ge(padded, 1)
            for i in range(KP):
                Z.cut_hi(a, 2 * i + 3)
                Z.cut_hi(a, 2 * i + 4)
                p = J.wait_made(a, ("z", 4 + i))
                J.take(a.copy(halves(uR[:, i, CBUF:CBUF + NT]), pair[p][:, :, 0:HALF]), ("z", 4 + i))
            for i in range(KP):
                Z.cut_hi(a, 2 * (KP + i) + 3)
                Z.cut_hi(a, 2 * (KP + i) + 4)
                p = J.wait_made(a, ("z", 8 + i))
                J.take(a.activation(halves(gT[:, i, :]), pair[p][:, :, 0:HALF], ACT.Gelu_apprx_tanh), ("z", 8 + i))
                if i == 1:
                    a.wait_ge(mem_in, 16)
                    for t in range(MT):
                        c.add(a.activation(msq[:, t, :], mraw[:, t, :], ACT.Square, accum_out=mss[:, t:t + 1]), act_step)
                    a.wait_ge(act_step, NTT + MT)
                    c.add(a.activation(mss, mss, ACT.Sqrt, bias=eps_c, scale=1.0 / D), mem_ss)
                    a.wait_ge(mem_inv, 1)
                    for t in range(MT):
                        c.add(a.activation(mraw[:, t, :], mraw[:, t, :], ACT.Copy, scale=mrs[:, t:t + 1]), mem_scaled)
            for i in range(KP):
                for what, out, bias in (("r", rT, "gate_a_b"), ("i", iT, "gate_x_b")):
                    p = J.wait_made(a, (what, i))
                    J.take(a.activation(halves(out[:, i, :]), pair[p][:, :, 0:HALF], ACT.Sigmoid,
                                        bias=par[:, COL[bias] + i:COL[bias] + i + 1]), (what, i))
            a.wait_ge(sp_in, 1)
            c.add(a.activation(spt[:, 12:16], spt[:, 4:8], ACT.Exp), sp_exp)
            for q in range(2):
                p = J.wait_made(a, ("mT", q))
                for j in range(4):
                    k = 4 * q + j
                    cl = COL["norm_mem"] + k
                    ins = a.activation(mT[:, k, :], pair[p][:, j // 2, (j % 2) * NMEM:(j % 2 + 1) * NMEM], ACT.Copy,
                                       scale=par[:, cl:cl + 1])
                J.take(ins, ("mT", q))
            for g in range(KP):
                Z.cut_hi(a, 2 * (2 * KP + g) + 3)
                Z.cut_hi(a, 2 * (2 * KP + g) + 4)
                p = J.wait_made(a, ("z", g))
                J.take(a.copy(halves(uP[:, g, PBUF:PBUF + NT]), pair[p][:, :, 0:HALF]), ("z", g))
            p = J.wait_made(a, "st")
            a.copy(stO[0:CBUF + DEC, 0, :], pair[p][0:CBUF + DEC, 0, :])
            J.take(a.copy(stO[0:PBUF + DEC, 1, :], pair[p][0:PBUF + DEC, 1, :]), "st")
            a.wait_ge(conv_done, KP)
            a.wait_ge(sp_ready, 2)
            J.wait_taken(a, ("i", KP - 1))
            for i in range(KP):
                c.add(a.activation(aT[:, i, :], rT[:, i, :], ACT.Exp, scale=nsp[:, i:i + 1]), lru_a)
            for i in range(KP):
                c.add(a.activation(rT[:, i, :], rT[:, i, :], ACT.Tanh, scale=psp[:, i:i + 1]), lru_s)
            for what, out in (("K", Kt), ("V", Vt)):
                for t in range(MT):
                    if what == "K" and t == 1:
                        for i in range(KP):
                            a.wait_ge(lru_m2, i + 1)
                            c.add(a.activation(rT[:, i, :], rT[:, i, :], ACT.Sqrt), lru_m)
                    p = J.wait_made(a, (what, t))
                    J.take(a.copy(out[:, t, :].rearrange("p (h n) -> p h n", h=2), pair[p][:, :, :]), (what, t))
            for q in range(2):
                p = J.wait_made(a, ("KT", q))
                J.take(a.copy(KT[:, 4 * q:4 * q + 4, :].rearrange("p (h k) n -> p h (k n)", h=2), pair[p][:, :, :]), ("KT", q))
            for g in range(KP):
                p = J.wait_made(a, ("yp", g))
                cl = COL["pool_scale"] + g
                J.take(a.activation(halves(dT[:, g, :]), pair[p][:, :, 0:HALF], ACT.Copy, scale=par[:, cl:cl + 1]), ("yp", g))
            for g in range(KP):
                J.wait_taken(a, ("yp", g))
                squared(sqP[:, g, :], dT[:, g, :])
            rooted(DP)
            for i in range(KP):
                a.wait_ge(y_rnn, i + 1)
                squared(rT[:, i, :], gT[:, i, :])
            a.wait_ge(kv_stored, 32)
            O.cut_hi(a, 0)
            O.cut_hi(a, 1)
            cut_norm(ytmp, KD, 0, KP)
            rooted(DP)
            O.cut_hi(a, 2)
            cut_norm(ytmp, KD + KP, KP, KP)
            p = J.wait_made(a, "hl")
            J.take(a.copy(hlO[0:1 + DEC, :], pair[p][0:1 + DEC, 0, :]), "hl")
            for m in range(KD):
                O.cut_hi(a, 2 * m + 3)
                O.cut_hi(a, 2 * m + 4)
                J.wait_taken(a, ("x1", m))
                squared(sqT[:, m, :], xT[:, m, :])
            rooted(D)
            a.wait_ge(stored, 16 * 8)
            for u in range(2):
                Q.cut_hi(a, u)
            cut_norm(htmp2, 2 * KD)
            Q.cut_hi(a, 2)
            for m in range(KD):
                Q.cut_hi(a, 2 * m + 3)
                Q.cut_hi(a, 2 * m + 4)
                p = J.wait_made(a, ("q", m))
                J.take(a.copy(halves(qT[:, m, :]), pair[p][:, :, 0:HALF]), ("q", m))
            p = J.wait_made(a, "qs")
            J.take(a.copy(qsr[0:DEC, :].rearrange("p (h n) -> p h n", h=2), pair[p][0:DEC, :, :]), "qs")
            nb = DEC * HEADS

            def out(h, cc):
                q = J.wait_made(a, ("o", h, cc))
                J.take(a.copy(oT[:, 2 * h + cc, 0:SEQ], bank[q]), ("o", h, cc))

            for n in range(len(STEPS) + BEHIND):
                if n < len(STEPS):
                    q = J.wait_made(a, ("s", *STEPS[n]))
                    r = n % 4
                    a.wait_ge(att_max, n + 1)
                    if n >= 4:
                        a.wait_ge(made, J.no[("pT", *STEPS[n - 4])] + 1)
                    J.take(a.activation(pr[:, r, :], bank[q][:, 0:NMEM], ACT.Exp, bias=nmax[:, r:r + 1],
                                        scale=SCALE, accum_out=asum[:, r:r + 1]), ("s", *STEPS[n]))
                if 1 <= n <= len(STEPS):
                    r = (n - 1) % 4
                    a.wait_ge(att_inv, n)
                    c.add(a.activation(pr[:, r, :], pr[:, r, :], ACT.Copy, scale=rsum[:, r:r + 1]), att_norm)
                if n >= BEHIND:
                    h, t = STEPS[n - BEHIND]
                    if (h, t) == (1, 0):
                        a.wait_ge(q_stored, 16)
                    q = J.wait_made(a, ("pT", h, t))
                    J.take(a.copy(PT[:, h % 2, :, t * P:(t + 1) * P],
                                  bank[q][:, 0:NMEM].rearrange("p (m n) -> p m n", m=MT)), ("pT", h, t))
                    if h and t < 2:
                        out(h - 1, t)
            out(HEADS - 1, 0)
            q = J.wait_made(a, "sS")
            a.wait_ge(s_max, 1)
            J.take(a.activation(pSm[0:nb, :], bank[q][0:nb, 0:NMEM], ACT.Exp, bias=snm[0:nb, :], scale=SCALE,
                                accum_out=sss[0:nb, :]), "sS")
            out(HEADS - 1, 1)
            q = J.wait_made(a, "pS")
            J.take(a.copy(pad8[:, :, 0:DEC * DEC:DEC + 1], bank[q][:, 0:MT * nb].rearrange("p (g b) -> p g b", b=DEC)), "pS")
            p = J.wait_made(a, "oS")
            J.take(a.copy(oSr[0:DEC, :].rearrange("p (h n) -> p h n", h=2), pair[p][0:DEC, :, :]), "oS")
            q = J.wait_made(a, "oST")
            J.take(a.copy(oT[:, :, SEQ:NT], bank[q][:, 0:KD * DEC].rearrange("p (k b) -> p k b", k=KD)), "oST")
            for m in range(KD):
                J.wait_taken(a, ("x2", m))
                squared(sqT[:, m, :], xT[:, m, :])
            rooted(D)
            p = J.wait_made(a, "rt")
            a.wait_ge(sco_ones, 1)
            a.activation(sco[:, 0:TT, :], pair[p][:, 0, 0:TT * NE].rearrange("p (t e) -> p t e", t=TT), ACT.Sigmoid)
            J.take(a.activation(sco[0:DEC, TT, :], pair[p][0:DEC, 0, TT * NE:NTT * NE], ACT.Sigmoid), "rt")
            for t, (t0, n) in enumerate(TILES):
                p = J.wait_made(a, ("hR", t))
                J.take(a.copy(rows[0:n, t, :].rearrange("p (h n) -> p h n", h=2), pair[p][0:n, :, :]), ("hR", t))
            for m in range(KF):
                p = J.wait_made(a, ("sg", m))
                J.take(a.activation(halves(sA[:, m, :]), pair[p][:, :, 0:HALF], ACT.Silu), ("sg", m))
            a.wait_ge(h_stored, 16 * NTT)
            for t, (t0, n) in enumerate(TILES):
                p = J.wait_made(a, ("xR", t))
                J.take(a.copy(rows[0:n, t, :].rearrange("p (h n) -> p h n", h=2), pair[p][0:n, :, :]), ("xR", t))

            a.wait_ge(row_table, 1)
            n_turns = turns(a)
            a.sem_inc(down_a, 1)

            def silu(b, first=False):
                a.wait_ge(gu_made, b + (1 + RING))
                if not first:
                    a.wait_ge(act_b, b)
                a.activation(sil[0:SLOTS, :], pair[0][0:SLOTS, 0, 0:FE], ACT.Silu).then_inc(silu_b, 1)

            def turn(b):
                a.wait_ge(turned, b + (1 + RING))
                a.copy(hX[:, 0:4, :].rearrange("p k n -> p (k n)"), pair[1][:, 0, 0:4 * SLOTS]).then_inc(turned_a, 1)

            def at(b):
                a.wait_ge(at_made, b + 1)
                a.copy(aX.rearrange("p k n -> p (k n)"), pair[0][:, 1, 0:KF * SLOTS]).then_inc(at_taken, 1)

            def down(r, b):
                a.wait_ge(down_made, b + (1 + RING))
                a.wait_ge(sidx_ready, b + 1)
                a.activation(yX[r][0:SLOTS, 0:512], pair[2][0:SLOTS, 0, :], ACT.Copy, scale=swl[0:SLOTS, r:r + 1]).then_inc(down_a, 1)

            turn(0)
            silu(0, first=True)
            turn(1)
            with a.Fori(0, n_turns) as i:
                for j in range(RING):
                    b = i * RING + (j + 1)
                    at(b - 1)
                    silu(b)
                    turn(b + 1)
                    down(j, b - 1)
            at(n_turns * RING)
            down(0, n_turns * RING)

            for t, (t0, n) in enumerate(TILES):
                a.wait_ge(fin_in[t], 16)
                a.activation(junk[0:n, :], yf[0:n, t, :], ACT.Square, accum_out=fin[0:n, t:t + 1]).then_inc(fin_ss, 1)
                a.wait_ge(fin_ss, t + 1)
                a.activation(fin[0:n, 5 + t:6 + t], fin[0:n, t:t + 1], ACT.Sqrt, bias=eps_c[0:n, :], scale=1.0 / D).then_inc(fin_root, 1)

        @block.vector
        def _(v):
            c = Count()

            def mark(ins):
                return c.add(ins, dve_step)

            def step(ins):
                v.wait_ge(*mark(ins))

            def inverted():
                n = c.n.get(id(inverse), 0)
                v.wait_ge(root, n + 1)
                c.add(v.reciprocal(rs, ssq), inverse)

            def apply(nb, src, dst, gain, tiles):
                p = J.wait_made(v, nb)
                for k in range(tiles):
                    ins = v.scalar_tensor_tensor(halves(dst[:, k, :]), halves(src[:, k, :]),
                                                 par[:, COL[gain] + k:COL[gain] + k + 1],
                                                 pair[p][:, :, 0:HALF], ALU.mult, ALU.mult)
                    if k < tiles - 1:
                        c.add(ins, normed)
                    else:
                        J.take(ins, nb)

            def apply_split(nb, src, tmp, lo, gain, before, first=0, tiles=KD):
                p = J.wait_made(v, nb)

                def leave(k):
                    v.wait_ge(h_hi_made, before + k + 1)
                    v.tensor_tensor(lo[:, first + k, :], tmp[:, k % 2, :], h_hi[:, first + k, :].bitcast(F32),
                                    ALU.subtract).then_inc(h_lo_made, 1)

                for k in range(tiles):
                    if k >= 2:
                        v.wait_ge(h_lo_made, before + k - 1)
                    ins = v.scalar_tensor_tensor(halves(tmp[:, k % 2, :]), halves(src[:, k, :]),
                                                 par[:, COL[gain] + k:COL[gain] + k + 1],
                                                 pair[p][:, :, 0:HALF], ALU.mult, ALU.mult).then_inc(h_made, 1)
                    if k:
                        leave(k - 1)
                leave(tiles - 1)
                v.wait_ge(h_made, before + tiles)
                J.take(v.tensor_copy(small[:, 100:101], small[:, 101:102]), nb)

            for t, (t0, n) in enumerate(TILES):
                p = J.wait_made(v, ("xT", t))
                J.take(v.tensor_copy(xT[:, :, t0:t0 + n].rearrange("p (h k) n -> p h k n", h=2),
                                     pair[p][:, :, 0:4 * n].rearrange("p h (k n) -> p h k n", k=4)), ("xT", t))
            p = J.wait_made(v, "par")
            J.take(v.tensor_copy(par[:, :], pair[p][:, 0, 0:NROWS]), "par")
            v.memset(uP[:, :, 0:PBUF], 0.0)
            c.add(v.memset(uR[:, :, 0:CBUF], 0.0), padded)
            inverted()
            J.wait_taken(v, "par")
            Z.cut_lo(v, 0)
            Z.cut_lo(v, 1)
            apply_split("nb1", xT, htmp1, h1_lo, "norm_mix", 0)
            Z.cut_lo(v, 2)
            p = J.wait_made(v, "sta")
            v.tensor_copy(stP.rearrange("p k b r -> p (k b r)"), pair[p][:, 0, 0:480])
            J.take(v.tensor_copy(view(regL, 13032, 128), pair[p][:, 1, 0:128]), "sta")
            def softplus():
                lam = par[:, COL["lru_lambda"]:COL["lru_lambda"] + 4]
                v.wait_ge(consts, 4)
                sp4 = lambda j: spt[:, 4 * j:4 * j + 4]
                step(v.tensor_scalar(sp4(0), lam, -1.0, None, ALU.mult))
                v.tensor_tensor(sp4(1), sp4(0), lam, ALU.min)
                c.add(v.tensor_scalar(sp4(2), sp4(0), 0.0, None, ALU.max), sp_in)
                v.wait_ge(sp_exp, 1)
                step(v.tensor_scalar(sp4(4), sp4(3), 2.0, None, ALU.add))
                step(v.reciprocal(sp4(5), sp4(4)))
                step(v.tensor_tensor(sp4(6), sp4(3), sp4(5), ALU.mult))
                step(v.tensor_tensor(sp4(7), sp4(6), sp4(6), ALU.mult))
                step(v.tensor_scalar(sp4(8), sp4(7), 1.0 / 17, 1.0 / 15, ALU.mult, ALU.add))
                for k in (13, 11, 9, 7, 5, 3, 1):
                    step(v.tensor_tensor(sp4(8), sp4(8), sp4(7), ALU.mult))
                    step(v.tensor_scalar(sp4(8), sp4(8), 1.0 / k, None, ALU.add))
                step(v.tensor_tensor(sp4(8), sp4(8), sp4(6), ALU.mult))
                step(v.scalar_tensor_tensor(sp4(8), sp4(8), 2.0, sp4(2), ALU.mult, ALU.add))
                c.add(v.tensor_scalar(nsp, sp4(8), -LRU_C, None, ALU.mult), sp_ready)
                c.add(v.tensor_scalar(psp, sp4(8), LRU_C, None, ALU.mult), sp_ready)
                step(v.reciprocal(r15, r15))

            wcol = lambda k, i: par[:, COL["conv_w"] + 4 * k + i:COL["conv_w"] + 4 * k + i + 1]
            bcol = lambda i: par[:, COL["conv_b"] + i:COL["conv_b"] + i + 1]
            def conv(i):
                J.wait_taken(v, ("z", 4 + i))
                u = uR[:, i, :]
                v.tensor_scalar(cT[:, i, SEQ:NT], u[:, CBUF + SEQ:CBUF + NT], wcol(3, i), bcol(i), ALU.mult, ALU.add)
                step(v.tensor_scalar(cT[:, i, 0:SEQ], u[:, 0:SEQ], wcol(0, i), bcol(i), ALU.mult, ALU.add))
                for k in range(1, 4):
                    v.scalar_tensor_tensor(cT[:, i, SEQ:NT], stC[:, i, :, k - 1], wcol(k - 1, i), cT[:, i, SEQ:NT],
                                           ALU.mult, ALU.add)
                    ins = v.scalar_tensor_tensor(cT[:, i, 0:SEQ], u[:, k:k + SEQ], wcol(k, i), cT[:, i, 0:SEQ],
                                                 ALU.mult, ALU.add)
                    if k < 3:
                        step(ins)
                    else:
                        c.add(ins, conv_done)

            for n in range(len(z_order)):
                Z.cut_lo(v, 2 * n + 3)
                Z.cut_lo(v, 2 * n + 4)
                if 1 <= n <= KP:
                    conv(n - 1)
                if n == KP + 1:
                    v.wait_ge(mem_ss, 1)
                    c.add(v.reciprocal(mrs, mss), mem_inv)
                if n == 2 * KP - 1:
                    softplus()
            for g, w in enumerate(WINDOWS):
                v.wait_ge(pooled, g + 1)
                step(v.tensor_reduce(dT[:, g, SEQ:NT], stP[:, g, :, PBUF - w + 1:PBUF], AX.X, ALU.add))
                v.tensor_tensor(dT[:, g, SEQ:NT], dT[:, g, SEQ:NT], uP[:, g, PBUF + SEQ:PBUF + NT], ALU.add)
                step(v.scalar_tensor_tensor(dT[:, g, 0:w - 1], dT[:, g, 0:w - 1], float(w), r15[:, 0:w - 1],
                                            ALU.mult, ALU.mult))
                c.add(v.scalar_tensor_tensor(dT[:, g, :], dT[:, g, :], 1.0 / w, uP[:, g, PBUF:PBUF + NT],
                                             ALU.mult, ALU.subtract), d_ready)
            for i in range(KP):
                v.wait_ge(lru_a, i + 1)
                step(v.tensor_tensor(a2, aT[:, i, :], aT[:, i, :], ALU.mult))
                v.wait_ge(lru_s, i + 1)
                v.wait_ge(*c.add(v.scalar_tensor_tensor(rT[:, i, :], a2, 1.0, rT[:, i, :], ALU.add, ALU.mult), lru_m2))
            v.wait_ge(lru_m, KP)
            step(v.memset(rT[:, :, 0:1], 1.0))
            t0 = [mark(v.tensor_tensor(iT[:, i, :], iT[:, i, :], rT[:, i, :], ALU.mult)) for i in range(KP)]
            t1 = []
            for i in range(KP):
                v.wait_ge(*t0[i])
                t1.append(mark(v.tensor_tensor(iT[:, i, :], iT[:, i, :], cT[:, i, :], ALU.mult)))
            v.wait_ge(*t1[-1])
            t2 = mark(v.tensor_tensor(stH, aT[:, :, SEQ:NT], stH, ALU.mult))
            t3 = [mark(v.tensor_tensor_scan(cT[:, i, 0:SEQ], aT[:, i, 0:SEQ], iT[:, i, 0:SEQ], 0.0, ALU.mult, ALU.add))
                  for i in range(KP)]
            v.wait_ge(*t2)
            step(v.tensor_tensor(cT[:, :, SEQ:NT], stH, iT[:, :, SEQ:NT], ALU.add))
            for i in range(KP):
                c.add(v.tensor_tensor(gT[:, i, :], cT[:, i, :], gT[:, i, :], ALU.mult), y_rnn)
            inverted()
            O.cut_lo(v, 0)
            O.cut_lo(v, 1)
            apply_split("nbp", dT, ytmp, y_lo, "norm_pool_out", KD, 0, KP)
            inverted()
            O.cut_lo(v, 2)
            v.wait_ge(h_lo_made, KD + KP)
            apply_split("nbr", gT, ytmp, y_lo, "norm_rnn_out", KD + KP, KP, KP)

            def residual(what, before):
                for m in range(KD):
                    if what == "x1":
                        O.cut_lo(v, 2 * m + 3)
                        O.cut_lo(v, 2 * m + 4)
                    if 2 <= m < KD:
                        v.wait_ge(squares, before + m)
                        v.wait_ge(sq_added, c.n.get(id(sq_added), 0)) if m > 2 else None
                        c.add(v.tensor_tensor(sqT[:, 0, :], sqT[:, 0, :], sqT[:, m - 1, :], ALU.add), sq_added)
                    p = J.wait_made(v, (what, m))
                    J.take(v.tensor_tensor(halves(xT[:, m, :]), halves(xT[:, m, :]), pair[p][:, :, 0:HALF], ALU.add), (what, m))

            residual("x1", 2 * KP)
            inverted()
            Q.cut_lo(v, 0)
            Q.cut_lo(v, 1)
            apply_split("nb2", xT, htmp2, h2_lo, "norm_xattn", 2 * KD)
            Q.cut_lo(v, 2)
            for u in range(3, Q.units):
                Q.cut_lo(v, u)

            units = [(b, mt) for b in range(DEC) for mt in range(MT)]

            def scores(b, mt):
                if mt == 0:
                    v.wait_ge(qb_in[b % 2], 16 * (b // 2 + 1))
                    if b < 4:
                        v.wait_ge(kb_in, 64)
                    else:
                        v.wait_ge(kc_in[b - 4], 16)
                for h in range(HEADS):
                    kk = kcache[b][:, mt, h * HD:(h + 1) * HD]
                    ins = v.tensor_tensor_reduce(kk, kk, qb[:, b % 2, h * HD:(h + 1) * HD], 1.0, 0.0, ALU.mult, ALU.add,
                                                 sS[:, mt, h * DEC + b:h * DEC + b + 1])
                if mt == MT - 1:
                    ins.then_inc(qb_used, 1)

            v.wait_ge(stored, 16 * 8)
            v.memset(pad8, 0.0)
            for n in range(len(STEPS) + 1):
                if n < len(STEPS):
                    q = J.wait_made(v, ("s", *STEPS[n]))
                    r = n % 4
                    if n >= 4:
                        v.wait_ge(att_norm, n - 3)
                    step(v.tensor_reduce(amax[:, r:r + 1], bank[q][:, 0:NMEM], AX.X, ALU.max))
                    c.add(v.tensor_scalar(nmax[:, r:r + 1], amax[:, r:r + 1], -SCALE, None, ALU.mult), att_max)
                if n >= 1:
                    r = (n - 1) % 4
                    J.wait_taken(v, ("s", *STEPS[n - 1]))
                    c.add(v.reciprocal(rsum[:, r:r + 1], asum[:, r:r + 1]), att_inv)
                if n >= 2:
                    for u in range(n - 2, n - 1 if n < len(STEPS) else len(units)):
                        scores(*units[u])
            nb = DEC * HEADS
            q = J.wait_made(v, "sS")
            step(v.tensor_reduce(smx[0:nb, :], bank[q][0:nb, 0:NMEM], AX.X, ALU.max))
            c.add(v.tensor_scalar(snm[0:nb, :], smx[0:nb, :], -SCALE, None, ALU.mult), s_max)
            J.wait_taken(v, "sS")
            step(v.reciprocal(srs[0:nb, :], sss[0:nb, :]))
            c.add(v.tensor_scalar(pSm[0:nb, :], pSm[0:nb, :], srs[0:nb, :], None, ALU.mult), s_norm)
            v.wait_ge(made, J.no["oS"] + 1)
            c.add(v.memset(sco, 1.0), sco_ones)
            residual("x2", 2 * KP + KD)
            inverted()
            apply("nb3", xT, hT, "norm_ffn", KD)

            def onehot_(b):
                e = v.value_load(ET[0:1, bass.ds(b, 1)].bitcast(I32), min_val=0, max_val=NE - 1)
                v.tensor_tensor(oneh, iots.unsqueeze(1).to_broadcast((P, NTT, SLOTS)),
                                slot[:, :, bass.ds(e, 1)].to_broadcast((P, NTT, SLOTS)), ALU.is_equal)
                v.tensor_copy(rhsw[:, :, 3:6], wparts[:, :, :, bass.ds(e, 1)].rearrange("p c t e -> p t (c e)")).then_inc(onehot, 1)
                v.wait_ge(onehot, b + 1)
                v.tensor_scalar(iots, iots, float(SLOTS), None, ALU.add).then_inc(counted, 1)
                v.wait_ge(counted, b + 1)

            def slots(r, b):
                v.wait_ge(slots_made, b + 1)
                v.tensor_reduce(sums[0:SLOTS, r, :], pS[0:SLOTS, 0, 0:6].rearrange("p (s c) -> p s c", s=2), AX.X,
                                ALU.add).then_inc(summed, 1)
                v.wait_ge(summed, b + 1)
                v.tensor_scalar(idx[0:SLOTS, r:r + 1].bitcast(U32), sums[0:SLOTS, r, 0:1], float(FAR), None, ALU.add).then_inc(idx_ready, 1)

            J.wait_taken(v, "rt")
            v.wait_ge(rw_in, 32)
            v.wait_ge(consts, 15)
            over = lambda x, n: x.unsqueeze(1).to_broadcast((P, NTT, n))
            step(v.tensor_tensor(bia, sco, over(rbias, NE), ALU.add))
            for t in range(NTT):
                for g in range(NG):
                    ins = v.max(m8[:, t, g * 8:(g + 1) * 8], bia[:, t, g * EG:(g + 1) * EG])
            step(ins)
            m8v = m8.rearrange("p t (g j) -> p t g j", j=8)
            step(v.tensor_tensor(gs, m8v[:, :, :, 0], m8v[:, :, :, 1], ALU.add))
            for t in range(NTT):
                ins = v.max(g8[:, t, :], gs[:, t, :])
            step(ins)
            for t in range(NTT):
                ins = v.max_index(gi[:, t, :].bitcast(U32), g8[:, t, :], gs[:, t, :])
            step(ins)
            step(v.tensor_copy(gif, gi.bitcast(U32)))
            for j in range(TOPG):
                out = gmk if j == 0 else geq
                step(v.tensor_tensor(out, over(iot8, NG), gif[:, :, j:j + 1].to_broadcast((P, NTT, NG)), ALU.is_equal))
                if j:
                    step(v.tensor_tensor(gmk, gmk, geq, ALU.add))
            step(v.tensor_scalar(pen, gmk, -1.0, 1e30, ALU.add, ALU.mult))
            gm4 = lambda x: x.unsqueeze(3).to_broadcast((P, NTT, NG, EG))
            b4 = bia.rearrange("p t (g j) -> p t g j", j=EG)
            for t in range(NTT):
                ins = v.tensor_tensor(b4[:, t], b4[:, t], gmk[:, t, :].unsqueeze(2).to_broadcast((P, NG, EG)), ALU.mult)
            step(ins)
            for t in range(NTT):
                ins = v.tensor_tensor(b4[:, t], b4[:, t], pen[:, t, :].unsqueeze(2).to_broadcast((P, NG, EG)), ALU.add)
            step(ins)
            for t in range(NTT):
                ins = v.max(top[:, t, :], bia[:, t, :])
            step(ins)
            for t in range(NTT):
                ins = v.match_replace(mrep[:, t, :], top[:, t, :], bia[:, t, :], -3e38)
            step(ins)
            step(v.tensor_scalar(msk, mrep, -3e38, None, ALU.is_equal))
            step(v.tensor_tensor(gwt, msk, sco, ALU.mult))
            step(v.tensor_reduce(wsu, gwt, AX.X, ALU.add))
            step(v.reciprocal(wsu, wsu))
            step(v.tensor_scalar(wsu, wsu, ROUTED, None, ALU.mult))
            t0 = mark(v.tensor_tensor(gwt, gwt, wsu.unsqueeze(2).to_broadcast((P, NTT, NE)), ALU.mult))
            c.add(v.tensor_tensor(msk, msk, valid.unsqueeze(2).to_broadcast((P, NTT, NE)), ALU.mult), masked)
            for m in range(KF):
                p = J.wait_made(v, ("su", m))
                J.wait_taken(v, ("sg", m))
                J.take(v.tensor_tensor(halves(sA[:, m, :]), halves(sA[:, m, :]), pair[p][:, :, 0:HALF], ALU.mult), ("su", m))
            v.wait_ge(*t0)
            v.memset(rhsw[:, :, 2:3], 0.0)
            v.tensor_copy(rhsw[:, :, 0:2], whole)
            for j in range(3):
                step(v.tensor_copy(wparts[:, j], part if j else gwt))
                if j < 2:
                    step(v.tensor_tensor(part, part if j else gwt, wparts[:, j], ALU.subtract))
            p = J.wait_made(v, "pos")
            cnt = pair[p][:, 0, NTT * NE:(NTT + 1) * NE]
            step(v.tensor_scalar(nblk, cnt, 0.0, None, ALU.is_gt))
            for k in range(1, -(-NT // SLOTS)):
                step(v.scalar_tensor_tensor(nblk, cnt, float(SLOTS * k), nblk, ALU.is_gt, ALU.add))
            step(v.tensor_tensor_scan(bend, ones[:, 0:NE], nblk, 0.0, ALU.mult, ALU.add))
            step(v.tensor_tensor(bbase, bend, nblk, ALU.subtract))
            step(v.tensor_scalar(bbase, bbase, float(SLOTS), 1.0, ALU.mult, ALU.add))
            J.take(v.tensor_tensor(slot, pair[p][:, 0, 0:NTT * NE].rearrange("p (t e) -> p t e", t=NTT), over(bbase, NE), ALU.add), "pos")
            J.wait_taken(v, "pos")
            step(v.tensor_tensor(slot, slot, msk, ALU.mult))
            step(v.tensor_scalar(slot, slot, -1.0, None, ALU.add))
            step(v.tensor_scalar(cmp, bend, iotp, 0.0, ALU.is_le, ALU.add, accum_out=ebc[:, 0:1]))
            c.add(v.tensor_scalar(ebc[:, 0:1], ebc[:, 0:1], float(NE - 1), None, ALU.min), tab_ready)
            step(v.tensor_scalar(ebc[:, 1:2], bend[:, NE - 1:NE], -1.0, None, ALU.add))
            step(v.tensor_scalar(cmp[:, 0:48], j3, ebc[:, 1:2], 0.0, ALU.is_lt, ALU.add, accum_out=cmp[:, 48:49]))
            step(v.tensor_copy(NI[:, 0:1].bitcast(I32), cmp[:, 48:49]))
            p = J.wait_made(v, "tab")
            J.take(v.tensor_copy(ET[0:1, :].bitcast(I32), pair[p][0:1, 0, 0:P]), "tab")
            J.wait_taken(v, "tab")
            c.add(v.tensor_copy(cmp[:, 49:50], cmp[:, 48:49]), row_table)
            v.wait_ge(row_table, 1)
            n_turns = turns(v)
            onehot_(0)
            for t, (t0_, n) in enumerate(TILES):
                p = J.wait_made(v, ("sd", t))
                J.wait_taken(v, ("xR", t))
                row = rows[0:n, t, :].rearrange("p (h n) -> p h n", h=2)
                J.take(v.tensor_tensor(row, row, pair[p][0:n, :, :], ALU.add), ("sd", t))
                J.wait_taken(v, ("sd", t))
                c.add(v.tensor_copy(cmp[:, 50:51], cmp[:, 48:49]), acc_ready)
                if t < 3:
                    slots(t, t)
                    onehot_(t + 1)

            v.sem_inc(down_d, 1)

            def keep(r, b):
                v.wait_ge(idx_ready, b + 1)
                v.wait_ge(rows_left, b + 1)
                v.tensor_copy(swl[0:SLOTS, r:r + 1], sums[0:SLOTS, r, 1:2])
                v.tensor_copy(sidx[0:SLOTS, r:r + 1].bitcast(U32), idx[0:SLOTS, r:r + 1].bitcast(U32)).then_inc(sidx_ready, 1)

            def turn(b):
                v.wait_ge(turned, b + (1 + RING))
                v.tensor_copy(hX[:, 4:8, :].rearrange("p k n -> p (k n)"), pair[1][:, 1, 0:4 * SLOTS]).then_inc(turned_d, 1)

            def gate(b, first=False):
                v.wait_ge(silu_b, b + 1)
                if not first:
                    v.wait_ge(at_made, b)
                v.tensor_tensor(act[0:SLOTS, :], sil[0:SLOTS, :], pair[0][0:SLOTS, 0, FE:2 * FE], ALU.mult).then_inc(act_b, 1)

            def down(r, b):
                v.wait_ge(down_made, b + (1 + RING))
                v.wait_ge(sidx_ready, b + 1)
                v.tensor_scalar(yX[r][0:SLOTS, 512:D], pair[2][0:SLOTS, 1, :], swl[0:SLOTS, r:r + 1], None, ALU.mult).then_inc(down_d, 1)

            turn(0)
            gate(0, first=True)
            turn(1)
            with v.Fori(0, n_turns) as i:
                for j in range(RING):
                    b = i * RING + (j + 1)
                    keep(j, b - 1)
                    v.wait_ge(sidx_ready, b)
                    slots(j, b + 2)
                    onehot_(b + 3)
                    gate(b)
                    turn(b + 1)
                    down(j, b - 1)
            keep(0, n_turns * RING)
            down(0, n_turns * RING)

            v.wait_ge(fin_g, 16)
            for t, (t0_, n) in enumerate(TILES):
                v.wait_ge(fin_root, t + 1)
                v.reciprocal(fin[0:n, 10 + t:11 + t], fin[0:n, 5 + t:6 + t]).then_inc(fin_inv, 1)
                v.wait_ge(fin_inv, t + 1)
                v.scalar_tensor_tensor(yf[0:n, t, :], yf[0:n, t, :], fin[0:n, 10 + t:11 + t], gfin[0:n, :],
                                       ALU.mult, ALU.mult).then_inc(fin_y, 1)

        @block.tensor
        def _(pe):
            seen = {"squares": 0, "norms": 1}

            def project(name, weights, acts, ks, ready=None):
                p = J.begin(pe, name)
                for k in ks:
                    if ready:
                        ready(k)
                    for h in range(2):
                        ins = pe.matmul(pair[p][:, h, 0:HALF], weights(k), acts(k)[:, h * HALF:(h + 1) * HALF],
                                        start=k == ks[0], stop=k == ks[-1])
                J.made_by(ins)

            def sum_squares(k, sq, first, last, ready=None):
                if not ready:
                    seen["squares"] += 1
                if first:
                    pe.wait_ge(root, seen["norms"])
                    seen["norms"] += 1
                    pe.matmul(pS[:, 0, 0:NTT], ones[:, :], zero5, start=True, stop=False, skip_group_check=True)
                pe.wait_ge(*(ready or (squares, seen["squares"])))
                for t, (t0, n) in enumerate(TILES):
                    ins = pe.matmul(pS[0:n, 0, t:t + 1], sq[:, k, t0:t0 + n], ones[:, 0:1], start=False,
                                    stop=last and t == NTT - 1, skip_group_check=True)
                if last:
                    ins.then_inc(ss_done, 1)

            def spread(name):
                p = J.begin(pe, name)
                pe.wait_ge(inverse, seen["norms"])
                for lo, hi, t in ((0, 128, 0), (128, 256, 1), (256, 260, 2), (260, 384, 2), (384, 512, 3), (512, 520, 4)):
                    h, t0 = lo // HALF, t * P
                    ins = pe.matmul(pair[p][:, h, lo - h * HALF:hi - h * HALF], rs[:, t:t + 1].to_broadcast((P, P)),
                                    ident[:, lo - t0:hi - t0], start=True, stop=True)
                J.made_by(ins)

            def normed_tiles(base, nb, tiles):
                def ready(k):
                    if k < tiles - 1:
                        pe.wait_ge(normed, base + k + 1)
                    else:
                        J.wait_taken(pe, nb)
                return ready

            pe.sem_inc(gu_made, RING)
            pe.sem_inc(down_made, RING)
            pe.sem_inc(turned, RING)
            pe.wait_ge(consts, 4)
            for t, (t0, n) in enumerate(TILES):
                p = J.begin(pe, ("xT", t))
                pe.wait_ge(x_in[t], 16)
                for k in range(KD):
                    ins = pe.transpose(pair[p][:, k // 4, (k % 4) * n:(k % 4 + 1) * n], xraw[0:n, t, k * P:(k + 1) * P], ident[0:n, 0:n])
                J.made_by(ins)
            pe.wait_ge(rows_in, 16 * 12)
            p = J.begin(pe, "par")
            J.made_by(pe.transpose(pair[p][:, 0, 0:NROWS], rawR[0:NROWS, :], ident[0:NROWS, 0:NROWS]))
            spread("nb1")
            pe.wait_ge(states_in, 16 * 3)
            p = J.begin(pe, "sta")
            for k in range(KP):
                ks = slice(k * P, (k + 1) * P)
                n = DEC * PBUF
                pe.transpose(pair[p][:, 0, k * n:(k + 1) * n], rawP[0:n, ks], ident[0:n, 0:n])
                n = DEC * CBUF
                pe.transpose(pair[p][:, 1, k * n:(k + 1) * n], rawC[0:n, ks], ident[0:n, 0:n])
                ins = pe.transpose(pair[p][:, 1, 96 + k * DEC:96 + (k + 1) * DEC], rawH[0:DEC, ks], ident[0:DEC, 0:DEC])
            J.made_by(ins)
            for n in range(2 * KP):
                Z.product(pe, pair, n, h_hi, h1_lo, (lambda k: pe.wait_ge(h_lo_made, k + 1)) if n == 0 else None)
            pe.wait_ge(bd_in, 16 * 4)
            for i in range(KP):
                pe.wait_ge(conv_done, i + 1)
                for s, what in enumerate("ri"):
                    project((what, i), lambda k: bdw[:, s, i, :], lambda k: cT[:, i, :], range(1))
            pe.wait_ge(mem_scaled, MT)
            for q in range(2):
                p = J.begin(pe, ("mT", q))
                for j in range(4):
                    for t in range(MT):
                        k = 4 * q + j
                        ins = pe.transpose(pair[p][:, j // 2, (j % 2) * NMEM + t * P:(j % 2) * NMEM + (t + 1) * P],
                                           mraw[:, t, k * P:(k + 1) * P], ident[:, :])
                J.made_by(ins)
            for n in range(2 * KP, 3 * KP):
                Z.product(pe, pair, n, h_hi, h1_lo)
            p = J.begin(pe, "st")
            J.wait_taken(pe, ("z", 3))
            for i in range(KP):
                pe.transpose(pair[p][0:CBUF + DEC, 0, i * P:(i + 1) * P], uR[:, i, SEQ:CBUF + NT], ident[:, :])
                ins = pe.transpose(pair[p][0:PBUF + DEC, 1, i * P:(i + 1) * P], uP[:, i, SEQ:PBUF + NT], ident[:, :])
            J.made_by(ins)
            for what, w, arrived in (("K", wk_v, wk_in), ("V", wv_v, wv_in)):
                pe.wait_ge(arrived, 16)
                for t in range(MT):
                    p = J.begin(pe, (what, t))
                    for k in range(KD):
                        if what == "K" and t == 0:
                            J.wait_taken(pe, ("mT", k // 4))
                        for h in range(2):
                            ins = pe.matmul(pair[p][:, h, :], mT[:, k, t * P:(t + 1) * P], w[:, k, h * 512:(h + 1) * 512],
                                            start=k == 0, stop=k == KD - 1)
                    J.made_by(ins)
            for q in range(2):
                p = J.begin(pe, ("KT", q))
                if q == 0:
                    J.wait_taken(pe, ("K", 1))
                for j in range(4):
                    for t in range(MT):
                        k = 4 * q + j
                        ins = pe.transpose(pair[p][:, j // 2, (j % 2) * NMEM + t * P:(j % 2) * NMEM + (t + 1) * P],
                                           Kt[:, t, k * P:(k + 1) * P], ident[:, :])
                J.made_by(ins)
            pe.wait_ge(plw_in, 16)
            for g in range(KP):
                pe.wait_ge(d_ready, g + 1)
                project(("yp", g), lambda k: plw[:, g, :], lambda k: dT[:, g, :], range(1))
            for k in range(KP):
                sum_squares(k, sqP, k == 0, k == KP - 1)
            spread("nbp")
            for k in range(KP):
                sum_squares(k, rT, k == 0, k == KP - 1)
            spread("nbr")
            p = J.begin(pe, "hl")
            for i in range(KP):
                ins = pe.transpose(pair[p][0:1 + DEC, 0, i * P:(i + 1) * P], cT[:, i, SEQ - 1:NT], ident[:, :])
            J.made_by(ins)

            def into_residual(what, product):
                for m in range(KD):
                    product(m)
                added = KD - 2 if what == "x1" else 2 * (KD - 2)
                sum_squares(0, sqT, True, False, (sq_added, added))
                seen["squares"] += KD - 1
                sum_squares(KD - 1, sqT, False, True)

            into_residual("x1", lambda m: O.product(pe, pair, m, h_hi, y_lo,
                                                    (lambda k: pe.wait_ge(h_lo_made, KD + k + 1)) if m == 0 else None))
            spread("nb2")
            for n in range(KD):
                Q.product(pe, pair, n, h_hi, h2_lo, (lambda k: pe.wait_ge(h_lo_made, 2 * KD + k + 1)) if n == 0 else None)
            p = J.begin(pe, "qs")
            for k in range(KD):
                J.wait_taken(pe, ("q", k))
                ins = pe.transpose(pair[p][0:DEC, k // 4, (k % 4) * P:(k % 4 + 1) * P], qT[:, k, SEQ:NT], ident[:, :])
            J.made_by(ins)
            nb = DEC * HEADS
            def out(h, cc):
                q = J.begin(pe, ("o", h, cc))
                J.wait_taken(pe, ("pT", h, TT - 1))
                for m in range(MT):
                    lo = h * HD + cc * P
                    ins = pe.matmul(bank[q], Vt[:, m, lo:lo + P], PT[:, h % 2, m, :], start=m == 0, stop=m == MT - 1)
                J.made_by(ins)

            for n in range(len(STEPS) + BEHIND):
                if n < len(STEPS):
                    h, t = STEPS[n]
                    q = J.begin(pe, ("s", h, t))
                    for k in range(2):
                        ins = pe.matmul(bank[q][:, 0:NMEM], qT[:, 2 * h + k, t * P:(t + 1) * P], KT[:, 2 * h + k, :],
                                        start=k == 0, stop=k == 1)
                    J.made_by(ins)
                if n >= BEHIND:
                    h, t = STEPS[n - BEHIND]
                    q = J.begin(pe, ("pT", h, t))
                    pe.wait_ge(att_norm, n - BEHIND + 1)
                    for m in range(MT):
                        ins = pe.transpose(bank[q][:, m * P:(m + 1) * P], pr[:, (n - BEHIND) % 4, m * P:(m + 1) * P], ident[:, :])
                    J.made_by(ins)
                    if h and t < 2:
                        out(h - 1, t)
            out(HEADS - 1, 0)
            q = J.begin(pe, "sS")
            pe.wait_ge(qb_used, DEC)
            for m in range(MT):
                ins = pe.transpose(bank[q][0:nb, m * P:(m + 1) * P], sS[:, m, :], ident[:, :])
            J.made_by(ins)
            out(HEADS - 1, 1)
            q = J.begin(pe, "pS")
            pe.wait_ge(s_norm, 1)
            for m in range(MT):
                ins = pe.transpose(bank[q][:, m * nb:(m + 1) * nb], pSm[0:nb, m * P:(m + 1) * P], ident[0:nb, 0:nb])
            J.made_by(ins)
            p = J.begin(pe, "oS")
            J.wait_taken(pe, "pS")
            pe.wait_ge(v_in[0], 32)
            pe.wait_ge(v_in[1], 64)
            pe.wait_ge(v_in[2], 32)
            for h in range(HEADS):
                for b in range(DEC):
                    for m in range(MT):
                        ins = pe.matmul(pair[p][0:DEC, h // 2, h % 2 * HD:(h % 2 + 1) * HD],
                                        pad8[:, m * HEADS + h, b * DEC:(b + 1) * DEC], vc[b][:, m, h * HD:(h + 1) * HD],
                                        start=b == 0 and m == 0, stop=b == DEC - 1 and m == MT - 1)
            J.made_by(ins)
            q = J.begin(pe, "oST")
            J.wait_taken(pe, "oS")
            for k in range(KD):
                ins = pe.transpose(bank[q][:, k * DEC:(k + 1) * DEC], oSr[0:DEC, k * P:(k + 1) * P], ident[0:DEC, 0:DEC])
            J.made_by(ins)
            wo_v = view(regB, 0, KD, D)
            J.wait_taken(pe, "oST")
            pe.wait_ge(wo_in, 16)
            into_residual("x2", lambda m: project(("x2", m), lambda k: wo_v[:, k, m * P:(m + 1) * P], lambda k: oT[:, k, :], range(KD)))
            spread("nb3")
            ready = normed_tiles(0, "nb3", KD)
            p = J.begin(pe, "rt")
            pe.wait_ge(rw_in, 32)
            for t, (t0, n) in enumerate(TILES):
                for k in range(KD):
                    ready(k)
                    ins = pe.matmul(pair[p][0:n, 0, t * NE:(t + 1) * NE], hT[:, k, t0:t0 + n], rw[:, k, :], start=k == 0, stop=k == KD - 1)
            J.made_by(ins)

            def rows_of(name, src, t0, n):
                p = J.begin(pe, name)
                for k in range(KD):
                    ins = pe.transpose(pair[p][0:n, k // 4, (k % 4) * P:(k % 4 + 1) * P], src[:, k, t0:t0 + n], ident[:, :])
                J.made_by(ins)

            for t, (t0, n) in enumerate(TILES):
                rows_of(("hR", t), hT, t0, n)
            pe.wait_ge(sh_in, 48)
            for m in range(KF):
                project(("sg", m), lambda k: sgw[:, k, m * P:(m + 1) * P], lambda k: hT[:, k, :], range(KD))
                project(("su", m), lambda k: suw[:, k, m * P:(m + 1) * P], lambda k: hT[:, k, :], range(KD))
            p = J.begin(pe, "pos")
            pe.wait_ge(masked, 1)
            for t in range(NTT):
                for s in range(t + 1):
                    pe.matmul(pair[p][:, 0, t * NE:(t + 1) * NE], low if s == t else ones[:, :], msk[:, s, :], start=s == 0, stop=s == t)
            for s in range(NTT):
                ins = pe.matmul(pair[p][:, 0, NTT * NE:(NTT + 1) * NE], ones[:, :], msk[:, s, :], start=s == 0, stop=s == NTT - 1)
            J.made_by(ins)
            for t in range(2):
                rows_of(("xR", t), xT, t * P, P)
            p = J.begin(pe, "tab")
            pe.wait_ge(tab_ready, 1)
            J.made_by(pe.transpose(pair[p][0:1, 0, 0:P], ebc[:, 0:1], ident[:, :]))

            def slots(b):
                pe.wait_ge(onehot, b + 1)
                for t in range(NTT):
                    ins = pe.matmul(pS[0:SLOTS, 0, 0:6], oneh[:, t, :], rhsw[:, t, :], start=t == 0, stop=t == NTT - 1)
                ins.then_inc(slots_made, 1)

            for t, (t0, n) in enumerate(TILES):
                if t >= 2:
                    rows_of(("xR", t), xT, t0, n)
                p = J.begin(pe, ("sd", t))
                for m in range(KF):
                    J.wait_taken(pe, ("su", m))
                    for h in range(2):
                        ins = pe.matmul(pair[p][0:n, h, :], sA[:, m, t0:t0 + n], sdw[:, m, h * 512:(h + 1) * 512],
                                        start=m == 0, stop=m == KF - 1)
                J.made_by(ins)
                if t < 3:
                    if t:
                        pe.wait_ge(idx_ready, t)
                    slots(t)

            pe.wait_ge(row_table, 1)
            n_turns = turns(pe)
            J.wait_taken(pe, ("xR", NTT - 1))
            J.wait_taken(pe, ("sd", NTT - 1))
            J.wait_taken(pe, "pos")

            def turn(r, b, q, first=False):
                pe.wait_ge(gath_in[r], q * 16 + 16)
                if not first:
                    pe.wait_ge(turned_a, b)
                    pe.wait_ge(turned_d, b)
                g3 = gath[r].rearrange("p (f k) -> p k f", k=KD)
                for k in range(KD):
                    ins = pe.transpose(pair[1][:, k // 4, (k % 4) * SLOTS:(k % 4 + 1) * SLOTS], g3[0:SLOTS, k, :], ident[0:SLOTS, 0:SLOTS])
                ins.then_inc(turned, 1)

            def gate_up(r, b, q, ks, first=False):
                if ks[0] == 0:
                    pe.wait_ge(wg_in[r], q * 32 + 32)
                    pe.wait_ge(turned_a, b + 1)
                    pe.wait_ge(turned_d, b + 1)
                    if not first:
                        pe.wait_ge(act_b, b)
                w = WG[r].rearrange("p s (k f) -> p s k f", k=KD)
                for k in ks:
                    ins = pe.matmul(pair[0][0:SLOTS, 0, :].rearrange("p (s f) -> p s f", s=2), hX[:, k, :], w[:, :, k, :],
                                    start=k == 0, stop=k == KD - 1, skip_group_check=True)
                if ks[-1] == KD - 1:
                    ins.then_inc(gu_made, 1)

            def turn_act(b):
                pe.wait_ge(act_b, b + 1)
                a3 = act.rearrange("p (f k) -> p k f", k=KF)
                for k in range(KF):
                    ins = pe.transpose(pair[0][:, 1, k * SLOTS:(k + 1) * SLOTS], a3[0:SLOTS, k, :], ident[0:SLOTS, 0:SLOTS])
                ins.then_inc(at_made, 1)

            def down(r, b, q):
                pe.wait_ge(at_taken, b + 1)
                pe.wait_ge(wd_in[r], q * 16 + 16)
                pe.wait_ge(down_a, b + 1)
                pe.wait_ge(down_d, b + 1)
                for k in range(KF):
                    for h in range(2):
                        ins = pe.matmul(pair[2][0:SLOTS, h, :], aX[:, k, :], WD[r][:, k, h * 512:(h + 1) * 512],
                                        start=k == 0, stop=k == KF - 1)
                ins.then_inc(down_made, 1)

            turn(0, 0, 0, first=True)
            gate_up(0, 0, 0, range(KD), first=True)
            turn(1, 1, 0)
            with pe.Fori(0, n_turns) as i:
                for j in range(RING):
                    b = i * RING + (j + 1)
                    pe.wait_ge(idx_ready, b + 2)
                    slots(b + 2)
                    gate_up((j + 1) % RING, b, i + (j + 1) // RING, range(0, 4))
                    turn_act(b - 1)
                    gate_up((j + 1) % RING, b, i + (j + 1) // RING, range(4, KD))
                    turn((j + 2) % RING, b + 1, i + (j + 2) // RING)
                    down(j, b - 1, i)
            turn_act(n_turns * RING)
            down(0, n_turns * RING, n_turns)


_INS = ["x_prompt", "x_sample", "state_pool", "state_conv", "state_h", "cache_mem_k", "cache_mem_v", "mem_prompt",
        "norm_mix", "w_in", "pool_w", "pool_scale", "conv_w", "conv_b", "gate_a_w", "gate_a_b", "gate_x_w",
        "gate_x_b", "lru_lambda", "norm_pool_out", "norm_rnn_out", "w_out", "norm_xattn", "norm_mem", "xa_wq",
        "xa_wk", "xa_wv", "xa_wo", "norm_ffn", "router_w", "router_bias", "exp_w_gate", "exp_w_up", "exp_w_down",
        "sh_w_gate", "sh_w_up", "sh_w_down", "norm_final"]
_OUTS = [(1, SEQ, D), (DEC, 1, D), (1, 1, PBUF, DP), (1, 1, CBUF, DP), (1, 1, DP), (1, 1, NMEM, HEADS, HD),
         (1, 1, NMEM, HEADS, HD), (1, DEC, PBUF, DP), (1, DEC, CBUF, DP), (1, DEC, DP)]


def kernel(**inputs):
    import numpy as _np
    import concourse.bacc as _bacc
    from concourse.bass_utils import run_bass_kernel_spmd as _run

    nc = _bacc.Bacc("TRN2", target_bir_lowering=False, num_devices=1)
    arrays, args = {}, []
    for name in _INS:
        a = _np.ascontiguousarray(inputs[name])
        arrays[f"in_{name}"] = a
        args.append(nc.dram_tensor(f"in_{name}", a.shape, F32, kind="ExternalInput").ap())
    for i, shape in enumerate(_OUTS):
        args.append(nc.dram_tensor(f"out_{i}", shape, F32, kind="ExternalOutput").ap())
    for name, shape in (("h_rows", (NT, D)), ("acc_rows", (NT, D)), ("q_rows", (DEC, D))):
        args.append(nc.dram_tensor(name, shape, F32, kind="Internal").ap())
    trunk(nc, *args)
    r = _run(nc, [arrays], core_ids=[0])
    return tuple(r.results[0][f"out_{i}"] for i in range(len(_OUTS)))
```

```python
from contextlib import ExitStack

import concourse.bass as bass
from concourse import mybir

F32, I32, U32, BF16 = mybir.dt.float32, mybir.dt.int32, mybir.dt.uint32, mybir.dt.bfloat16
F32R = mybir.dt.float32r
ACT, ALU, AX = mybir.ActivationFunctionType, mybir.AluOpType, mybir.AxisListType

P = 128
D = 1024
KD = D // P
SEQ, DEC = 512, 8
NT = SEQ + DEC
HALF = NT // 2
TT = SEQ // P
TILES = [(t * P, P) for t in range(TT)] + [(SEQ, DEC)]
NTT = len(TILES)
DP = D // 2
KP = DP // P
WINDOWS = (2, 4, 8, 16)
PBUF, CBUF = 15, 3
NMEM, MT = 256, 2
HEADS, HD = 4, 256
NE, NG, EG, TOPG = 64, 8, 8, 4
FE, KF = 256, 2
EPS = 1e-6
SCALE = HD ** -0.5
LRU_C = 8.0
ROUTED = 2.5
FAR = 1024
HALF_K = KD // 2
SPLIT_RING = 3
SLOTS = 96
RING = 4
PAIR = 2
STEPS = [(h, t) for h in range(HEADS) for t in range(TT)]
BEHIND = 3

ROWS = [("norm_mix", 8), ("norm_xattn", 8), ("norm_mem", 8), ("norm_ffn", 8), ("pool_scale", 4), ("conv_w", 16),
        ("conv_b", 4), ("gate_a_b", 4), ("gate_x_b", 4), ("lru_lambda", 4), ("norm_pool_out", 4), ("norm_rnn_out", 4)]
COL, NROWS = {}, 0
for _n, _k in ROWS:
    COL[_n] = NROWS
    NROWS += _k

MAX_TURNS = -(-(NE + NT * 8 // SLOTS) // RING)


class Count:

    def __init__(self):
        self.n = {}

    def add(self, ins, sem, k=1):
        ins.then_inc(sem, k)
        self.n[id(sem)] = self.n.get(id(sem), 0) + k
        return sem, self.n[id(sem)]


class Products:

    def __init__(self, order, made, taken):
        self.names = [o[0] for o in order]
        self.no = {n: j for j, n in enumerate(self.names)}
        self.by = [o[1] for o in order]
        self.made, self.taken = made, taken
        self.at = [self.by[:j + 1].count(e) for j, e in enumerate(self.by)]
        self.began, self.sent = 0, dict.fromkeys(taken, 0)
        self.place, self.before, last, nxt = [], [], {}, 0
        for j, o in enumerate(order):
            single = len(o) > 2 and o[2] == 1
            nxt = 2 * o[3] if len(o) > 3 else (nxt if single else nxt + nxt % 2) % 6
            banks = (nxt,) if single else (nxt, nxt + 1)
            self.place.append(nxt if single else nxt // 2)
            self.before.append([last[b] for b in banks if b in last])
            last.update((b, j) for b in banks)
            nxt += len(banks)

    def begin(self, pe, name):
        j = self.no[name]
        assert j == self.began, (name, self.names[self.began])
        self.began += 1
        for e in self.taken:
            earlier = [i for i in self.before[j] if self.by[i] == e]
            if earlier:
                pe.wait_ge(self.taken[e], self.at[max(earlier)])
        return self.place[j]

    def made_by(self, ins):
        ins.then_inc(self.made, 1)

    def wait_made(self, eng, name):
        j = self.no[name]
        eng.wait_ge(self.made, j + 1)
        return self.place[j]

    def take(self, ins, name):
        j = self.no[name]
        e = self.by[j]
        self.sent[e] += 1
        assert self.sent[e] == self.at[j], name
        ins.then_inc(self.taken[e], 1)
        return self.taken[e], self.at[j]

    def wait_taken(self, eng, name):
        j = self.no[name]
        eng.wait_ge(self.taken[self.by[j]], self.at[j])


class SplitWeights:

    def __init__(self, J, names, weights, arrived, parts, hi_made, lo_made, half_used):
        self.J, self.names, self.weights, self.arrived, self.parts = J, names, weights, arrived, parts
        self.hi_made, self.lo_made, self.half_used = hi_made, lo_made, half_used
        self.units = 2 * len(names)

    def cut_hi(self, a, u):
        if u >= self.units:
            return
        if u in self.arrived:
            a.wait_ge(self.arrived[u], 16)
        old = u - SPLIT_RING
        if old >= 0 and old % 2:
            a.wait_ge(self.J.made, self.J.no[self.names[old // 2]] + 1)
        elif old >= 0:
            a.wait_ge(self.half_used, old // 2 + 1)
        a.copy(self.parts[:, u % SPLIT_RING, 0], self.weights(u // 2, u % 2)).then_inc(self.hi_made, 1)

    def cut_lo(self, v, u):
        if u >= self.units:
            return
        v.wait_ge(self.hi_made, u + 1)
        v.tensor_tensor(self.parts[:, u % SPLIT_RING, 1], self.weights(u // 2, u % 2),
                        self.parts[:, u % SPLIT_RING, 0].bitcast(F32), ALU.subtract).then_inc(self.lo_made, 1)

    def product(self, pe, pair, n, acts_hi, acts_lo, ready=None):
        p = self.J.begin(pe, self.names[n])
        for u in (2 * n, 2 * n + 1):
            pe.wait_ge(self.lo_made, u + 1)
            for j in range(HALF_K):
                k = (u % 2) * HALF_K + j
                if ready:
                    ready(k)
                hi, lo = self.parts[:, u % SPLIT_RING, 0, j, :], self.parts[:, u % SPLIT_RING, 1, j, :]
                for h in range(2):
                    cols = slice(h * HALF, (h + 1) * HALF)
                    for i, (w, x) in enumerate(((hi, acts_hi), (lo, acts_hi), (hi, acts_lo))):
                        ins = pe.matmul(pair[p][:, h, 0:HALF], w, x[:, k, cols], start=k == 0 and i == 0,
                                        stop=k == KD - 1 and i == 2)
            if u % 2 == 0:
                ins.then_inc(self.half_used, 1)
        self.J.made_by(ins)


def product_order():
    o = [(("xT", t), "dve") for t in range(NTT)] + [("par", "dve"), ("nb1", "dve"), ("sta", "dve")]
    o += [(("z", m), "act") for m in (4, 5, 6, 7, 8, 9, 10, 11)]
    for i in range(KP):
        o += [(("r", i), "act"), (("i", i), "act")]
    o += [(("mT", q), "act") for q in range(2)]
    o += [(("z", m), "act") for m in range(4)] + [("st", "act")]
    o += [(("K", t), "act") for t in range(MT)] + [(("yp", g), "act") for g in range(KP)] + [(("V", 0), "act"), (("KT", 0), "act")]
    o += [("nbp", "dve"), (("KT", 1), "act"), (("V", 1), "act"), ("nbr", "dve"), ("hl", "act")]
    o += [(("x1", m), "dve") for m in range(KD)] + [("nb2", "dve")]
    o += [(("q", m), "act") for m in range(KD)] + [("qs", "act")]
    for n in range(len(STEPS) + BEHIND):
        if n < len(STEPS):
            o.append((("s", *STEPS[n]), "act", 1))
        if n >= BEHIND:
            h, t = STEPS[n - BEHIND]
            o.append((("pT", h, t), "act", 1))
            if h and t % 2:
                o.append((("o", h - 1, t // 2), "act", 1))
    o += [(("o", HEADS - 1, 0), "act", 1), ("sS", "act", 1), (("o", HEADS - 1, 1), "act", 1)]
    o += [("pS", "act", 1), ("oS", "act"), ("oST", "act", 1)]
    o += [(("x2", m), "dve") for m in range(KD)] + [("nb3", "dve")]
    o += [("rt", "act")]
    o += [(("hR", t), "act") for t in range(NTT)]
    for m in range(KF):
        o += [(("sg", m), "act"), (("su", m), "dve")]
    o += [("pos", "dve", 2, 0), (("sd", 0), "act", 2, 1), (("sd", 1), "act", 2, 2), ("tab", "dve", 2, 0)]
    o += [(("sd", 2), "act", 2, 1), (("sd", 3), "act", 2, 2), (("sd", 4), "act", 2, 2)]
    return o


def trunk(nc, x_prompt, x_sample, state_pool, state_conv, state_h, cache_mem_k, cache_mem_v, mem_prompt, norm_mix,
          w_in, pool_w, pool_scale, conv_w, conv_b, gate_a_w, gate_a_b, gate_x_w, gate_x_b, lru_lambda,
          norm_pool_out, norm_rnn_out, w_out, norm_xattn, norm_mem, xa_wq, xa_wk, xa_wv, xa_wo, norm_ffn, router_w,
          router_bias, exp_w_gate, exp_w_up, exp_w_down, sh_w_gate, sh_w_up, sh_w_down, norm_final,
          y_prompt, y_sample, new_pool_p, new_conv_p, new_h_p, new_k, new_v, new_pool_s, new_conv_s, new_h_s,
          h_rows, acc_rows, q_rows):
    with ExitStack() as ctx:
        def sb(name, shape, dt=F32):
            return ctx.enter_context(nc.sbuf_tensor(name, shape, dt))

        def sem(name):
            return ctx.enter_context(nc.semaphore(name))

        with nc.sbuf_tensor("down_parts1", [P, 2, KF, D], F32R) as down_parts1:
            pass
        xT = sb("xT", [P, KD, NT])
        with nc.sbuf_tensor("down_parts0", [P, 2, KF, D], F32R) as down_parts0:
            pass
        with nc.sbuf_tensor("h_hi", [P, KD, NT], F32R) as h_hi:
            pass
        hT = sb("hT", [P, KD, NT])
        with nc.sbuf_tensor("unused_A", [P, 8192], F32), nc.sbuf_tensor("w_parts", [P, SPLIT_RING, 2, HALF_K, P], F32R) as w_parts:
            pass
        regA = sb("regA", [P, 12288])
        regB = sb("regB", [P, 8192])
        with nc.sbuf_tensor("h1_lo", [P, KD, NT], F32R) as h1_lo, nc.sbuf_tensor("win_parts", [P, SPLIT_RING, 2, HALF_K, P], F32R) as win_parts:
            pass
        with nc.sbuf_tensor("unused_C", [P, 6144], F32), nc.sbuf_tensor("act_parts", [P, 2, KF, SLOTS], F32R) as act_parts:
            pass
        down_parts = [down_parts0, down_parts1]
        regC = sb("regC", [P, 8192])
        with nc.sbuf_tensor("y_lo", [P, KD, NT], F32R) as y_lo:
            pass
        with nc.sbuf_tensor("unused_L2", [P, 6144], F32), nc.sbuf_tensor("o_hi", [P, KD, NT], F32R) as o_hi:
            pass
        with nc.sbuf_tensor("unused_L", [P, 4160], F32), nc.sbuf_tensor("h2_lo", [P, KD, NT], F32R) as h2_lo:
            pass
        regL = sb("regL", [P, 14640])
        par = sb("par", [P, NROWS])
        ident = sb("ident", [P, P])
        ones = sb("ones", [P, P])
        small = sb("small", [P, 160])

        def view(reg, at, *shape):
            n = 1
            for s in shape:
                n *= s
            v = reg[:, at:at + n]
            if len(shape) == 2:
                v = v.rearrange("p (a b) -> p a b", a=shape[0])
            elif len(shape) == 3:
                v = v.rearrange("p (a b c) -> p a b c", a=shape[0], b=shape[1])
            return v

        ssq, rs = small[:, 0:5], small[:, 5:10]
        mss, mrs = small[:, 10:12], small[:, 12:14]
        eps_c = small[:, 14:15]
        nsp, psp = small[:, 16:20], small[:, 20:24]
        spt = small[:, 24:64]
        r15 = small[:, 64:80]
        amax, asum = small[:, 80:84], small[:, 84:88]
        nmax, rsum = small[:, 88:92], small[:, 92:96]
        smx, snm, sss, srs = (small[:, 96 + j:97 + j] for j in range(4))
        zero5 = small[:, 104:109]
        fin = small[:, 110:130]

        w_in_v = [view(regA, KD * DP * j, KD, DP) for j in range(3)]
        xraw = view(regL, 6312, NTT, D)
        xsq = view(regL, 11432, D)
        htmp1, ytmp, htmp2 = view(regL, 11432, 2, NT), view(regL, 12552, 2, NT), view(regL, 8320, 2, NT)
        rawP, rawC, rawH = view(regL, 4232, DP), view(regL, 4232 + DP, DP), view(regL, 4232 + 2 * DP, DP)
        rawR = view(regL, 4232 + 3 * DP, P)
        uP = view(regL, 0, KP, PBUF + NT)
        uR = view(regL, 2140, KP, CBUF + NT)
        aT = view(regL, 2140, KP, NT)
        gT = view(regL, 4232, KP, NT)
        cT = view(regL, 6312, KP, NT)
        rT = view(regL, 8392, KP, NT)
        iT = view(regL, 10472, KP, NT)
        sqT, sqU = view(regL, 8392, KD, NT), view(regL, 10304, KD, NT)
        stP = view(regL, 12552, KP, DEC, PBUF)
        stC = view(regL, 13032, KP, DEC, CBUF)
        stH = view(regL, 13128, KP, DEC)
        bdw = view(regL, 13160, 2, KP, P)
        hflat = hT[:, :, :].rearrange("p k n -> p (k n)")
        dT = hT[:, 0:KP, :]
        ptmp = [hflat[:, 2080 + 535 * j:2080 + 535 * (j + 1)] for j in range(2)]
        a2 = hflat[:, 3150:3670]
        sqP = view(regL, 0, KP, NT)
        stO = view(regA, 8192, 2, DP)
        plw = view(regA, 10240, KP, P)
        hlO = view(regA, 11264, DP)
        wk_v, wv_v = view(regB, 0, KD, D), view(regC, 0, KD, D)
        mraw = view(regA, 0, MT, D)
        KT = view(regA, 0, KD, NMEM)
        mT = view(regA, 2048, KD, NMEM)
        msq = view(regA, 2048, MT, D)
        Kt, Vt = view(regA, 4096, MT, D), view(regA, 6144, MT, D)
        qT = view(regL, 0, KD, NT)
        PT = view(regL, 4160, 2, MT, SEQ)
        kc = [view(regL, 6208 + 2048 * j, MT, D) for j in range(2)]
        kroom = [view(regB, 2048 * j, MT, D) for j in range(4)]
        kcache = kroom + kc + kroom[0:2]
        vspare = [view(regL, 10304, MT, D), view(regL, 12352, MT, D)]
        qb = view(regA, 8192, 2, D)
        pr = view(regA, 10240, 4, NMEM)
        sS = view(regA, 11264, MT, DEC * HEADS)
        pSm = view(regA, 11328, NMEM)
        pad8 = view(regA, 11648, MT * HEADS, DEC * DEC)
        oSr = view(regL, 4160, D)
        qsr = view(regL, 5184, D)
        oT, o_lo = hT, h_hi
        vc = [view(regC, 2048 * j, MT, D) for j in range(4)] + vspare + [view(regA, 2048, MT, D), view(regA, 4096, MT, D)]
        sgw, suw = view(regC, 0, KD, FE), view(regC, 2048, KD, FE)
        sdw = view(regC, 4096, KF, D)
        rw = view(regC, 6144, KD, NE)
        sco = view(regC, 6656, NTT, NE)
        bia = view(regC, 6976, NTT, NE)
        rbias = view(regC, 7296, NE)
        msk = view(regC, 7360, NTT, NE)
        gwt = view(regC, 7680, NTT, NE)
        rows = view(regL, 0, NTT, D)
        sA = view(regL, 5120, KF, NT)
        m8 = view(regL, 6160, NTT, NG * 8)
        gs = view(regL, 6480, NTT, NG)
        g8 = view(regL, 6520, NTT, 8)
        gi = view(regL, 6560, NTT, 8)
        gif = view(regL, 6600, NTT, 8)
        gmk = view(regL, 6640, NTT, NG)
        geq = view(regL, 6680, NTT, NG)
        pen = view(regL, 6720, NTT, NG)
        top = view(regL, 6760, NTT, 8)
        mrep = view(regL, 6800, NTT, NE)
        wsu = view(regL, 7120, NTT)
        valid = view(regL, 7125, NTT)
        iot8 = view(regL, 7130, NG)
        low = view(regL, 7140, P)
        slot = view(regL, 7268, NTT, NE)
        nblk, bend, bbase = view(regL, 7588, NE), view(regL, 7652, NE), view(regL, 7716, NE)
        iotp = view(regL, 7780, 1)
        ebc = view(regL, 7781, 2)
        j3 = view(regL, 7784, 48)
        cmp = view(regL, 7832, NE)
        iots = view(regL, 7896, SLOTS)
        first3, expert3 = view(regL, 8026, RING), view(regL, 8030, 1)
        delta, later = view(regL, 8750, RING), view(regL, 8754, NTT, RING)
        NI = view(regL, 8024, 8)
        ET = view(regL, 8032, P)
        oneh = view(regL, 8160, NTT * SLOTS // 2).bitcast(BF16).rearrange("p (t n) -> p t n", t=NTT)
        whole, part = view(regL, 8400, NTT, 2), view(regL, 8410, NTT, NE)
        rhsw = view(regL, 8730, 16).bitcast(BF16)[:, 0:NTT * 6].rearrange("p (t c) -> p t c", t=NTT)
        wparts = view(regL, 13688, 3 * NTT * NE // 2).bitcast(BF16).rearrange("p (c t e) -> p c t e", c=3, t=NTT)
        idx = view(regL, 8808, RING)
        sums = view(regL, 8800, RING, 2)
        sidx = view(regL, 8812, RING)
        swl = view(regL, 8816, RING)
        gath = [view(regL, 8824 + D * j, D) for j in range(PAIR)]
        hX = view(regL, 11896, KD, SLOTS)
        sil = view(regL, 12920, FE)
        act = view(regL, 13176, FE)
        yX = [view(regL, 0 + D * j, D) for j in range(RING)]
        WG = [view(regA, 0, 2, KD * FE), view(regA, 6144, 2, KD * FE), view(regB, 0, 2, KD * FE), view(regC, 0, 2, KD * FE)]
        WD = [view(regA, 4096, KF, D), view(regA, 10240, KF, D), view(regB, 4096, KF, D), view(regB, 6144, KF, D)]
        yf = view(regA, 0, NTT, D)
        gfin = view(regC, 4096, D)
        junk = view(regC, 5120, D)

        pair = [ctx.enter_context(nc.psum_tensor(f"pair{j}", [P, 2, 512], F32)) for j in range(3)]
        bank = [pair[j // 2][:, j % 2, :] for j in range(6)]
        pS = ctx.enter_context(nc.psum_tensor("pS", [P, 2, 512], F32))

        made, act_took, dve_took = sem("made"), sem("act_took"), sem("dve_took")
        J = Products(product_order(), made, {"act": act_took, "dve": dve_took})
        x_in, rows_in, states_in, mem_in = [sem(f"x_in{t}") for t in range(NTT)], sem("rows_in"), sem("states_in"), sem("mem_in")
        win_in = [sem(f"win_in{j}") for j in range(4)]
        h_made, h_hi_made, h_lo_made = sem("h_made"), sem("h_hi_made"), sem("h_lo_made")
        split_z = [sem(s) for s in ("win_hi", "win_lo", "win_half_used")]
        split_o = [sem(s) for s in ("wout_hi", "wout_lo", "wout_half_used")]
        split_x = [sem(s) for s in ("wo_hi", "wo_lo", "wo_half_used")]
        o_hi_made, o_lo_made, group_added = sem("o_hi_made"), sem("o_lo_made"), sem("group_added")
        split_q = [sem(s) for s in ("wq_hi", "wq_lo", "wq_half_used")]
        wk_in, wv_in, bd_in, plw_in = sem("wk_in"), sem("wv_in"), sem("bd_in"), sem("plw_in")
        wout_in, wq_in, wo_in, sh_in, rw_in = sem("wout_in"), sem("wq_in"), sem("wo_in"), sem("sh_in"), sem("rw_in")
        consts, bd_zero = sem("consts"), sem("bd_zero")
        dve_step, act_step, pool_step = sem("dve_step"), sem("act_step"), sem("pool_step")
        squares, ss_done, root, inverse, normed = sem("squares"), sem("ss_done"), sem("root"), sem("inverse"), sem("normed")
        mem_scaled, mem_ss, mem_inv = sem("mem_scaled"), sem("mem_ss"), sem("mem_inv")
        conv_done, lru_a, lru_s, lru_m2, lru_m, y_rnn, padded = (
            sem(s) for s in ("conv_done", "lru_a", "lru_s", "lru_m2", "lru_m", "y_rnn", "padded"))
        sp_ready, pooled, d_ready = sem("sp_ready"), sem("pooled"), sem("d_ready")
        stored = sem("stored")
        q_stored, qb_in, qb_used = sem("q_stored"), [sem("qb_in0"), sem("qb_in1")], sem("qb_used")
        kc_in, kb_in, v_in = [sem(f"kc_in{b}") for b in range(4, DEC)], sem("kb_in"), [sem(f"v_in{j}") for j in range(3)]
        kv_stored = sem("kv_stored")
        att_max, att_inv, att_norm = sem("att_max"), sem("att_inv"), sem("att_norm")
        s_max, s_norm = sem("s_max"), sem("s_norm")
        h_stored, sums_landed, rows_left, clear = sem("h_stored"), sem("sums_landed"), sem("rows_left"), sem("clear")
        masked, row_table = sem("masked"), sem("row_table")
        wg_in, wd_in = [sem(f"wg_in{j}") for j in range(RING)], [sem(f"wd_in{j}") for j in range(RING)]
        onehot, counted, slots_made, summed, idx_ready = (sem(s) for s in ("onehot", "counted", "slots_made", "summed", "idx_ready"))
        sp_in, sp_exp, tab_ready = sem("sp_in"), sem("sp_exp"), sem("tab_ready")
        gath_in = [sem(f"gath_in{j}") for j in range(PAIR)]
        turned, turned_a, turned_d, gu_made, silu_b, act_b = (sem(s) for s in ("turned", "turned_a", "turned_d", "gu_made", "silu_b", "act_b"))
        at_made, at_taken, down_made, down_a, down_d, sidx_ready = (
            sem(s) for s in ("at_made", "at_taken", "down_made", "down_a", "down_d", "sidx_ready"))
        sco_ones, at_hi, wd_hi, wd_lo = sem("sco_ones"), sem("at_hi"), sem("wd_hi"), sem("wd_lo")
        fin_in = [sem(f"fin_in{t}") for t in range(NTT)]
        fin_ss, fin_root, fin_inv, fin_y, fin_g, sq_added = (sem(s) for s in ("fin_ss", "fin_root", "fin_inv", "fin_y", "fin_g", "sq_added"))

        z_order = [4, 5, 6, 7, 8, 9, 10, 11, 0, 1, 2, 3]
        wout_v, wq_v = view(regB, 0, KD, D), view(regC, 0, KD, D)
        Z = SplitWeights(J, [("z", m) for m in z_order],
                         lambda n, u: w_in_v[n // 4][:, u * HALF_K:(u + 1) * HALF_K, n % 4 * P:(n % 4 + 1) * P],
                         {0: win_in[3], 1: win_in[0], 8: win_in[1], 16: win_in[2]}, win_parts, *split_z)
        O = SplitWeights(J, [("x1", m) for m in range(KD)],
                         lambda n, u: wout_v[:, u * HALF_K:(u + 1) * HALF_K, n * P:(n + 1) * P],
                         {0: wout_in}, w_parts, *split_o)
        X = SplitWeights(J, [("x2", m) for m in range(KD)],
                         lambda n, u: wout_v[:, u * HALF_K:(u + 1) * HALF_K, n * P:(n + 1) * P],
                         {0: wo_in}, w_parts, *split_x)
        Q = SplitWeights(J, [("q", m) for m in range(KD)],
                         lambda n, u: wq_v[:, u * HALF_K:(u + 1) * HALF_K, n * P:(n + 1) * P],
                         {0: wq_in}, w_parts, *split_q)

        block = ctx.enter_context(nc.Block())
        halves = lambda v: v.rearrange("p (h n) -> p h n", h=2)

        def turns(eng):
            return eng.value_load(NI[0:1, 0:1].bitcast(I32), min_val=2, max_val=MAX_TURNS)

        @block.sync
        def _(sp):
            xp = x_prompt.rearrange("o (t p) d -> p (o t) d", p=P)
            for t in range(TT):
                sp.dma_start(xraw[:, t, :], xp[:, t, :]).then_inc(x_in[t], 16)
            sp.dma_start(xraw[0:DEC, TT, :], x_sample.rearrange("b o d -> b (o d)")).then_inc(x_in[TT], 16)
            for name, src in (("norm_mix", norm_mix), ("norm_xattn", norm_xattn), ("norm_mem", norm_mem),
                              ("norm_ffn", norm_ffn), ("pool_scale", pool_scale), ("conv_b", conv_b),
                              ("gate_a_b", gate_a_b), ("gate_x_b", gate_x_b), ("lru_lambda", lru_lambda),
                              ("norm_pool_out", norm_pool_out), ("norm_rnn_out", norm_rnn_out)):
                k = dict(ROWS)[name]
                sp.dma_start(rawR[COL[name]:COL[name] + k, :], src.rearrange("o (k p) -> (o k) p", p=P)).then_inc(rows_in, 16)
            sp.dma_start(rawR[COL["conv_w"]:COL["conv_w"] + 16, :],
                         conv_w.rearrange("o w (k p) -> (o w k) p", p=P)).then_inc(rows_in, 16)
            win = w_in.rearrange("o (k p) n -> p (o k) n", p=P)
            for j, c in enumerate((1, 2, 0)):
                if j == 0:
                    sp.dma_start(w_in_v[j][:, 0:4, :], win[:, 0:4, c * DP:(c + 1) * DP]).then_inc(win_in[3], 16)
                    sp.dma_start(w_in_v[j][:, 4:8, :], win[:, 4:8, c * DP:(c + 1) * DP]).then_inc(win_in[j], 16)
                else:
                    sp.dma_start(w_in_v[j], win[:, :, c * DP:(c + 1) * DP]).then_inc(win_in[j], 16)
                if j == 0:
                    sp.wait_ge(bd_zero, 1)
                    for s, src in enumerate((gate_a_w, gate_x_w)):
                        for half in range(2):
                            lo = half * 64
                            sp.dma_start(bdw[lo:lo + 64, s, :, lo:lo + 64],
                                         src.rearrange("o (k two) i j -> two i (o k) j", two=2)[half]).then_inc(bd_in, 16)
            sp.dma_start(wk_v, xa_wk.rearrange("o (k p) n -> p (o k) n", p=P)).then_inc(wk_in, 16)
            sp.dma_start(new_pool_s[0, :, 0:PBUF - 1, :], state_pool[0, :, 1:PBUF, :]).then_inc(stored, 16)
            sp.dma_start(new_conv_s[0, :, 0:CBUF - 1, :], state_conv[0, :, 1:CBUF, :]).then_inc(stored, 16)
            sp.wait_ge(made, J.no[("z", 7)] + 1)
            sp.dma_start(mraw, mem_prompt.rearrange("o (t p) d -> p (o t) d", p=P)).then_inc(mem_in, 16)
            sp.wait_ge(made, J.no[("z", 3)] + 1)
            sp.dma_start(wv_v, xa_wv.rearrange("o (k p) n -> p (o k) n", p=P)).then_inc(wv_in, 16)
            sp.dma_start(plw, pool_w.rearrange("o g c d -> c (o g) d")).then_inc(plw_in, 16)
            J.wait_taken(sp, "st")
            sp.dma_start(new_conv_p[0, 0], stO[0:CBUF, 0, :]).then_inc(stored, 16)
            sp.dma_start(new_conv_s[0, :, CBUF - 1, :], stO[CBUF:CBUF + DEC, 0, :]).then_inc(stored, 16)
            sp.dma_start(new_pool_p[0, 0], stO[0:PBUF, 1, :]).then_inc(stored, 16)
            sp.dma_start(new_pool_s[0, :, PBUF - 1, :], stO[PBUF:PBUF + DEC, 1, :]).then_inc(stored, 16)
            sp.wait_ge(made, J.no[("K", 1)] + 1)
            sp.dma_start(view(regB, 0, KD, D), w_out.rearrange("o (k p) n -> p (o k) n", p=P)).then_inc(wout_in, 16)
            J.wait_taken(sp, ("V", 1))
            sp.dma_start(new_k.rearrange("o b (t p) h d -> p (o b t) (h d)", p=P), Kt).then_inc(kv_stored, 16)
            sp.dma_start(new_v.rearrange("o b (t p) h d -> p (o b t) (h d)", p=P), Vt).then_inc(kv_stored, 16)
            ck = cache_mem_k.rearrange("o b (t p) h d -> p (o b) t (h d)", p=P)
            cv = cache_mem_v.rearrange("o b (t p) h d -> p (o b) t (h d)", p=P)
            sp.dma_start(view(regC, 0, KD, D), xa_wq.rearrange("o (k p) n -> p (o k) n", p=P)).then_inc(wq_in, 16)
            J.wait_taken(sp, "hl")
            sp.dma_start(new_h_p[0], hlO[0:1, :]).then_inc(stored, 16)
            sp.dma_start(new_h_s[0], hlO[1:1 + DEC, :]).then_inc(stored, 16)
            sp.wait_ge(made, J.no[("x1", KD - 1)] + 1)
            for b in range(4):
                sp.dma_start(kcache[b], ck[:, b]).then_inc(kb_in, 16)
            sp.wait_ge(kv_stored, 32)
            for b in (6, 7):
                sp.dma_start(vc[b], cv[:, b]).then_inc(v_in[2], 16)
            sp.wait_ge(ss_done, 3)
            for b in (4, 5):
                sp.dma_start(vc[b], cv[:, b]).then_inc(v_in[0], 16)
            J.wait_taken(sp, "qs")
            sp.dma_start(q_rows, qsr[0:DEC, :]).then_inc(q_stored, 16)
            sp.wait_ge(q_stored, 16)
            sp.wait_ge(stored, 16 * 8)
            for b in range(DEC):
                if b >= 2:
                    sp.wait_ge(qb_used, b - 1)
                sp.dma_start(qb[:, b % 2, :], q_rows[b, :].partition_broadcast(P)).then_inc(qb_in[b % 2], 16)
                if b == 1:
                    for j in (4, 5):
                        sp.dma_start(kcache[j], ck[:, j]).then_inc(kc_in[j - 4], 16)
                if b in (2, 3):
                    sp.dma_start(kcache[b + 4], ck[:, b + 4]).then_inc(kc_in[b], 16)
                if b >= 4:
                    sp.dma_start(vc[b - 4], cv[:, b - 4]).then_inc(v_in[1], 16)
            sp.wait_ge(qb_used, DEC)
            sp.dma_start(view(regB, 0, KD, D), xa_wo.rearrange("o (k p) n -> p (o k) n", p=P)).then_inc(wo_in, 16)
            sp.wait_ge(made, J.no["oS"] + 1)
            sp.dma_start(rw, router_w.rearrange("o (k p) e -> p (o k) e", p=P)).then_inc(rw_in, 16)
            sp.dma_start(rbias, router_bias[0].partition_broadcast(P)).then_inc(rw_in, 16)
            sp.dma_start(sgw, sh_w_gate.rearrange("o (k p) f -> p (o k) f", p=P)).then_inc(sh_in, 16)
            sp.dma_start(suw, sh_w_up.rearrange("o (k p) f -> p (o k) f", p=P)).then_inc(sh_in, 16)
            sp.dma_start(sdw, sh_w_down.rearrange("o (k p) d -> p (o k) d", p=P)).then_inc(sh_in, 16)
            eg = exp_w_gate.rearrange("o e (p k) f -> (o e) p (k f)", p=P)
            eu = exp_w_up.rearrange("o e (p k) f -> (o e) p (k f)", p=P)
            ed = exp_w_down.rearrange("o e (p k) d -> (o e) p k d", p=P)
            for e in range(RING):
                if e == 1:
                    sp.wait_ge(made, J.no[("x2", KD - 1)] + 1)
                if e == RING - 1:
                    break
                sp.dma_start(WG[e][:, 0:1, :], eg[e:e + 1].rearrange("e p n -> p e n")).then_inc(wg_in[e], 16)
                sp.dma_start(WG[e][:, 1:2, :], eu[e:e + 1].rearrange("e p n -> p e n")).then_inc(wg_in[e], 16)
                sp.dma_start(WD[e][:, :, :], ed[e:e + 1].rearrange("e p k d -> p (e k) d")).then_inc(wd_in[e], 16)
            for t, (t0, n) in enumerate(TILES):
                J.wait_taken(sp, ("hR", t))
                sp.dma_start(h_rows[t0:t0 + n, :], rows[0:n, t, :]).then_inc(h_stored, 16)

            sp.wait_ge(made, J.no[("su", KF - 1)] + 1)
            e = RING - 1
            sp.dma_start(WG[e][:, 0:1, :], eg[e:e + 1].rearrange("e p n -> p e n")).then_inc(wg_in[e], 16)
            sp.dma_start(WG[e][:, 1:2, :], eu[e:e + 1].rearrange("e p n -> p e n")).then_inc(wg_in[e], 16)
            sp.dma_start(WD[e][:, :, :], ed[e:e + 1].rearrange("e p k d -> p (e k) d")).then_inc(wd_in[e], 16)
            sp.wait_ge(row_table, 1)
            n_turns = turns(sp)

            def load(r, b):
                e = sp.value_load(ET[0:1, bass.ds(b, 1)].bitcast(I32), min_val=0, max_val=NE - 1)
                sp.wait_ge(gu_made, b + 1)
                sp.dma_start(WG[r][:, 0:1, :], eg[bass.ds(e, 1)].rearrange("e p n -> p e n")).then_inc(wg_in[r], 16)
                sp.dma_start(WG[r][:, 1:2, :], eu[bass.ds(e, 1)].rearrange("e p n -> p e n")).then_inc(wg_in[r], 16)
                sp.wait_ge(down_made, b + 1)
                sp.dma_start(WD[r][:, :, :], ed[bass.ds(e, 1)].rearrange("e p k d -> p (e k) d")).then_inc(wd_in[r], 16)

            with sp.Fori(1, n_turns) as i:
                for j in range(RING):
                    load(j, i * RING + j)
            sp.wait_ge(made, J.no[("sd", NTT - 1)] + 1)
            sp.dma_start(gfin, norm_final.partition_broadcast(P)).then_inc(fin_g, 16)
            sp.wait_ge(sums_landed, n_turns * (RING * 16) + 16 * NTT)
            for t, (t0, n) in enumerate(TILES):
                sp.dma_start(yf[0:n, t, :], acc_rows[t0:t0 + n, :]).then_inc(fin_in[t], 16)
            for t, (t0, n) in enumerate(TILES):
                sp.wait_ge(fin_y, t + 1)
                dst = y_prompt[0, t0:t0 + n, :] if t < TT else y_sample.rearrange("b o d -> b (o d)")
                sp.dma_start(dst, yf[0:n, t, :]).then_inc(stored, 16)
            sp.wait_ge(stored, 16 * 13)

        @block.gpsimd
        def _(pool):
            c = Count()

            def step(ins):
                pool.wait_ge(*c.add(ins, pool_step))

            step(pool.memset(small[:, :], 0.0))
            pool.memset(eps_c, EPS).then_inc(consts, 1)
            step(pool.memset(ident[:, :], 0.0))
            pool.affine_select(out=ident[:, :], in_=ident[:, :], compare_op=ALU.not_equal, fill=1.0, base=0,
                               pattern=[[-1, P]], channel_multiplier=1).then_inc(consts, 1)
            pool.memset(ones[:, :], 1.0).then_inc(consts, 1)
            pool.dma_start(rawP[0:DEC * PBUF, :], state_pool.rearrange("o b r c -> (o b r) c")).then_inc(states_in, 16)
            pool.dma_start(rawC[0:DEC * CBUF, :], state_conv.rearrange("o b r c -> (o b r) c")).then_inc(states_in, 16)
            pool.dma_start(rawH[0:DEC, :], state_h[0]).then_inc(states_in, 16)
            pool.iota(r15, pattern=[[1, 16]], base=1, channel_multiplier=0,
                      allow_small_or_imprecise_dtypes=True).then_inc(consts, 1)
            pool.memset(bdw, 0.0).then_inc(bd_zero, 1)

            for g, w in enumerate(WINDOWS):
                J.wait_taken(pool, ("z", g))
                if g == 0:
                    pool.wait_ge(made, J.no[("z", 3)] + 1)
                src, have, n = uP[:, g, 0:PBUF + SEQ], 1, 0
                while have < w:
                    last = 2 * have == w
                    lo = PBUF if last else 2 * have - 1
                    out = dT[:, g, 0:SEQ] if last else ptmp[n % 2][:, lo:PBUF + SEQ]
                    ins = pool.tensor_tensor(out, src[:, lo:PBUF + SEQ], src[:, lo - have:PBUF + SEQ - have], ALU.add)
                    if last:
                        ins.then_inc(pooled, 1)
                        pool.wait_ge(pooled, g + 1)
                    else:
                        step(ins)
                    src, have, n = ptmp[n % 2], 2 * have, n + 1
            for sq, before in ((sqP, 0), (rT, KP)):
                for k in range(1, KP):
                    pool.wait_ge(squares, before + k + 1)
                    if k > 1:
                        pool.wait_ge(group_added, (KP - 1) * (before // KP) + k - 1)
                    pool.tensor_tensor(sq[:, 0, :], sq[:, 0, :], sq[:, k, :], ALU.add).then_inc(group_added, 1)
            pool.wait_ge(ss_done, 4)
            step(pool.memset(valid, 1.0))
            step(pool.memset(low, 1.0))
            pool.affine_select(out=valid[:, TT:TT + 1], in_=valid[:, TT:TT + 1], compare_op=ALU.is_gt, fill=0.0,
                               base=DEC, pattern=[[0, 1]], channel_multiplier=-1).then_inc(consts, 1)
            pool.affine_select(out=low, in_=low, compare_op=ALU.is_gt, fill=0.0, base=0, pattern=[[1, P]],
                               channel_multiplier=-1).then_inc(consts, 1)
            step(pool.iota(expert3, pattern=[[0, 1]], base=0, channel_multiplier=1, allow_small_or_imprecise_dtypes=True))
            pool.affine_select(out=expert3, in_=expert3, compare_op=ALU.is_gt, fill=0.0, base=RING, pattern=[[0, 1]],
                               channel_multiplier=-1).then_inc(consts, 1)
            for out, pattern, base, up in ((first3, [[SLOTS, RING]], 1, 0), (iot8, [[1, NG]], 0, 0), (iotp, [[0, 1]], 0, 1), (j3, [[RING, 48]], 0, 0),
                                           (iots, [[1, SLOTS]], 0, 0), (whole[:, :, 0], [[P, NTT]], -FAR, 0),
                                           (whole[:, :, 1], [[0, NTT]], 0, 1)):
                pool.iota(out, pattern=pattern, base=base, channel_multiplier=up,
                          allow_small_or_imprecise_dtypes=True).then_inc(consts, 1)
            for j in range(PAIR):
                pool.memset(gath[j], 0.0).then_inc(consts, 1)

            pool.wait_ge(row_table, 1)
            pool.wait_ge(consts, 16)
            n_turns = turns(pool)
            limit = pool.to_reg(NT - 1)
            pool.wait_ge(h_stored, 16 * NTT)

            def gather(g, r, b):
                pool.wait_ge(turned, b + (1 + RING - PAIR))
                pool.wait_ge(idx_ready, b + 1)
                pool.sem_inc(clear, 1)
                pool.indirect_dma_start(gath[g][0:SLOTS, :], None, h_rows,
                                        bass.IndirectOffsetOnAxis(ap=idx[0:SLOTS, r:r + 1].bitcast(U32), axis=0),
                                        bounds_check=limit, oob_is_err=False).then_inc(gath_in[g], 16)

            def scatter(r, b):
                pool.wait_ge(sidx_ready, b + 1)
                pool.wait_ge(down_a, b + 2)
                pool.wait_ge(down_d, b + 2)
                pool.wait_ge(sums_landed, b * 16 + 16 * NTT)
                pool.sem_inc(rows_left, 1)
                pool.sem_inc(clear, 1)
                pool.indirect_dma_start(acc_rows, bass.IndirectOffsetOnAxis(ap=sidx[0:SLOTS, r:r + 1].bitcast(U32), axis=0),
                                        yX[r][0:SLOTS, :], None, bounds_check=limit, oob_is_err=False,
                                        compute_op=ALU.add).then_inc(sums_landed, 16)

            for b in range(PAIR):
                gather(b, b, b)
            for t, (t0, n) in enumerate(TILES):
                if t == NTT - 1:
                    gather(0, PAIR, PAIR)
                J.wait_taken(pool, ("sd", t))
                pool.dma_start(acc_rows[t0:t0 + n, :], rows[0:n, t, :]).then_inc(sums_landed, 16)
            pool.wait_ge(sums_landed, 16 * NTT)
            pool.sem_inc(rows_left, RING - 1)

            def step_of_block(i, j):
                b = i * RING + j
                gather(j % PAIR, (j + 2) % RING, b + 2)
                scatter((j - 1) % RING, b - 1)

            for j in range(1, RING):
                step_of_block(0, j)
            with pool.Fori(1, n_turns) as i:
                for j in range(RING):
                    step_of_block(i, j)
            scatter(RING - 1, n_turns * RING - 1)
            pool.wait_ge(sums_landed, n_turns * (RING * 16) + 16 * NTT)

        @block.scalar
        def _(a):
            c = Count()

            def rooted(width):
                n = c.n.get(id(root), 0)
                a.wait_ge(ss_done, n)
                a.wait_ge(inverse, n)
                c.add(a.activation(ssq, pS[:, 0, 0:5], ACT.Sqrt, bias=eps_c, scale=1.0 / width), root)

            def squared(out, x):
                c.add(a.activation(out, x, ACT.Square), squares)

            a.wait_ge(consts, 4)
            for t, (t0, n) in enumerate(TILES):
                a.wait_ge(x_in[t], 16)
                if t:
                    a.wait_ge(act_step, t)
                c.add(a.activation(xsq[0:n, :], xraw[0:n, t, :], ACT.Square, accum_out=ssq[0:n, t:t + 1]), act_step)
            a.wait_ge(act_step, NTT)
            c.add(a.activation(ssq, ssq, ACT.Sqrt, bias=eps_c, scale=1.0 / D), root)

            def cut_norm(tmp, before, first=0, tiles=KD):
                for k in range(tiles):
                    a.wait_ge(h_made, before + k + 1)
                    a.copy(h_hi[:, first + k, :], tmp[:, k % 2, :]).then_inc(h_hi_made, 1)

            Z.cut_hi(a, 0)
            Z.cut_hi(a, 1)
            cut_norm(htmp1, 0)
            Z.cut_hi(a, 2)
            a.wait_ge(padded, 1)
            for i in range(KP):
                Z.cut_hi(a, 2 * i + 3)
                Z.cut_hi(a, 2 * i + 4)
                p = J.wait_made(a, ("z", 4 + i))
                J.take(a.copy(halves(uR[:, i, CBUF:CBUF + NT]), pair[p][:, :, 0:HALF]), ("z", 4 + i))
            for i in range(KP):
                Z.cut_hi(a, 2 * (KP + i) + 3)
                Z.cut_hi(a, 2 * (KP + i) + 4)
                p = J.wait_made(a, ("z", 8 + i))
                J.take(a.activation(halves(gT[:, i, :]), pair[p][:, :, 0:HALF], ACT.Gelu_apprx_tanh), ("z", 8 + i))
                if i == 1:
                    a.wait_ge(mem_in, 16)
                    for t in range(MT):
                        c.add(a.activation(msq[:, t, :], mraw[:, t, :], ACT.Square, accum_out=mss[:, t:t + 1]), act_step)
                    a.wait_ge(act_step, NTT + MT)
                    c.add(a.activation(mss, mss, ACT.Sqrt, bias=eps_c, scale=1.0 / D), mem_ss)
                    a.wait_ge(mem_inv, 1)
                    for t in range(MT):
                        c.add(a.activation(mraw[:, t, :], mraw[:, t, :], ACT.Copy, scale=mrs[:, t:t + 1]), mem_scaled)
            for i in range(KP):
                for what, out, bias in (("r", rT, "gate_a_b"), ("i", iT, "gate_x_b")):
                    p = J.wait_made(a, (what, i))
                    J.take(a.activation(halves(out[:, i, :]), pair[p][:, :, 0:HALF], ACT.Sigmoid,
                                        bias=par[:, COL[bias] + i:COL[bias] + i + 1]), (what, i))
            a.wait_ge(sp_in, 1)
            c.add(a.activation(spt[:, 12:16], spt[:, 4:8], ACT.Exp), sp_exp)
            for q in range(2):
                p = J.wait_made(a, ("mT", q))
                for j in range(4):
                    k = 4 * q + j
                    cl = COL["norm_mem"] + k
                    ins = a.activation(mT[:, k, :], pair[p][:, j // 2, (j % 2) * NMEM:(j % 2 + 1) * NMEM], ACT.Copy,
                                       scale=par[:, cl:cl + 1])
                J.take(ins, ("mT", q))
            for g in range(KP):
                Z.cut_hi(a, 2 * (2 * KP + g) + 3)
                Z.cut_hi(a, 2 * (2 * KP + g) + 4)
                p = J.wait_made(a, ("z", g))
                J.take(a.copy(halves(uP[:, g, PBUF:PBUF + NT]), pair[p][:, :, 0:HALF]), ("z", g))
            p = J.wait_made(a, "st")
            a.copy(stO[0:CBUF + DEC, 0, :], pair[p][0:CBUF + DEC, 0, :])
            J.take(a.copy(stO[0:PBUF + DEC, 1, :], pair[p][0:PBUF + DEC, 1, :]), "st")
            a.wait_ge(conv_done, KP)
            a.wait_ge(sp_ready, 2)
            J.wait_taken(a, ("i", KP - 1))
            for i in range(KP):
                c.add(a.activation(aT[:, i, :], rT[:, i, :], ACT.Exp, scale=nsp[:, i:i + 1]), lru_a)
            for i in range(KP):
                c.add(a.activation(rT[:, i, :], rT[:, i, :], ACT.Tanh, scale=psp[:, i:i + 1]), lru_s)

            def take_kv(what, out, t):
                p = J.wait_made(a, (what, t))
                J.take(a.copy(out[:, t, :].rearrange("p (h n) -> p h n", h=2), pair[p][:, :, :]), (what, t))

            def take_kt(q):
                p = J.wait_made(a, ("KT", q))
                J.take(a.copy(KT[:, 4 * q:4 * q + 4, :].rearrange("p (h k) n -> p h (k n)", h=2), pair[p][:, :, :]), ("KT", q))

            take_kv("K", Kt, 0)
            for i in range(KP):
                a.wait_ge(lru_m2, i + 1)
                c.add(a.activation(rT[:, i, :], rT[:, i, :], ACT.Sqrt), lru_m)
            take_kv("K", Kt, 1)
            for g in range(KP):
                p = J.wait_made(a, ("yp", g))
                cl = COL["pool_scale"] + g
                J.take(a.activation(halves(dT[:, g, :]), pair[p][:, :, 0:HALF], ACT.Copy, scale=par[:, cl:cl + 1]), ("yp", g))
            for g in range(KP):
                J.wait_taken(a, ("yp", g))
                squared(sqP[:, g, :], dT[:, g, :])
            for i in range(KP):
                a.wait_ge(y_rnn, i + 1)
                squared(rT[:, i, :], gT[:, i, :])
            take_kv("V", Vt, 0)
            rooted(DP)
            take_kt(0)
            a.wait_ge(stored, 16 * 6)
            O.cut_hi(a, 0)
            O.cut_hi(a, 1)
            cut_norm(ytmp, KD, 0, KP)
            rooted(DP)
            take_kt(1)
            O.cut_hi(a, 2)
            take_kv("V", Vt, 1)
            cut_norm(ytmp, KD + KP, KP, KP)
            p = J.wait_made(a, "hl")
            J.take(a.copy(hlO[0:1 + DEC, :], pair[p][0:1 + DEC, 0, :]), "hl")
            for m in range(KD):
                O.cut_hi(a, 2 * m + 3)
                O.cut_hi(a, 2 * m + 4)
                J.wait_taken(a, ("x1", m))
                squared(sqT[:, m, :], xT[:, m, :])
            rooted(D)
            for u in range(2):
                Q.cut_hi(a, u)
            cut_norm(htmp2, 2 * KD)
            Q.cut_hi(a, 2)
            for m in range(KD):
                Q.cut_hi(a, 2 * m + 3)
                Q.cut_hi(a, 2 * m + 4)
                p = J.wait_made(a, ("q", m))
                J.take(a.copy(halves(qT[:, m, :]), pair[p][:, :, 0:HALF]), ("q", m))
            p = J.wait_made(a, "qs")
            J.take(a.copy(qsr[0:DEC, :].rearrange("p (h n) -> p h n", h=2), pair[p][0:DEC, :, :]), "qs")
            nb = DEC * HEADS
            a.wait_ge(stored, 16 * 8)

            def out(h, cc):
                q = J.wait_made(a, ("o", h, cc))
                J.take(a.copy(oT[:, 2 * h + cc, 0:SEQ], bank[q]), ("o", h, cc))

            for n in range(len(STEPS) + BEHIND):
                if n < len(STEPS):
                    q = J.wait_made(a, ("s", *STEPS[n]))
                    r = n % 4
                    a.wait_ge(att_max, n + 1)
                    if n >= 4:
                        a.wait_ge(made, J.no[("pT", *STEPS[n - 4])] + 1)
                    J.take(a.activation(pr[:, r, :], bank[q][:, 0:NMEM], ACT.Exp, bias=nmax[:, r:r + 1],
                                        scale=SCALE, accum_out=asum[:, r:r + 1]), ("s", *STEPS[n]))
                if 1 <= n <= len(STEPS):
                    r = (n - 1) % 4
                    a.wait_ge(att_inv, n)
                    c.add(a.activation(pr[:, r, :], pr[:, r, :], ACT.Copy, scale=rsum[:, r:r + 1]), att_norm)
                if n >= BEHIND:
                    h, t = STEPS[n - BEHIND]
                    if (h, t) == (1, 0):
                        a.wait_ge(q_stored, 16)
                    q = J.wait_made(a, ("pT", h, t))
                    J.take(a.copy(PT[:, h % 2, :, t * P:(t + 1) * P],
                                  bank[q][:, 0:NMEM].rearrange("p (m n) -> p m n", m=MT)), ("pT", h, t))
                    if h and t % 2:
                        out(h - 1, t // 2)
            out(HEADS - 1, 0)
            q = J.wait_made(a, "sS")
            a.wait_ge(s_max, 1)
            J.take(a.activation(pSm[0:nb, :], bank[q][0:nb, 0:NMEM], ACT.Exp, bias=snm[0:nb, :], scale=SCALE,
                                accum_out=sss[0:nb, :]), "sS")
            out(HEADS - 1, 1)
            q = J.wait_made(a, "pS")
            J.take(a.copy(pad8[:, :, 0:DEC * DEC:DEC + 1], bank[q][:, 0:MT * nb].rearrange("p (g b) -> p g b", b=DEC)), "pS")
            a.wait_ge(qb_used, DEC)
            J.wait_taken(a, ("o", HEADS - 1, 1))
            for k in range(KD):
                a.copy(o_hi[:, k, 0:SEQ], oT[:, k, 0:SEQ]).then_inc(o_hi_made, 1)
            for u in range(3):
                X.cut_hi(a, u)
            p = J.wait_made(a, "oS")
            J.take(a.copy(oSr[0:DEC, :].rearrange("p (h n) -> p h n", h=2), pair[p][0:DEC, :, :]), "oS")
            q = J.wait_made(a, "oST")
            J.take(a.copy(oT[:, :, SEQ:NT], bank[q][:, 0:KD * DEC].rearrange("p (k b) -> p k b", k=KD)), "oST")
            J.wait_taken(a, "oST")
            a.copy(o_hi[:, :, SEQ:NT], oT[:, :, SEQ:NT]).then_inc(o_hi_made, 1)
            for m in range(KD):
                X.cut_hi(a, 2 * m + 3)
                X.cut_hi(a, 2 * m + 4)
                J.wait_taken(a, ("x2", m))
                squared(sqU[:, m, :], xT[:, m, :])
            rooted(D)
            p = J.wait_made(a, "rt")
            a.wait_ge(sco_ones, 1)
            a.activation(sco[:, 0:TT, :], pair[p][:, 0, 0:TT * NE].rearrange("p (t e) -> p t e", t=TT), ACT.Sigmoid)
            J.take(a.activation(sco[0:DEC, TT, :], pair[p][0:DEC, 0, TT * NE:NTT * NE], ACT.Sigmoid), "rt")
            for t, (t0, n) in enumerate(TILES):
                p = J.wait_made(a, ("hR", t))
                J.take(a.copy(rows[0:n, t, :].rearrange("p (h n) -> p h n", h=2), pair[p][0:n, :, :]), ("hR", t))
            for m in range(KF):
                p = J.wait_made(a, ("sg", m))
                J.take(a.activation(halves(sA[:, m, :]), pair[p][:, :, 0:HALF], ACT.Silu), ("sg", m))
            a.wait_ge(h_stored, 16 * NTT)

            def start_sums(t):
                n = TILES[t][1]
                p = J.wait_made(a, ("sd", t))
                J.take(a.copy(rows[0:n, t, :].rearrange("p (h n) -> p h n", h=2), pair[p][0:n, :, :]), ("sd", t))

            for t in range(4):
                start_sums(t)

            a.wait_ge(row_table, 1)
            n_turns = turns(a)
            a.sem_inc(down_a, 1)

            def silu(b, first=False):
                a.wait_ge(gu_made, b + (1 + RING))
                if not first:
                    a.wait_ge(act_b, b)
                a.activation(sil[0:SLOTS, :], pair[0][0:SLOTS, 0, 0:FE], ACT.Silu).then_inc(silu_b, 1)

            def turn(b):
                a.wait_ge(turned, b + (1 + RING))
                a.copy(hX[:, 0:4, :].rearrange("p k n -> p (k n)"), pair[1][:, 0, 0:4 * SLOTS]).then_inc(turned_a, 1)

            def at(b):
                a.wait_ge(at_made, b + 1)
                a.wait_ge(down_made, b + RING)
                a.copy(act_parts[:, 0].rearrange("p k n -> p (k n)"), pair[0][:, 1, 0:KF * SLOTS]).then_inc(at_hi, 1)

            def cut_down(r, b, q):
                a.wait_ge(wd_in[r], q * 16 + 16)
                a.wait_ge(down_made, b + (1 + RING - PAIR))
                a.copy(down_parts[r % PAIR][:, 0], WD[r]).then_inc(wd_hi, 1)

            def down(r, b):
                a.wait_ge(down_made, b + (1 + RING))
                a.wait_ge(sidx_ready, b + 1)
                a.activation(yX[r][0:SLOTS, 0:512], pair[2][0:SLOTS, 0, :], ACT.Copy, scale=swl[0:SLOTS, r:r + 1]).then_inc(down_a, 1)

            turn(0)
            silu(0, first=True)
            cut_down(0, 0, 0)
            start_sums(4)
            turn(1)

            def step_of_block(i, j):
                b = i * RING + j
                at(b - 1)
                cut_down(j, b, i)
                silu(b)
                turn(b + 1)
                down((j - 1) % RING, b - 1)

            for j in range(1, RING):
                step_of_block(0, j)
            with a.Fori(1, n_turns) as i:
                for j in range(RING):
                    step_of_block(i, j)
            at(n_turns * RING - 1)
            down(RING - 1, n_turns * RING - 1)

            for t, (t0, n) in enumerate(TILES):
                a.wait_ge(fin_in[t], 16)
                a.activation(junk[0:n, :], yf[0:n, t, :], ACT.Square, accum_out=fin[0:n, t:t + 1]).then_inc(fin_ss, 1)
                a.wait_ge(fin_ss, t + 1)
                a.activation(fin[0:n, 5 + t:6 + t], fin[0:n, t:t + 1], ACT.Sqrt, bias=eps_c[0:n, :], scale=1.0 / D).then_inc(fin_root, 1)

        @block.vector
        def _(v):
            c = Count()

            def mark(ins):
                return c.add(ins, dve_step)

            def step(ins):
                v.wait_ge(*mark(ins))

            def inverted():
                n = c.n.get(id(inverse), 0)
                v.wait_ge(root, n + 1)
                c.add(v.reciprocal(rs, ssq), inverse)

            def apply(nb, src, dst, gain, tiles):
                p = J.wait_made(v, nb)
                for k in range(tiles):
                    ins = v.scalar_tensor_tensor(halves(dst[:, k, :]), halves(src[:, k, :]),
                                                 par[:, COL[gain] + k:COL[gain] + k + 1],
                                                 pair[p][:, :, 0:HALF], ALU.mult, ALU.mult)
                    if k < tiles - 1:
                        c.add(ins, normed)
                    else:
                        J.take(ins, nb)

            def apply_split(nb, src, tmp, lo, gain, before, first=0, tiles=KD):
                p = J.wait_made(v, nb)

                def leave(k):
                    v.wait_ge(h_hi_made, before + k + 1)
                    v.tensor_tensor(lo[:, first + k, :], tmp[:, k % 2, :], h_hi[:, first + k, :].bitcast(F32),
                                    ALU.subtract).then_inc(h_lo_made, 1)

                for k in range(tiles):
                    if k >= 2:
                        v.wait_ge(h_lo_made, before + k - 1)
                    ins = v.scalar_tensor_tensor(halves(tmp[:, k % 2, :]), halves(src[:, k, :]),
                                                 par[:, COL[gain] + k:COL[gain] + k + 1],
                                                 pair[p][:, :, 0:HALF], ALU.mult, ALU.mult).then_inc(h_made, 1)
                    if k:
                        leave(k - 1)
                leave(tiles - 1)
                v.wait_ge(h_made, before + tiles)
                J.take(v.tensor_copy(small[:, 100:101], small[:, 101:102]), nb)

            for t, (t0, n) in enumerate(TILES):
                p = J.wait_made(v, ("xT", t))
                J.take(v.tensor_copy(xT[:, :, t0:t0 + n].rearrange("p (h k) n -> p h k n", h=2),
                                     pair[p][:, :, 0:4 * n].rearrange("p h (k n) -> p h k n", k=4)), ("xT", t))
            p = J.wait_made(v, "par")
            J.take(v.tensor_copy(par[:, :], pair[p][:, 0, 0:NROWS]), "par")
            v.memset(uP[:, :, 0:PBUF], 0.0)
            c.add(v.memset(uR[:, :, 0:CBUF], 0.0), padded)
            inverted()
            J.wait_taken(v, "par")
            Z.cut_lo(v, 0)
            Z.cut_lo(v, 1)
            apply_split("nb1", xT, htmp1, h1_lo, "norm_mix", 0)
            Z.cut_lo(v, 2)
            p = J.wait_made(v, "sta")
            v.tensor_copy(stP.rearrange("p k b r -> p (k b r)"), pair[p][:, 0, 0:480])
            J.take(v.tensor_copy(view(regL, 13032, 128), pair[p][:, 1, 0:128]), "sta")
            def softplus():
                lam = par[:, COL["lru_lambda"]:COL["lru_lambda"] + 4]
                v.wait_ge(consts, 4)
                sp4 = lambda j: spt[:, 4 * j:4 * j + 4]
                step(v.tensor_scalar(sp4(0), lam, -1.0, None, ALU.mult))
                v.tensor_tensor(sp4(1), sp4(0), lam, ALU.min)
                c.add(v.tensor_scalar(sp4(2), sp4(0), 0.0, None, ALU.max), sp_in)
                v.wait_ge(sp_exp, 1)
                step(v.tensor_scalar(sp4(4), sp4(3), 2.0, None, ALU.add))
                step(v.reciprocal(sp4(5), sp4(4)))
                step(v.tensor_tensor(sp4(6), sp4(3), sp4(5), ALU.mult))
                step(v.tensor_tensor(sp4(7), sp4(6), sp4(6), ALU.mult))
                step(v.tensor_scalar(sp4(8), sp4(7), 1.0 / 17, 1.0 / 15, ALU.mult, ALU.add))
                for k in (13, 11, 9, 7, 5, 3, 1):
                    step(v.tensor_tensor(sp4(8), sp4(8), sp4(7), ALU.mult))
                    step(v.tensor_scalar(sp4(8), sp4(8), 1.0 / k, None, ALU.add))
                step(v.tensor_tensor(sp4(8), sp4(8), sp4(6), ALU.mult))
                step(v.scalar_tensor_tensor(sp4(8), sp4(8), 2.0, sp4(2), ALU.mult, ALU.add))
                c.add(v.tensor_scalar(nsp, sp4(8), -LRU_C, None, ALU.mult), sp_ready)
                c.add(v.tensor_scalar(psp, sp4(8), LRU_C, None, ALU.mult), sp_ready)
                step(v.reciprocal(r15, r15))

            wcol = lambda k, i: par[:, COL["conv_w"] + 4 * k + i:COL["conv_w"] + 4 * k + i + 1]
            bcol = lambda i: par[:, COL["conv_b"] + i:COL["conv_b"] + i + 1]
            def conv(i):
                J.wait_taken(v, ("z", 4 + i))
                u = uR[:, i, :]
                v.tensor_scalar(cT[:, i, SEQ:NT], u[:, CBUF + SEQ:CBUF + NT], wcol(3, i), bcol(i), ALU.mult, ALU.add)
                step(v.tensor_scalar(cT[:, i, 0:SEQ], u[:, 0:SEQ], wcol(0, i), bcol(i), ALU.mult, ALU.add))
                for k in range(1, 4):
                    v.scalar_tensor_tensor(cT[:, i, SEQ:NT], stC[:, i, :, k - 1], wcol(k - 1, i), cT[:, i, SEQ:NT],
                                           ALU.mult, ALU.add)
                    ins = v.scalar_tensor_tensor(cT[:, i, 0:SEQ], u[:, k:k + SEQ], wcol(k, i), cT[:, i, 0:SEQ],
                                                 ALU.mult, ALU.add)
                    if k < 3:
                        step(ins)
                    else:
                        c.add(ins, conv_done)

            for n in range(len(z_order)):
                Z.cut_lo(v, 2 * n + 3)
                Z.cut_lo(v, 2 * n + 4)
                if 1 <= n <= KP:
                    conv(n - 1)
                if n == KP + 1:
                    v.wait_ge(mem_ss, 1)
                    c.add(v.reciprocal(mrs, mss), mem_inv)
                if n == 2 * KP - 1:
                    softplus()
            for g, w in enumerate(WINDOWS):
                v.wait_ge(pooled, g + 1)
                step(v.tensor_reduce(dT[:, g, SEQ:NT], stP[:, g, :, PBUF - w + 1:PBUF], AX.X, ALU.add))
                v.tensor_tensor(dT[:, g, SEQ:NT], dT[:, g, SEQ:NT], uP[:, g, PBUF + SEQ:PBUF + NT], ALU.add)
                step(v.scalar_tensor_tensor(dT[:, g, 0:w - 1], dT[:, g, 0:w - 1], float(w), r15[:, 0:w - 1],
                                            ALU.mult, ALU.mult))
                c.add(v.scalar_tensor_tensor(dT[:, g, :], dT[:, g, :], 1.0 / w, uP[:, g, PBUF:PBUF + NT],
                                             ALU.mult, ALU.subtract), d_ready)
            for i in range(KP):
                v.wait_ge(lru_a, i + 1)
                step(v.tensor_tensor(a2, aT[:, i, :], aT[:, i, :], ALU.mult))
                v.wait_ge(lru_s, i + 1)
                v.wait_ge(*c.add(v.scalar_tensor_tensor(rT[:, i, :], a2, 1.0, rT[:, i, :], ALU.add, ALU.mult), lru_m2))
            v.wait_ge(lru_m, KP)
            step(v.memset(rT[:, :, 0:1], 1.0))
            t0 = [mark(v.tensor_tensor(iT[:, i, :], iT[:, i, :], rT[:, i, :], ALU.mult)) for i in range(KP)]
            t1 = []
            for i in range(KP):
                v.wait_ge(*t0[i])
                t1.append(mark(v.tensor_tensor(iT[:, i, :], iT[:, i, :], cT[:, i, :], ALU.mult)))
            v.wait_ge(*t1[-1])
            t2 = mark(v.tensor_tensor(stH, aT[:, :, SEQ:NT], stH, ALU.mult))
            for i in range(KP):
                mark(v.tensor_tensor_scan(cT[:, i, 0:SEQ], aT[:, i, 0:SEQ], iT[:, i, 0:SEQ], 0.0, ALU.mult, ALU.add))
            v.wait_ge(*t2)
            step(v.tensor_tensor(cT[:, :, SEQ:NT], stH, iT[:, :, SEQ:NT], ALU.add))
            for i in range(KP):
                c.add(v.tensor_tensor(gT[:, i, :], cT[:, i, :], gT[:, i, :], ALU.mult), y_rnn)
            inverted()
            O.cut_lo(v, 0)
            O.cut_lo(v, 1)
            apply_split("nbp", dT, ytmp, y_lo, "norm_pool_out", KD, 0, KP)
            inverted()
            O.cut_lo(v, 2)
            v.wait_ge(h_lo_made, KD + KP)
            apply_split("nbr", gT, ytmp, y_lo, "norm_rnn_out", KD + KP, KP, KP)

            def residual(what, before):
                for m in range(KD):
                    W, sq = (O, sqT) if what == "x1" else (X, sqU)
                    W.cut_lo(v, 2 * m + 3)
                    W.cut_lo(v, 2 * m + 4)
                    if 2 <= m < KD:
                        v.wait_ge(squares, before + m)
                        v.wait_ge(sq_added, c.n.get(id(sq_added), 0)) if m > 2 else None
                        c.add(v.tensor_tensor(sq[:, 0, :], sq[:, 0, :], sq[:, m - 1, :], ALU.add), sq_added)
                    p = J.wait_made(v, (what, m))
                    J.take(v.tensor_tensor(halves(xT[:, m, :]), halves(xT[:, m, :]), pair[p][:, :, 0:HALF], ALU.add), (what, m))

            residual("x1", 2 * KP)
            inverted()
            Q.cut_lo(v, 0)
            Q.cut_lo(v, 1)
            apply_split("nb2", xT, htmp2, h2_lo, "norm_xattn", 2 * KD)
            Q.cut_lo(v, 2)
            for u in range(3, Q.units):
                Q.cut_lo(v, u)

            units = [(b, mt) for b in range(DEC) for mt in range(MT)]

            def scores(b, mt):
                if mt == 0:
                    v.wait_ge(qb_in[b % 2], 16 * (b // 2 + 1))
                    if b < 4:
                        v.wait_ge(kb_in, 64)
                    else:
                        v.wait_ge(kc_in[b - 4], 16)
                for h in range(HEADS):
                    kk = kcache[b][:, mt, h * HD:(h + 1) * HD]
                    ins = v.tensor_tensor_reduce(kk, kk, qb[:, b % 2, h * HD:(h + 1) * HD], 1.0, 0.0, ALU.mult, ALU.add,
                                                 sS[:, mt, h * DEC + b:h * DEC + b + 1])
                if mt == MT - 1:
                    ins.then_inc(qb_used, 1)

            v.wait_ge(stored, 16 * 8)
            v.memset(pad8, 0.0)
            for n in range(len(STEPS) + 1):
                if n < len(STEPS):
                    q = J.wait_made(v, ("s", *STEPS[n]))
                    r = n % 4
                    if n >= 4:
                        v.wait_ge(att_norm, n - 3)
                    step(v.tensor_reduce(amax[:, r:r + 1], bank[q][:, 0:NMEM], AX.X, ALU.max))
                    c.add(v.tensor_scalar(nmax[:, r:r + 1], amax[:, r:r + 1], -SCALE, None, ALU.mult), att_max)
                if n >= 1:
                    r = (n - 1) % 4
                    J.wait_taken(v, ("s", *STEPS[n - 1]))
                    c.add(v.reciprocal(rsum[:, r:r + 1], asum[:, r:r + 1]), att_inv)
                if n >= 2:
                    for u in range(n - 2, n - 1 if n < len(STEPS) else len(units)):
                        scores(*units[u])
            nb = DEC * HEADS
            q = J.wait_made(v, "sS")
            step(v.tensor_reduce(smx[0:nb, :], bank[q][0:nb, 0:NMEM], AX.X, ALU.max))
            c.add(v.tensor_scalar(snm[0:nb, :], smx[0:nb, :], -SCALE, None, ALU.mult), s_max)
            J.wait_taken(v, "sS")
            step(v.reciprocal(srs[0:nb, :], sss[0:nb, :]))
            c.add(v.tensor_scalar(pSm[0:nb, :], pSm[0:nb, :], srs[0:nb, :], None, ALU.mult), s_norm)
            for k in range(KD):
                v.wait_ge(o_hi_made, k + 1)
                v.tensor_tensor(o_lo[:, k, 0:SEQ], oT[:, k, 0:SEQ], o_hi[:, k, 0:SEQ].bitcast(F32), ALU.subtract).then_inc(o_lo_made, 1)
            for u in range(3):
                X.cut_lo(v, u)
            v.wait_ge(made, J.no["oS"] + 1)
            c.add(v.memset(sco, 1.0), sco_ones)
            v.wait_ge(o_hi_made, KD + 1)
            v.tensor_tensor(o_lo[:, :, SEQ:NT], oT[:, :, SEQ:NT], o_hi[:, :, SEQ:NT].bitcast(F32), ALU.subtract).then_inc(o_lo_made, 1)
            residual("x2", 2 * KP + KD)
            inverted()
            apply("nb3", xT, hT, "norm_ffn", KD)

            def onehot_(b):
                e = v.value_load(ET[0:1, bass.ds(b, 1)].bitcast(I32), min_val=0, max_val=NE - 1)
                v.tensor_tensor(oneh, iots.unsqueeze(1).to_broadcast((P, NTT, SLOTS)),
                                slot[:, :, bass.ds(e, 1)].to_broadcast((P, NTT, SLOTS)), ALU.is_equal)
                v.tensor_copy(rhsw[:, :, 3:6], wparts[:, :, :, bass.ds(e, 1)].rearrange("p c t e -> p t (c e)")).then_inc(onehot, 1)
                v.wait_ge(onehot, b + 1)
                v.tensor_scalar(iots, iots, float(SLOTS), None, ALU.add).then_inc(counted, 1)
                v.wait_ge(counted, b + 1)

            def slots(r, b):
                v.wait_ge(slots_made, b + 1)
                v.tensor_reduce(sums[0:SLOTS, r, :], pS[0:SLOTS, 0, 0:6].rearrange("p (s c) -> p s c", s=2), AX.X,
                                ALU.add).then_inc(summed, 1)
                v.wait_ge(summed, b + 1)
                v.tensor_scalar(idx[0:SLOTS, r:r + 1].bitcast(U32), sums[0:SLOTS, r, 0:1], float(FAR), None, ALU.add).then_inc(idx_ready, 1)

            J.wait_taken(v, "rt")
            v.wait_ge(rw_in, 32)
            v.wait_ge(consts, 16)
            over = lambda x, n: x.unsqueeze(1).to_broadcast((P, NTT, n))
            step(v.tensor_tensor(bia, sco, over(rbias, NE), ALU.add))
            for t in range(NTT):
                for g in range(NG):
                    ins = v.max(m8[:, t, g * 8:(g + 1) * 8], bia[:, t, g * EG:(g + 1) * EG])
            step(ins)
            m8v = m8.rearrange("p t (g j) -> p t g j", j=8)
            step(v.tensor_tensor(gs, m8v[:, :, :, 0], m8v[:, :, :, 1], ALU.add))
            for t in range(NTT):
                ins = v.max(g8[:, t, :], gs[:, t, :])
            step(ins)
            for t in range(NTT):
                ins = v.max_index(gi[:, t, :].bitcast(U32), g8[:, t, :], gs[:, t, :])
            step(ins)
            step(v.tensor_copy(gif, gi.bitcast(U32)))
            for j in range(TOPG):
                out = gmk if j == 0 else geq
                step(v.tensor_tensor(out, over(iot8, NG), gif[:, :, j:j + 1].to_broadcast((P, NTT, NG)), ALU.is_equal))
                if j:
                    step(v.tensor_tensor(gmk, gmk, geq, ALU.add))
            step(v.tensor_scalar(pen, gmk, -1.0, 1e30, ALU.add, ALU.mult))
            b4 = bia.rearrange("p t (g j) -> p t g j", j=EG)
            for t in range(NTT):
                ins = v.tensor_tensor(b4[:, t], b4[:, t], gmk[:, t, :].unsqueeze(2).to_broadcast((P, NG, EG)), ALU.mult)
            step(ins)
            for t in range(NTT):
                ins = v.tensor_tensor(b4[:, t], b4[:, t], pen[:, t, :].unsqueeze(2).to_broadcast((P, NG, EG)), ALU.add)
            step(ins)
            for t in range(NTT):
                ins = v.max(top[:, t, :], bia[:, t, :])
            step(ins)
            for t in range(NTT):
                ins = v.match_replace(mrep[:, t, :], top[:, t, :], bia[:, t, :], -3e38)
            step(ins)
            step(v.tensor_scalar(msk, mrep, -3e38, None, ALU.is_equal))
            step(v.tensor_tensor(gwt, msk, sco, ALU.mult))
            step(v.tensor_reduce(wsu, gwt, AX.X, ALU.add))
            step(v.reciprocal(wsu, wsu))
            step(v.tensor_scalar(wsu, wsu, ROUTED, None, ALU.mult))
            t0 = mark(v.tensor_tensor(gwt, gwt, wsu.unsqueeze(2).to_broadcast((P, NTT, NE)), ALU.mult))
            c.add(v.tensor_tensor(msk, msk, valid.unsqueeze(2).to_broadcast((P, NTT, NE)), ALU.mult), masked)
            for m in range(KF):
                p = J.wait_made(v, ("su", m))
                J.wait_taken(v, ("sg", m))
                J.take(v.tensor_tensor(halves(sA[:, m, :]), halves(sA[:, m, :]), pair[p][:, :, 0:HALF], ALU.mult), ("su", m))
            v.wait_ge(*t0)
            v.memset(rhsw[:, :, 2:3], 0.0)
            v.tensor_copy(rhsw[:, :, 0:2], whole)
            for j in range(3):
                step(v.tensor_copy(wparts[:, j], part if j else gwt))
                if j < 2:
                    step(v.tensor_tensor(part, part if j else gwt, wparts[:, j], ALU.subtract))
            p = J.wait_made(v, "pos")
            cnt = pair[p][:, 0, NTT * NE:(NTT + 1) * NE]
            step(v.tensor_scalar(nblk, cnt, 0.0, None, ALU.is_gt))
            step(v.memset(nblk[:, 0:RING], 0.0))
            for k in range(1, -(-NT // SLOTS)):
                step(v.scalar_tensor_tensor(nblk, cnt, float(SLOTS * k), nblk, ALU.is_gt, ALU.add))
            step(v.tensor_tensor_scan(bend, ones[:, 0:NE], nblk, float(RING), ALU.mult, ALU.add))
            step(v.tensor_tensor(bbase, bend, nblk, ALU.subtract))
            step(v.tensor_scalar(bbase, bbase, float(SLOTS), 1.0, ALU.mult, ALU.add))
            pos = pair[p][:, 0, 0:NTT * NE].rearrange("p (t e) -> p t e", t=NTT)
            step(v.tensor_tensor(slot, pos, over(bbase, NE), ALU.add))
            pos3 = pos[:, :, 0:RING]
            step(v.scalar_tensor_tensor(delta, bbase[:, 0:RING], -float(SLOTS), first3, ALU.add, ALU.subtract))
            step(v.scalar_tensor_tensor(later, pos3, float(SLOTS), over(delta, RING), ALU.is_ge, ALU.mult))
            step(v.tensor_tensor(later, later, over(first3, RING), ALU.add))
            J.take(v.tensor_tensor(slot[:, :, 0:RING], later, pos3, ALU.add), "pos")
            J.wait_taken(v, "pos")
            step(v.tensor_tensor(slot, slot, msk, ALU.mult))
            step(v.tensor_scalar(slot, slot, -1.0, None, ALU.add))
            step(v.tensor_scalar(cmp, bend, iotp, 0.0, ALU.is_le, ALU.add, accum_out=ebc[:, 0:1]))
            c.add(v.tensor_scalar(ebc[:, 0:1], ebc[:, 0:1], float(NE - 1), expert3, ALU.min, ALU.max), tab_ready)
            step(v.tensor_scalar(cmp[:, 0:48], j3, bend[:, NE - 1:NE], 0.0, ALU.is_lt, ALU.add, accum_out=cmp[:, 48:49]))
            step(v.tensor_copy(NI[:, 0:1].bitcast(I32), cmp[:, 48:49]))
            p = J.wait_made(v, "tab")
            J.take(v.tensor_copy(ET[0:1, :].bitcast(I32), pair[p][0:1, 0, 0:P]), "tab")
            J.wait_taken(v, "tab")
            c.add(v.tensor_copy(cmp[:, 49:50], cmp[:, 48:49]), row_table)
            v.wait_ge(row_table, 1)
            n_turns = turns(v)
            onehot_(0)
            for t in range(3):
                slots(t, t)
                onehot_(t + 1)

            v.sem_inc(down_d, 1)

            def keep(r, b):
                v.wait_ge(idx_ready, b + 1)
                v.wait_ge(rows_left, b + 1)
                v.tensor_copy(swl[0:SLOTS, r:r + 1], sums[0:SLOTS, r, 1:2])
                v.tensor_copy(sidx[0:SLOTS, r:r + 1].bitcast(U32), idx[0:SLOTS, r:r + 1].bitcast(U32)).then_inc(sidx_ready, 1)

            def turn(b):
                v.wait_ge(turned, b + (1 + RING))
                v.tensor_copy(hX[:, 4:8, :].rearrange("p k n -> p (k n)"), pair[1][:, 1, 0:4 * SLOTS]).then_inc(turned_d, 1)

            def gate(b, first=False):
                v.wait_ge(silu_b, b + 1)
                if not first:
                    v.wait_ge(at_made, b)
                v.tensor_tensor(act[0:SLOTS, :], sil[0:SLOTS, :], pair[0][0:SLOTS, 0, FE:2 * FE], ALU.mult).then_inc(act_b, 1)

            def leave(r, b):
                v.wait_ge(wd_hi, b + 1)
                v.tensor_tensor(down_parts[r % PAIR][:, 1], WD[r], down_parts[r % PAIR][:, 0].bitcast(F32), ALU.subtract).then_inc(wd_lo, 1)

            def at(b):
                v.wait_ge(at_hi, b + 1)
                v.tensor_tensor(act_parts[:, 1].rearrange("p k n -> p (k n)"), pair[0][:, 1, 0:KF * SLOTS],
                                act_parts[:, 0].bitcast(F32).rearrange("p k n -> p (k n)"), ALU.subtract).then_inc(at_taken, 1)

            def down(r, b):
                v.wait_ge(down_made, b + (1 + RING))
                v.wait_ge(sidx_ready, b + 1)
                v.tensor_scalar(yX[r][0:SLOTS, 512:D], pair[2][0:SLOTS, 1, :], swl[0:SLOTS, r:r + 1], None, ALU.mult).then_inc(down_d, 1)

            turn(0)
            gate(0, first=True)
            leave(0, 0)
            turn(1)

            def step_of_block(i, j):
                b = i * RING + j
                keep((j - 1) % RING, b - 1)
                v.wait_ge(sidx_ready, b)
                slots((j + 2) % RING, b + 2)
                onehot_(b + 3)
                at(b - 1)
                leave(j, b)
                gate(b)
                turn(b + 1)
                down((j - 1) % RING, b - 1)

            for j in range(1, RING):
                step_of_block(0, j)
            with v.Fori(1, n_turns) as i:
                for j in range(RING):
                    step_of_block(i, j)
            at(n_turns * RING - 1)
            keep(RING - 1, n_turns * RING - 1)
            down(RING - 1, n_turns * RING - 1)

            v.wait_ge(fin_g, 16)
            for t, (t0_, n) in enumerate(TILES):
                v.wait_ge(fin_root, t + 1)
                v.reciprocal(fin[0:n, 10 + t:11 + t], fin[0:n, 5 + t:6 + t]).then_inc(fin_inv, 1)
                v.wait_ge(fin_inv, t + 1)
                v.scalar_tensor_tensor(yf[0:n, t, :], yf[0:n, t, :], fin[0:n, 10 + t:11 + t], gfin[0:n, :],
                                       ALU.mult, ALU.mult).then_inc(fin_y, 1)

        @block.tensor
        def _(pe):
            seen = {"squares": 0, "norms": 1}

            def project(name, weights, acts, ks, ready=None):
                p = J.begin(pe, name)
                for k in ks:
                    if ready:
                        ready(k)
                    for h in range(2):
                        ins = pe.matmul(pair[p][:, h, 0:HALF], weights(k), acts(k)[:, h * HALF:(h + 1) * HALF],
                                        start=k == ks[0], stop=k == ks[-1])
                J.made_by(ins)

            def sum_squares(k, sq, first, last, ready=None):
                if not ready:
                    seen["squares"] += 1
                if first:
                    pe.wait_ge(root, seen["norms"])
                    seen["norms"] += 1
                    pe.matmul(pS[:, 0, 0:NTT], ones[:, :], zero5, start=True, stop=False, skip_group_check=True)
                pe.wait_ge(*(ready or (squares, seen["squares"])))
                for t, (t0, n) in enumerate(TILES):
                    ins = pe.matmul(pS[0:n, 0, t:t + 1], sq[:, k, t0:t0 + n], ones[:, 0:1], start=False,
                                    stop=last and t == NTT - 1, skip_group_check=True)
                if last:
                    ins.then_inc(ss_done, 1)

            def spread(name):
                p = J.begin(pe, name)
                pe.wait_ge(inverse, seen["norms"])
                for lo, hi, t in ((0, 128, 0), (128, 256, 1), (256, 260, 2), (260, 384, 2), (384, 512, 3), (512, 520, 4)):
                    h, t0 = lo // HALF, t * P
                    ins = pe.matmul(pair[p][:, h, lo - h * HALF:hi - h * HALF], rs[:, t:t + 1].to_broadcast((P, P)),
                                    ident[:, lo - t0:hi - t0], start=True, stop=True)
                J.made_by(ins)

            def normed_tiles(base, nb, tiles):
                def ready(k):
                    if k < tiles - 1:
                        pe.wait_ge(normed, base + k + 1)
                    else:
                        J.wait_taken(pe, nb)
                return ready

            pe.sem_inc(gu_made, RING)
            pe.sem_inc(down_made, RING)
            pe.sem_inc(turned, RING)
            pe.wait_ge(consts, 4)
            for t, (t0, n) in enumerate(TILES):
                p = J.begin(pe, ("xT", t))
                pe.wait_ge(x_in[t], 16)
                for k in range(KD):
                    ins = pe.transpose(pair[p][:, k // 4, (k % 4) * n:(k % 4 + 1) * n], xraw[0:n, t, k * P:(k + 1) * P], ident[0:n, 0:n])
                J.made_by(ins)
            pe.wait_ge(rows_in, 16 * 12)
            p = J.begin(pe, "par")
            J.made_by(pe.transpose(pair[p][:, 0, 0:NROWS], rawR[0:NROWS, :], ident[0:NROWS, 0:NROWS]))
            spread("nb1")
            pe.wait_ge(states_in, 16 * 3)
            p = J.begin(pe, "sta")
            for k in range(KP):
                ks = slice(k * P, (k + 1) * P)
                n = DEC * PBUF
                pe.transpose(pair[p][:, 0, k * n:(k + 1) * n], rawP[0:n, ks], ident[0:n, 0:n])
                n = DEC * CBUF
                pe.transpose(pair[p][:, 1, k * n:(k + 1) * n], rawC[0:n, ks], ident[0:n, 0:n])
                ins = pe.transpose(pair[p][:, 1, 96 + k * DEC:96 + (k + 1) * DEC], rawH[0:DEC, ks], ident[0:DEC, 0:DEC])
            J.made_by(ins)
            for n in range(2 * KP):
                Z.product(pe, pair, n, h_hi, h1_lo, (lambda k: pe.wait_ge(h_lo_made, k + 1)) if n == 0 else None)
            pe.wait_ge(bd_in, 16 * 4)
            for i in range(KP):
                pe.wait_ge(conv_done, i + 1)
                for s, what in enumerate("ri"):
                    project((what, i), lambda k: bdw[:, s, i, :], lambda k: cT[:, i, :], range(1))
            pe.wait_ge(mem_scaled, MT)
            for q in range(2):
                p = J.begin(pe, ("mT", q))
                for j in range(4):
                    for t in range(MT):
                        k = 4 * q + j
                        ins = pe.transpose(pair[p][:, j // 2, (j % 2) * NMEM + t * P:(j % 2) * NMEM + (t + 1) * P],
                                           mraw[:, t, k * P:(k + 1) * P], ident[:, :])
                J.made_by(ins)
            for n in range(2 * KP, 3 * KP):
                Z.product(pe, pair, n, h_hi, h1_lo)
            p = J.begin(pe, "st")
            J.wait_taken(pe, ("z", 3))
            for i in range(KP):
                pe.transpose(pair[p][0:CBUF + DEC, 0, i * P:(i + 1) * P], uR[:, i, SEQ:CBUF + NT], ident[:, :])
                ins = pe.transpose(pair[p][0:PBUF + DEC, 1, i * P:(i + 1) * P], uP[:, i, SEQ:PBUF + NT], ident[:, :])
            J.made_by(ins)

            def kv(what, w, t):
                p = J.begin(pe, (what, t))
                for k in range(KD):
                    if what == "K" and t == 0:
                        J.wait_taken(pe, ("mT", k // 4))
                    for h in range(2):
                        ins = pe.matmul(pair[p][:, h, :], mT[:, k, t * P:(t + 1) * P], w[:, k, h * 512:(h + 1) * 512],
                                        start=k == 0, stop=k == KD - 1)
                J.made_by(ins)

            def turn_keys(q):
                p = J.begin(pe, ("KT", q))
                J.wait_taken(pe, ("K", 1))
                for j in range(4):
                    for t in range(MT):
                        k = 4 * q + j
                        ins = pe.transpose(pair[p][:, j // 2, (j % 2) * NMEM + t * P:(j % 2) * NMEM + (t + 1) * P],
                                           Kt[:, t, k * P:(k + 1) * P], ident[:, :])
                J.made_by(ins)

            pe.wait_ge(wk_in, 16)
            for t in range(MT):
                kv("K", wk_v, t)
            pe.wait_ge(plw_in, 16)
            for g in range(KP):
                pe.wait_ge(d_ready, g + 1)
                project(("yp", g), lambda k: plw[:, g, :], lambda k: dT[:, g, :], range(1))
            pe.wait_ge(wv_in, 16)
            kv("V", wv_v, 0)
            sum_squares(0, sqP, True, True, (group_added, KP - 1))
            turn_keys(0)
            spread("nbp")
            sum_squares(0, rT, True, True, (group_added, 2 * (KP - 1)))
            seen["squares"] += 2 * KP
            turn_keys(1)
            kv("V", wv_v, 1)
            spread("nbr")
            p = J.begin(pe, "hl")
            for i in range(KP):
                ins = pe.transpose(pair[p][0:1 + DEC, 0, i * P:(i + 1) * P], cT[:, i, SEQ - 1:NT], ident[:, :])
            J.made_by(ins)

            def into_residual(what, product):
                for m in range(KD):
                    product(m)
                added = KD - 2 if what == "x1" else 2 * (KD - 2)
                sq = sqT if what == "x1" else sqU
                sum_squares(0, sq, True, False, (sq_added, added))
                seen["squares"] += KD - 1
                sum_squares(KD - 1, sq, False, True)

            into_residual("x1", lambda m: O.product(pe, pair, m, h_hi, y_lo,
                                                    (lambda k: pe.wait_ge(h_lo_made, KD + k + 1)) if m == 0 else None))
            spread("nb2")
            for n in range(KD):
                Q.product(pe, pair, n, h_hi, h2_lo, (lambda k: pe.wait_ge(h_lo_made, 2 * KD + k + 1)) if n == 0 else None)
            p = J.begin(pe, "qs")
            for k in range(KD):
                J.wait_taken(pe, ("q", k))
                ins = pe.transpose(pair[p][0:DEC, k // 4, (k % 4) * P:(k % 4 + 1) * P], qT[:, k, SEQ:NT], ident[:, :])
            J.made_by(ins)
            nb = DEC * HEADS
            def out(h, cc):
                q = J.begin(pe, ("o", h, cc))
                J.wait_taken(pe, ("pT", h, TT - 1))
                for m in range(MT):
                    lo = h * HD + cc * P
                    ins = pe.matmul(bank[q], Vt[:, m, lo:lo + P], PT[:, h % 2, m, :], start=m == 0, stop=m == MT - 1)
                J.made_by(ins)

            for n in range(len(STEPS) + BEHIND):
                if n < len(STEPS):
                    h, t = STEPS[n]
                    q = J.begin(pe, ("s", h, t))
                    for k in range(2):
                        ins = pe.matmul(bank[q][:, 0:NMEM], qT[:, 2 * h + k, t * P:(t + 1) * P], KT[:, 2 * h + k, :],
                                        start=k == 0, stop=k == 1)
                    J.made_by(ins)
                if n >= BEHIND:
                    h, t = STEPS[n - BEHIND]
                    q = J.begin(pe, ("pT", h, t))
                    pe.wait_ge(att_norm, n - BEHIND + 1)
                    for m in range(MT):
                        ins = pe.transpose(bank[q][:, m * P:(m + 1) * P], pr[:, (n - BEHIND) % 4, m * P:(m + 1) * P], ident[:, :])
                    J.made_by(ins)
                    if h and t % 2:
                        out(h - 1, t // 2)
            out(HEADS - 1, 0)
            q = J.begin(pe, "sS")
            pe.wait_ge(qb_used, DEC)
            for m in range(MT):
                ins = pe.transpose(bank[q][0:nb, m * P:(m + 1) * P], sS[:, m, :], ident[:, :])
            J.made_by(ins)
            out(HEADS - 1, 1)
            q = J.begin(pe, "pS")
            pe.wait_ge(s_norm, 1)
            for m in range(MT):
                ins = pe.transpose(bank[q][:, m * nb:(m + 1) * nb], pSm[0:nb, m * P:(m + 1) * P], ident[0:nb, 0:nb])
            J.made_by(ins)
            p = J.begin(pe, "oS")
            J.wait_taken(pe, "pS")
            pe.wait_ge(v_in[0], 32)
            pe.wait_ge(v_in[1], 64)
            pe.wait_ge(v_in[2], 32)
            for h in range(HEADS):
                for b in range(DEC):
                    for m in range(MT):
                        ins = pe.matmul(pair[p][0:DEC, h // 2, h % 2 * HD:(h % 2 + 1) * HD],
                                        pad8[:, m * HEADS + h, b * DEC:(b + 1) * DEC], vc[b][:, m, h * HD:(h + 1) * HD],
                                        start=b == 0 and m == 0, stop=b == DEC - 1 and m == MT - 1)
            J.made_by(ins)
            q = J.begin(pe, "oST")
            J.wait_taken(pe, "oS")
            for k in range(KD):
                ins = pe.transpose(bank[q][:, k * DEC:(k + 1) * DEC], oSr[0:DEC, k * P:(k + 1) * P], ident[0:DEC, 0:DEC])
            J.made_by(ins)
            pe.wait_ge(o_lo_made, KD + 1)
            into_residual("x2", lambda m: X.product(pe, pair, m, o_hi, o_lo))
            spread("nb3")
            ready = normed_tiles(0, "nb3", KD)
            p = J.begin(pe, "rt")
            pe.wait_ge(rw_in, 32)
            for t, (t0, n) in enumerate(TILES):
                for k in range(KD):
                    ready(k)
                    ins = pe.matmul(pair[p][0:n, 0, t * NE:(t + 1) * NE], hT[:, k, t0:t0 + n], rw[:, k, :], start=k == 0, stop=k == KD - 1)
            J.made_by(ins)

            def rows_of(name, src, t0, n):
                p = J.begin(pe, name)
                for k in range(KD):
                    ins = pe.transpose(pair[p][0:n, k // 4, (k % 4) * P:(k % 4 + 1) * P], src[:, k, t0:t0 + n], ident[:, :])
                J.made_by(ins)

            for t, (t0, n) in enumerate(TILES):
                rows_of(("hR", t), hT, t0, n)
            pe.wait_ge(sh_in, 48)
            for m in range(KF):
                project(("sg", m), lambda k: sgw[:, k, m * P:(m + 1) * P], lambda k: hT[:, k, :], range(KD))
                project(("su", m), lambda k: suw[:, k, m * P:(m + 1) * P], lambda k: hT[:, k, :], range(KD))
            p = J.begin(pe, "pos")
            pe.wait_ge(masked, 1)
            for t in range(NTT):
                for s in range(t + 1):
                    pe.matmul(pair[p][:, 0, t * NE:(t + 1) * NE], low if s == t else ones[:, :], msk[:, s, :], start=s == 0, stop=s == t)
            for s in range(NTT):
                ins = pe.matmul(pair[p][:, 0, NTT * NE:(NTT + 1) * NE], ones[:, :], msk[:, s, :], start=s == 0, stop=s == NTT - 1)
            J.made_by(ins)

            def shared_down(t):
                t0, n = TILES[t]
                p = J.begin(pe, ("sd", t))
                for m in range(KF):
                    J.wait_taken(pe, ("su", m))
                    for h in range(2):
                        pe.matmul(pair[p][0:n, h, :], sA[:, m, t0:t0 + n], sdw[:, m, h * 512:(h + 1) * 512],
                                  start=m == 0, stop=False, skip_group_check=True)
                for k in range(KD):
                    ins = pe.matmul(pair[p][0:n, k // 4, (k % 4) * P:(k % 4 + 1) * P], xT[:, k, t0:t0 + n], ident[:, :],
                                    start=False, stop=k % 4 == 3, skip_group_check=True)
                J.made_by(ins)

            shared_down(0)
            shared_down(1)
            p = J.begin(pe, "tab")
            pe.wait_ge(tab_ready, 1)
            J.made_by(pe.transpose(pair[p][0:1, 0, 0:P], ebc[:, 0:1], ident[:, :]))

            def slots(b):
                pe.wait_ge(onehot, b + 1)
                for t in range(NTT):
                    ins = pe.matmul(pS[0:SLOTS, 0, 0:6], oneh[:, t, :], rhsw[:, t, :], start=t == 0, stop=t == NTT - 1)
                ins.then_inc(slots_made, 1)

            for t in range(3):
                if t:
                    pe.wait_ge(idx_ready, t)
                slots(t)
                if t < 2:
                    shared_down(t + 2)

            pe.wait_ge(row_table, 1)
            n_turns = turns(pe)
            for name in ("tab", ("sd", 2)):
                J.wait_taken(pe, name)

            def turn(g, b, q, first=False):
                pe.wait_ge(gath_in[g], q * 16 + 16)
                if not first:
                    pe.wait_ge(turned_a, b)
                    pe.wait_ge(turned_d, b)
                g3 = gath[g].rearrange("p (f k) -> p k f", k=KD)
                for k in range(KD):
                    ins = pe.transpose(pair[1][:, k // 4, (k % 4) * SLOTS:(k % 4 + 1) * SLOTS], g3[0:SLOTS, k, :], ident[0:SLOTS, 0:SLOTS])
                ins.then_inc(turned, 1)

            def gate_up(r, b, q, ks, first=False):
                if ks[0] == 0:
                    pe.wait_ge(wg_in[r], q * 32 + 32)
                    pe.wait_ge(turned_a, b + 1)
                    pe.wait_ge(turned_d, b + 1)
                    if not first:
                        pe.wait_ge(act_b, b)
                w = WG[r].rearrange("p s (k f) -> p s k f", k=KD)
                for k in ks:
                    ins = pe.matmul(pair[0][0:SLOTS, 0, :].rearrange("p (s f) -> p s f", s=2), hX[:, k, :], w[:, :, k, :],
                                    start=k == 0, stop=k == KD - 1, skip_group_check=True)
                if ks[-1] == KD - 1:
                    ins.then_inc(gu_made, 1)

            def turn_act(b):
                pe.wait_ge(act_b, b + 1)
                a3 = act.rearrange("p (f k) -> p k f", k=KF)
                for k in range(KF):
                    ins = pe.transpose(pair[0][:, 1, k * SLOTS:(k + 1) * SLOTS], a3[0:SLOTS, k, :], ident[0:SLOTS, 0:SLOTS])
                ins.then_inc(at_made, 1)

            def down(r, b):
                pe.wait_ge(at_taken, b + 1)
                pe.wait_ge(wd_lo, b + 1)
                pe.wait_ge(down_a, b + 1)
                pe.wait_ge(down_d, b + 1)
                for k in range(KF):
                    for h in range(2):
                        for s, (x, w) in enumerate(((0, 0), (1, 0), (0, 1))):
                            ins = pe.matmul(pair[2][0:SLOTS, h, :], act_parts[:, x, k, :],
                                            down_parts[r % PAIR][:, w, k, h * 512:(h + 1) * 512],
                                            start=k == 0 and s == 0, stop=k == KF - 1 and s == 2)
                ins.then_inc(down_made, 1)

            turn(0, 0, 0, first=True)
            gate_up(0, 0, 0, range(KD), first=True)
            shared_down(4)
            J.wait_taken(pe, ("sd", 4))
            turn(1, 1, 0)

            def step_of_block(i, j):
                b = i * RING + j
                pe.wait_ge(idx_ready, b + 2)
                slots(b + 2)
                gate_up(j, b, i, range(0, 4))
                turn_act(b - 1)
                gate_up(j, b, i, range(4, KD))
                turn((j + 1) % PAIR, b + 1, i * (RING // PAIR) + (j + 1) // PAIR)
                down((j - 1) % RING, b - 1)

            for j in range(1, RING):
                step_of_block(0, j)
            with pe.Fori(1, n_turns) as i:
                for j in range(RING):
                    step_of_block(i, j)
            turn_act(n_turns * RING - 1)
            down(RING - 1, n_turns * RING - 1)


_INS = ["x_prompt", "x_sample", "state_pool", "state_conv", "state_h", "cache_mem_k", "cache_mem_v", "mem_prompt",
        "norm_mix", "w_in", "pool_w", "pool_scale", "conv_w", "conv_b", "gate_a_w", "gate_a_b", "gate_x_w",
        "gate_x_b", "lru_lambda", "norm_pool_out", "norm_rnn_out", "w_out", "norm_xattn", "norm_mem", "xa_wq",
        "xa_wk", "xa_wv", "xa_wo", "norm_ffn", "router_w", "router_bias", "exp_w_gate", "exp_w_up", "exp_w_down",
        "sh_w_gate", "sh_w_up", "sh_w_down", "norm_final"]
_OUTS = [(1, SEQ, D), (DEC, 1, D), (1, 1, PBUF, DP), (1, 1, CBUF, DP), (1, 1, DP), (1, 1, NMEM, HEADS, HD),
         (1, 1, NMEM, HEADS, HD), (1, DEC, PBUF, DP), (1, DEC, CBUF, DP), (1, DEC, DP)]


def kernel(**inputs):
    import numpy as _np
    import concourse.bacc as _bacc
    from concourse.bass_utils import run_bass_kernel_spmd as _run

    nc = _bacc.Bacc("TRN2", target_bir_lowering=False, num_devices=1)
    arrays, args = {}, []
    for name in _INS:
        a = _np.ascontiguousarray(inputs[name])
        arrays[f"in_{name}"] = a
        args.append(nc.dram_tensor(f"in_{name}", a.shape, F32, kind="ExternalInput").ap())
    for i, shape in enumerate(_OUTS):
        args.append(nc.dram_tensor(f"out_{i}", shape, F32, kind="ExternalOutput").ap())
    for name, shape in (("h_rows", (NT, D)), ("acc_rows", (NT, D)), ("q_rows", (DEC, D))):
        args.append(nc.dram_tensor(name, shape, F32, kind="Internal").ap())
    trunk(nc, *args)
    r = _run(nc, [arrays], core_ids=[0])
    return tuple(r.results[0][f"out_{i}"] for i in range(len(_OUTS)))
```
